# Optimizing a Trainium2 kernel written in Bass

```python
import math
import jax, jax.numpy as jnp
from jax import lax
import numpy as np

D_MODEL = 1024
BATCH = 1
SEQ = 512
DEPTH = 2

SSM_WIDTH = D_MODEL // 2
SSM_GROUP = 16
SSM_GROUPS = SSM_WIDTH // SSM_GROUP
SSM_STATE = 64
SSM_DT_MIN = 1e-3
SSM_DT_MAX = 1e-1

RET_HEADS = 4
RET_QK_DIM = D_MODEL // 16
RET_V_DIM = 2 * RET_QK_DIM
RET_QK_WIDTH = RET_HEADS * RET_QK_DIM
RET_V_WIDTH = RET_HEADS * RET_V_DIM
RET_CHUNK = 128
RET_THETA = 10000.0

ATT_HEADS = 8
ATT_HEAD_DIM = 64
ATT_WIDTH = ATT_HEADS * ATT_HEAD_DIM
MOBA_BLOCK = 256
MOBA_TOPK = 3
ATT_Q_CHUNK = 128
ROPE_THETA = 500000.0
ROPE_DIM = ATT_HEAD_DIM // 4

N_BRANCH = 3
FFN_HIDDEN = 2816
CONV_WIDTH = 3
NORM_EPS = 1e-6
NEG_INF = -1e30

IN_SPLITS = [SSM_WIDTH, RET_QK_WIDTH, RET_QK_WIDTH, RET_V_WIDTH, RET_V_WIDTH,
             ATT_WIDTH, ATT_WIDTH, ATT_WIDTH, N_BRANCH * D_MODEL]
N_IN = sum(IN_SPLITS)

kernel_name = "hybrid_s5_retention_moba_convffn"

def rmsnorm(x, g):
    xf = x.astype(jnp.float32)
    r = xf * lax.rsqrt(jnp.mean(xf * xf, axis=-1, keepdims=True) + NORM_EPS)
    return (r * g.astype(jnp.float32)).astype(x.dtype)

def rotary(x, inv_freq):
    L = x.shape[1]
    half = inv_freq.shape[0]
    ang = jnp.arange(L, dtype=jnp.float32)[:, None] * inv_freq[None, :]
    cos = jnp.cos(ang)[None, :, None, :].astype(x.dtype)
    sin = jnp.sin(ang)[None, :, None, :].astype(x.dtype)
    x1 = x[..., :half]
    x2 = x[..., half:2 * half]
    rest = x[..., 2 * half:]
    return jnp.concatenate([x1 * cos - x2 * sin, x1 * sin + x2 * cos, rest], axis=-1)

def s5_branch(u, lam_re, lam_im, log_dt, b_re, b_im, c_re, c_im, d_skip, w_glu):
    bsz, L, _ = u.shape
    f32 = jnp.float32
    uf = u.astype(f32).reshape(bsz, L, SSM_GROUPS, SSM_GROUP)
    lam = lax.complex(lam_re.astype(f32), lam_im.astype(f32))
    dt = jnp.exp(log_dt.astype(f32))[:, None]
    lam_bar = jnp.exp(lam * dt)
    b = lax.complex(b_re.astype(f32), b_im.astype(f32))
    b_bar = ((lam_bar - 1.0) / lam)[..., None] * b
    bu = jnp.einsum('gph,blgh->blgp', b_bar, uf.astype(jnp.complex64))
    a = jnp.broadcast_to(lam_bar, bu.shape)

    def combine(e1, e2):
        a1, s1 = e1
        a2, s2 = e2
        return a1 * a2, a2 * s1 + s2

    _, states = lax.associative_scan(combine, (a, bu), axis=1)
    c = lax.complex(c_re.astype(f32), c_im.astype(f32))
    y = jnp.einsum('ghp,blgp->blgh', c, states).real \
        + d_skip.astype(f32).reshape(SSM_GROUPS, SSM_GROUP) * uf
    y = jax.nn.gelu(y.reshape(bsz, L, SSM_WIDTH))
    out = y * jax.nn.sigmoid(y @ w_glu.astype(f32))
    return out.astype(u.dtype)

def retention_branch(q, k, v, g, gn_g):
    bsz, L = q.shape[:2]
    f32 = jnp.float32
    C = RET_CHUNK
    n_chunks = L // C
    half = RET_QK_DIM // 2
    inv = 1.0 / (RET_THETA ** jnp.linspace(0.0, 1.0, half, dtype=f32))
    q = rotary(q, inv).astype(f32)
    k = rotary(k, inv).astype(f32) * (RET_QK_DIM ** -0.5)
    qc = q.reshape(bsz, n_chunks, C, RET_HEADS, RET_QK_DIM)
    kc = k.reshape(bsz, n_chunks, C, RET_HEADS, RET_QK_DIM)
    vc = v.astype(f32).reshape(bsz, n_chunks, C, RET_HEADS, RET_V_DIM)

    log_gamma = jnp.log1p(-jnp.exp2(-5.0 - jnp.arange(RET_HEADS, dtype=f32)))
    pos = jnp.arange(C, dtype=f32)
    rel = pos[:, None] - pos[None, :]
    decay = jnp.where(rel >= 0,
                      jnp.exp(log_gamma[:, None, None] * jnp.maximum(rel, 0.0)[None]),
                      0.0)
    s = jnp.einsum('bnchd,bnmhd->bnhcm', qc, kc) * decay
    o_intra = jnp.einsum('bnhcm,bnmhe->bnche', s, vc)
    zeta = jnp.exp(log_gamma[:, None] * (C - 1.0 - pos)[None, :])
    kv = jnp.einsum('bnmhd,bnmhe,hm->nbhde', kc, vc, zeta)
    chunk_decay = jnp.exp(log_gamma * C)[None, :, None, None]

    def step(state, kv_n):
        return chunk_decay * state + kv_n, state

    _, state_prev = lax.scan(step, jnp.zeros_like(kv[0]), kv)
    xi = jnp.exp(log_gamma[:, None] * (pos + 1.0)[None, :])
    o_cross = jnp.einsum('bnchd,nbhde,hc->bnche', qc, state_prev, xi)
    o = (o_intra + o_cross).reshape(bsz, L, RET_HEADS, RET_V_DIM)
    mu = jnp.mean(o, axis=-1, keepdims=True)
    var = jnp.mean(jnp.square(o - mu), axis=-1, keepdims=True)
    o = ((o - mu) * lax.rsqrt(var + NORM_EPS)).reshape(bsz, L, RET_V_WIDTH) * gn_g.astype(f32)
    return (jax.nn.silu(g.astype(f32)) * o).astype(g.dtype)

def moba_branch(q, k, v, qn_g, kn_g):
    bsz, L = q.shape[:2]
    out_dtype = q.dtype
    f32 = jnp.float32
    H, hd, BLK, QC = ATT_HEADS, ATT_HEAD_DIM, MOBA_BLOCK, ATT_Q_CHUNK
    q = rmsnorm(q, qn_g)
    k = rmsnorm(k, kn_g)
    rh = ROPE_DIM // 2
    inv = ROPE_THETA ** (-jnp.arange(rh, dtype=f32) / rh)
    q = rotary(q, inv)
    k = rotary(k, inv)

    nb = -(-L // BLK)
    Lp = nb * BLK
    pad = ((0, 0), (0, Lp - L), (0, 0), (0, 0))
    q = jnp.pad(q, pad).astype(f32).transpose(0, 2, 1, 3)
    k = jnp.pad(k, pad).astype(f32).transpose(0, 2, 1, 3)
    v = jnp.pad(v, pad).astype(f32).transpose(0, 2, 1, 3)
    kb = k.reshape(bsz, H, nb, BLK, hd)
    vb = v.reshape(bsz, H, nb, BLK, hd)
    scale = hd ** -0.5
    n_sel = min(MOBA_TOPK, nb - 1)
    nq = Lp // QC
    qc = q.reshape(bsz, H, nq, QC, hd).transpose(2, 0, 1, 3, 4)
    bi = jnp.arange(bsz)[:, None, None, None]
    hi = jnp.arange(H)[None, :, None, None]

    if n_sel > 0:
        k_mean = jnp.mean(kb, axis=3)
        qblk = jnp.arange(Lp) // BLK
        gate = jnp.einsum('bhtd,bhjd->bhtj', q, k_mean)
        past = jnp.arange(nb)[None, :] < qblk[:, None]
        gate = jnp.where(past, gate, NEG_INF)
        _, top_idx = lax.top_k(gate, n_sel)
        top_ok = top_idx < qblk[None, None, :, None]
        sel_c = top_idx.reshape(bsz, H, nq, QC, n_sel).transpose(2, 0, 1, 3, 4)
        ok_c = top_ok.reshape(bsz, H, nq, QC, n_sel).transpose(2, 0, 1, 3, 4)
    else:
        sel_c = jnp.zeros((nq, bsz, H, QC, 1), jnp.int32)
        ok_c = jnp.zeros((nq, bsz, H, QC, 1), bool)

    def attend(args):
        c, q_blk, sel, ok = args
        t = c * QC + jnp.arange(QC)
        own = (c * QC) // BLK
        k_own = lax.dynamic_index_in_dim(kb, own, axis=2, keepdims=False)
        v_own = lax.dynamic_index_in_dim(vb, own, axis=2, keepdims=False)
        kpos = own * BLK + jnp.arange(BLK)
        s_own = jnp.einsum('bhqd,bhkd->bhqk', q_blk, k_own) * scale
        s_own = jnp.where(kpos[None, :] <= t[:, None], s_own, NEG_INF)
        if n_sel > 0:
            k_sel = kb[bi, hi, sel]
            v_sel = vb[bi, hi, sel].reshape(bsz, H, QC, n_sel * BLK, hd)
            s_sel = jnp.einsum('bhqd,bhqnkd->bhqnk', q_blk, k_sel) * scale
            s_sel = jnp.where(ok[..., None], s_sel, NEG_INF).reshape(bsz, H, QC, n_sel * BLK)
            p = jax.nn.softmax(jnp.concatenate([s_sel, s_own], axis=-1), axis=-1)
            return (jnp.einsum('bhqk,bhqkd->bhqd', p[..., :n_sel * BLK], v_sel)
                    + jnp.einsum('bhqk,bhkd->bhqd', p[..., n_sel * BLK:], v_own))
        p = jax.nn.softmax(s_own, axis=-1)
        return jnp.einsum('bhqk,bhkd->bhqd', p, v_own)

    out = lax.map(attend, (jnp.arange(nq), qc, sel_c, ok_c))
    out = out.transpose(1, 0, 3, 2, 4).reshape(bsz, Lp, H * hd)[:, :L]
    return out.astype(out_dtype)

def conv_ffn(x, w_up, conv_w, conv_b, w_down):
    L = x.shape[1]
    h = x @ w_up
    hp = jnp.pad(h, ((0, 0), (CONV_WIDTH - 1, 0), (0, 0)))
    h = conv_b
    for j in range(CONV_WIDTH):
        h = h + hp[:, j:j + L] * conv_w[j]
    g, u = jnp.split(h, 2, axis=-1)
    return (jax.nn.silu(g) * u) @ w_down

def setup_inputs(seed: int = 0) -> dict:
    key = jax.random.key(seed)
    ks = jax.random.split(key, 24)
    f32 = jnp.float32
    Ld = DEPTH
    G, P, Hs = SSM_GROUPS, SSM_STATE, SSM_GROUP

    def nrm(k, shape, scale):
        return jax.random.normal(k, shape, f32) * scale

    return {
        "x": nrm(ks[0], (BATCH, SEQ, D_MODEL), 1.0),
        "norm1_g": 1.0 + nrm(ks[1], (Ld, D_MODEL), 0.02),
        "w_in": nrm(ks[2], (Ld, D_MODEL, N_IN), D_MODEL ** -0.5),
        "ssm_lambda_re": -0.5 + nrm(ks[3], (Ld, G, P), 0.01),
        "ssm_lambda_im": jnp.pi * jnp.arange(P, dtype=f32)[None, None, :] + nrm(ks[4], (Ld, G, P), 0.01),
        "ssm_log_dt": jax.random.uniform(ks[5], (Ld, G), f32, math.log(SSM_DT_MIN), math.log(SSM_DT_MAX)),
        "ssm_b_re": nrm(ks[6], (Ld, G, P, Hs), (2 * Hs) ** -0.5),
        "ssm_b_im": nrm(ks[7], (Ld, G, P, Hs), (2 * Hs) ** -0.5),
        "ssm_c_re": nrm(ks[8], (Ld, G, Hs, P), 0.5),
        "ssm_c_im": nrm(ks[9], (Ld, G, Hs, P), 0.5),
        "ssm_d": nrm(ks[10], (Ld, SSM_WIDTH), 1.0),
        "ssm_w_glu": nrm(ks[11], (Ld, SSM_WIDTH, SSM_WIDTH), SSM_WIDTH ** -0.5),
        "ret_gn_g": 1.0 + nrm(ks[12], (Ld, RET_V_WIDTH), 0.02),
        "attn_qn_g": 1.0 + nrm(ks[13], (Ld, ATT_HEAD_DIM), 0.02),
        "attn_kn_g": 1.0 + nrm(ks[14], (Ld, ATT_HEAD_DIM), 0.02),
        "w_br_ssm": nrm(ks[15], (Ld, SSM_WIDTH, D_MODEL), SSM_WIDTH ** -0.5),
        "w_br_ret": nrm(ks[16], (Ld, RET_V_WIDTH, D_MODEL), RET_V_WIDTH ** -0.5),
        "w_br_att": nrm(ks[17], (Ld, ATT_WIDTH, D_MODEL), ATT_WIDTH ** -0.5),
        "w_o": nrm(ks[18], (Ld, D_MODEL, D_MODEL), D_MODEL ** -0.5),
        "norm2_g": 1.0 + nrm(ks[19], (Ld, D_MODEL), 0.02),
        "ffn_w_up": nrm(ks[20], (Ld, D_MODEL, 2 * FFN_HIDDEN), D_MODEL ** -0.5),
        "ffn_conv_w": nrm(ks[21], (Ld, CONV_WIDTH, 2 * FFN_HIDDEN), CONV_WIDTH ** -0.5),
        "ffn_conv_b": nrm(ks[22], (Ld, 2 * FFN_HIDDEN), 0.01),
        "ffn_w_down": nrm(ks[23], (Ld, FFN_HIDDEN, D_MODEL), FFN_HIDDEN ** -0.5),
    }

def reference(x, norm1_g, w_in, ssm_lambda_re, ssm_lambda_im, ssm_log_dt, ssm_b_re, ssm_b_im,
              ssm_c_re, ssm_c_im, ssm_d, ssm_w_glu, ret_gn_g, attn_qn_g, attn_kn_g,
              w_br_ssm, w_br_ret, w_br_att, w_o, norm2_g, ffn_w_up, ffn_conv_w, ffn_conv_b,
              ffn_w_down):
    bsz, L, _ = x.shape
    offsets = [int(o) for o in np.cumsum(IN_SPLITS)[:-1]]
    for l in range(DEPTH):
        xn = rmsnorm(x, norm1_g[l])
        proj = xn @ w_in[l]
        (u_s, q_r, k_r, v_r, g_r, q_a, k_a, v_a, gates) = jnp.split(proj, offsets, axis=-1)
        y_s = s5_branch(u_s, ssm_lambda_re[l], ssm_lambda_im[l], ssm_log_dt[l], ssm_b_re[l],
                        ssm_b_im[l], ssm_c_re[l], ssm_c_im[l], ssm_d[l], ssm_w_glu[l])
        y_r = retention_branch(q_r.reshape(bsz, L, RET_HEADS, RET_QK_DIM),
                               k_r.reshape(bsz, L, RET_HEADS, RET_QK_DIM),
                               v_r.reshape(bsz, L, RET_HEADS, RET_V_DIM),
                               g_r, ret_gn_g[l])
        y_a = moba_branch(q_a.reshape(bsz, L, ATT_HEADS, ATT_HEAD_DIM),
                          k_a.reshape(bsz, L, ATT_HEADS, ATT_HEAD_DIM),
                          v_a.reshape(bsz, L, ATT_HEADS, ATT_HEAD_DIM),
                          attn_qn_g[l], attn_kn_g[l])
        g_s, g_rt, g_at = jnp.split(jax.nn.sigmoid(gates), N_BRANCH, axis=-1)
        merged = (g_s * (y_s @ w_br_ssm[l]) + g_rt * (y_r @ w_br_ret[l])
                  + g_at * (y_a @ w_br_att[l]))
        x = x + merged @ w_o[l]
        x = x + conv_ffn(rmsnorm(x, norm2_g[l]), ffn_w_up[l], ffn_conv_w[l], ffn_conv_b[l],
                         ffn_w_down[l])
    return x


_drawn_inputs = setup_inputs


def setup_inputs(seed=0):
    import zlib

    import numpy as np

    out = dict(_drawn_inputs(seed))
    spreads = {}
    factors = {'ssm_lambda_re': 200.0,
     'ret_gn_g': 5.833,
     'attn_qn_g': 8.0,
     'attn_kn_g': 8.0,
     'norm2_g': 2.702,
     'ffn_conv_b': 5.525,
     'ssm_b_re': 2.794,
     'ssm_c_im': 2.777,
     'ssm_b_im': 2.841,
     'ssm_c_re': 2.793}
    for name, (base, spread) in spreads.items():
        noise = np.random.default_rng([zlib.crc32(name.encode()), seed]).standard_normal(out[name].shape)
        drawn = base * np.exp(spread * noise) if base else spread * noise
        out[name] = __import__('jax').numpy.asarray(drawn.astype(out[name].dtype))
    for name, factor in factors.items():
        out[name] = (out[name] * factor).astype(out[name].dtype)
    return out
```

```python
from contextlib import ExitStack

import numpy as np

import concourse.bass as bass
from concourse import mybir

F32 = mybir.dt.float32
F32R = mybir.dt.float32r
ALU = mybir.AluOpType
ACT = mybir.ActivationFunctionType
AX_X = mybir.AxisListType.X

P = 128
EPS = 1e-6
MASKED = -1e30

DEPTH = 2
D = 1024
L = 512
DK = D // P
SSM_W = 512
SSM_H = 16
SSM_P = 64
ST = SSM_W // SSM_H * SSM_P // P
CH = 2 * SSM_H
RH = 4
RQ = 64
AH = 8
AD = 64
FH = 2816
FT = FH // P
FHALF = FT // 2
TT = L // P

SLAB = 2048
N_PROJ = 14
S_GLU = N_PROJ
S_GS = S_GLU + 1
S_BS = S_GS + 4
S_R = S_BS + 2
S_A = S_R + 6
S_O = S_A + 6
N_MIX = S_O + 4
N_UP = FHALF
N_DOWN = DK
N_SLABS = N_MIX + 2 * (N_UP + N_DOWN)
DOWN = FHALF * P


def is_down(n):
    return n >= N_MIX and (n - N_MIX) % (N_UP + N_DOWN) >= N_UP


_widths = [("g1", DK), ("g2", DK), ("gn", RH), ("qn", 1), ("kn", 1), ("d", 4), ("lre", ST), ("lim", ST),
           ("ldt", ST), ("cw", 3 * 2 * FT), ("cb", 2 * FT)]
PAR = {}
_at = 0
for _n, _w in _widths:
    PAR[_n] = (_at, _at + _w)
    _at += _w
N_PAR = -(-_at // 8) * 8

U0, QR, KR, VR, GR, QA, KA, VA = 0, 4, 6, 8, 12, 16, 20, 24
N_PT = 28

LEVELS = 9
BASE = 32
DIAG = [sum(L - P * i for i in range(j)) for j in range(TT + 1)]
TRI = [P * i * (i + 1) // 2 for i in range(TT + 1)]


def hybrid_trunk(nc, xT, wslab, wdown, par, bblk, cblk, cst, outT):
    ctx = ExitStack()
    with ctx:
        def sb(name, shape, dt=F32):
            return ctx.enter_context(nc.sbuf_tensor(name, shape, dt))

        sems = []

        def sem(name):
            s = ctx.enter_context(nc.semaphore(name))
            sems.append(s)
            return s

        x = sb("x_res", [P, DK, L])
        xh = sb("xn_hi", [P, DK, L], F32R)
        xl = sb("xn_lo", [P, DK, L], F32R)
        raw = sb("w_raw", [P, 2, SLAB])
        wh = sb("w_hi", [P, 2, SLAB], F32R)
        wl = sb("w_lo", [P, 2, SLAB], F32R)
        consts = sb("consts", [P, cst.shape[1]])
        pr = sb("params", [P, N_PAR])
        off = 0

        def const(width):
            nonlocal off
            off += width
            return consts[:, off - width:off]

        decay = const(RH * L).rearrange("p (h t) -> p h t", h=RH)
        r_cos, r_sin, a_cos, a_sin = const(L), const(L), const(L), const(L)
        ident, r_swap, a_swap, ones, blk64, mean128, mask = [const(P) for _ in range(7)]

        def prm(name):
            return pr[:, PAR[name][0]:PAR[name][1]]

        base = nc.sbuf_base
        KB = 1024
        work_kb = 36
        arena = sb("arena", [P, (2 * N_PT + work_kb) * KB // 4])

        def at(name, kb, shape, dt=F32):
            t = nc.alloc_sbuf_tensor_at(name, shape, dt, offset=base + int(kb * KB))
            return t

        W0 = 2 * N_PT
        proj = at("proj", 0, [P, N_PT, L])
        sq = at("sq", W0 + 8, [P, 2, L])
        rstd = at("rstd", W0 + 12, [P, L])
        xn = at("xn", W0 + 14, [P, 2, L])
        ph = at("phase", W0, [P, 2, L])
        p1 = at("prod1", W0 + 4, [P, 2, L])
        p2 = at("prod2", W0 + 8, [P, 2, L])
        zz = at("scan", W0 + 12, [P, 2, L])
        stt = at("states", W0 + 16, [P, 2, L])
        bw = at("b_blocks", W0 + 20, [P, 2, 4, P])
        cw_ = at("c_blocks", W0 + 24, [P, 2, ST, CH])
        ph0 = at("phase_base", W0 + 28, [P, ST, 2, BASE])
        pw = at("powers", W0 + 32, [P, 2, LEVELS, ST])
        sm = at("s5_small", W0 + 34, [P, 20, ST])
        gh = at("gelu_hi", W0, [P, 4, L], F32R)
        gl = at("gelu_lo", W0 + 8, [P, 4, L], F32R)
        ysh = at("ys_hi", W0 + 16, [P, 4, L], F32R)
        ysl = at("ys_lo", W0 + 24, [P, 4, L], F32R)
        sg = at("glu_sig", W0 + 32, [P, 2, L])
        merged = at("merged", W0, [P, DK, L])
        gates = at("gates", 0, [P, 4, L])
        mt = at("merge_tmp", W0 + 32, [P, 2, L])
        yrh = at("yr_hi", W0 + 16, [P, 4, L], F32R)
        yrl = at("yr_lo", W0 + 24, [P, 4, L], F32R)
        sd = at("ret_scores", 0, [P, DIAG[TT]])
        osb = at("ret_out", 5, [P, L])
        rsq = at("ret_sq", W0 + 32, [P, 2, L])
        yah = at("ya_hi", 8, [P, 4, L], F32R)
        yal = at("ya_lo", 16, [P, 4, L], F32R)
        pp = at("probs", 0, [P, TRI[TT]])
        pt = at("probs_t", 24, [P, DIAG[TT]])
        ast = at("attn_stat", 29.5, [P, 4, TT])
        asq = at("attn_sq", W0 + 32, [P, 2, L])
        hh = at("hid_hi", 0, [P, FHALF, L], F32R)
        hl = at("hid_lo", 22, [P, FHALF, L], F32R)
        cg = at("conv_g", W0, [P, 2, L])
        cu = at("conv_u", W0 + 4, [P, 2, L])
        ht = at("hid", W0 + 8, [P, 2, L])

        pg = ctx.enter_context(nc.psum_tensor("ps_gemm", [P, 4, L], F32))
        pb = ctx.enter_context(nc.psum_tensor("ps_pair", [P, 2, L], F32))
        py = ctx.enter_context(nc.psum_tensor("ps_out", [P, L], F32))
        pn = ctx.enter_context(nc.psum_tensor("ps_norm", [P, L], F32))

        s_x = ctx.enter_context(nc.semaphore("x_loaded"))
        s_store = ctx.enter_context(nc.semaphore("stored"))
        s_go = ctx.enter_context(nc.semaphore("layer_go"))
        s_ack = ctx.enter_context(nc.semaphore("layer_ack"))
        s_par = sem("params_in")
        s_raw = [sem("raw_in0"), sem("raw_in1")]
        s_hi, s_lo, s_used = sem("w_hi_done"), sem("w_lo_done"), sem("slab_used")
        s_mm, s_ev = sem("gemm_done"), sem("gemm_evacuated")
        s_sq = [sem("sq_a"), sem("sq_b")]
        s_ss = [sem("ssum_a"), sem("ssum_b")]
        s_rc = [sem("recip_a"), sem("recip_b")]
        s_rt = [sem("rstd_a"), sem("rstd_b")]
        s_xn = [sem("xn_a"), sem("xn_b")]
        s_xh = [sem("xh_a"), sem("xh_b")]
        s_xl = [sem("xl_a"), sem("xl_b")]
        s_dt, s_th, s_sc = sem("s5_exp"), sem("s5_theta"), sem("s5_sincos")
        s_cc = sem("c_scaled")
        s_bu, s_rot, s_st, s_y, s_yp = sem("bu_done"), sem("bu_rotated"), sem("states_ready"), sem("y_done"), sem("y_pre")
        s_ge, s_gh, s_gl = sem("gelu"), sem("gelu_hi_s"), sem("gelu_lo_s")
        s_sg, s_yf, s_yh, s_yl = sem("glu_sig_s"), sem("ys_full"), sem("ys_hi_s"), sem("ys_lo_s")
        s_gate = sem("gate_ready")
        s_mg = sem("merged_part")
        s_mh, s_ml = sem("merged_hi"), sem("merged_lo")
        s_vt, s_vc = sem("v_transposed"), sem("v_copied")
        s_sw, s_ro = sem("ret_swapped"), sem("ret_rotated")
        s_rs, s_rd, s_o, s_oc = sem("ret_scores_s"), sem("ret_decayed"), sem("ret_o"), sem("ret_o_copied")
        s_mu, s_ct, s_q2, s_va, s_r2, s_rr = (sem("gn_mean"), sem("gn_centred"), sem("gn_square"), sem("gn_var"),
                                              sem("gn_recip"), sem("gn_rstd"))
        s_yr, s_yrh, s_yrl = sem("yr_full"), sem("yr_hi_s"), sem("yr_lo_s")
        s_as, s_am, s_ar, s_at, s_an = (sem("att_sq"), sem("att_ms"), sem("att_recip"), sem("att_rstd"), sem("att_normed"))
        s_ap, s_ax = sem("att_swapped"), sem("att_rotated")
        s_sc_, s_mx, s_ex, s_pn = sem("att_scores"), sem("att_max"), sem("att_exp"), sem("att_probs")
        s_tp, s_tc, s_pv, s_yah, s_yal = (sem("att_transposed"), sem("att_t_copied"), sem("att_pv"), sem("ya_hi_s"), sem("ya_lo_s"))
        s_c0, s_c1, s_si, s_hd, s_hh, s_hl = (sem("conv_first"), sem("conv_done"), sem("silu"), sem("hidden"),
                                              sem("hid_hi_s"), sem("hid_lo_s"))
        s_end = sem("layer_end")
        nums = sorted(s.num if hasattr(s, "num") else int(s) for s in sems)
        assert nums == list(range(nums[0], nums[-1] + 1)), nums

        ENGINES = 5

        def layer_end(eng):
            eng.drain().then_inc(s_end, 1)
            eng.wait_ge(s_go, 1)
            eng.drain().then_inc(s_ack, 1)

        block = ctx.enter_context(nc.Block())

        @block.sync
        def _(sp):
            sp.dma_start(x[:, :, :], xT).then_inc(s_x, 16)
            sp.dma_start(consts[:, :], cst).then_inc(s_x, 16)
            with sp.Fori(0, DEPTH) as l:
                sp.dma_start(pr[:, :], par[l, :, :]).then_inc(s_par, 16)
                sp.dma_start(bw[:, :, :, :], bblk[l, :, :, :, :]).then_inc(s_par, 16)
                sp.dma_start(cw_[:, :, :, :], cblk[l, :, :, :, :]).then_inc(s_par, 16)
                for n in range(N_SLABS):
                    if n >= 2:
                        sp.wait_ge(s_lo, n - 1)
                    if is_down(n):
                        m = n - N_MIX
                        m = m // (N_UP + N_DOWN) * N_DOWN + m % (N_UP + N_DOWN) - N_UP
                        sp.dma_start(raw[:, n % 2, 0:DOWN], wdown[l, m, :, :]).then_inc(s_raw[n % 2], 16)
                    else:
                        m = n if n < N_MIX else N_MIX + (n - N_MIX) // (N_UP + N_DOWN) * N_UP + (n - N_MIX) % (N_UP + N_DOWN)
                        sp.dma_start(raw[:, n % 2, :], wslab[l, m, :, :]).then_inc(s_raw[n % 2], 16)
                layer_end(sp)
            sp.dma_start(outT, x[:, :, :]).then_inc(s_store, 16)
            sp.wait_ge(s_store, 16)

        @block.gpsimd
        def _(pool):
            with pool.Fori(0, DEPTH) as l:
                for n in range(N_SLABS):
                    w = DOWN if is_down(n) else SLAB
                    pool.wait_ge(s_hi, n + 1)
                    nc.gpsimd.tensor_tensor(wl[:, n % 2, 0:w], raw[:, n % 2, 0:w], wh[:, n % 2, 0:w].bitcast(F32),
                                            ALU.subtract).then_inc(s_lo, 1)
                pool.wait_ge(s_end, ENGINES - 1)
                pool.drain()
                pool.sem_clear(range(nums[0], nums[-1] + 1))
                pool.drain().then_inc(s_go, 1)
                pool.wait_ge(s_ack, ENGINES - 1)
                pool.drain()
                pool.sem_clear(s_go)
                pool.sem_clear(s_ack)

        @block.tensor
        def _(pe):
            def slab(n, rh, rl, kt, mt_, evac_of=None):
                pe.wait_ge(s_lo, n + 1)
                w = kt * mt_ * P
                vh = wh[:, n % 2, 0:w].rearrange("p (k c) -> p k c", k=kt)
                vl = wl[:, n % 2, 0:w].rearrange("p (k c) -> p k c", k=kt)
                for m in range(mt_):
                    t = tile[0]
                    tile[0] += 1
                    if t >= 4:
                        pe.wait_ge(s_ev, t - 3)
                    for k in range(kt):
                        c = slice(m * P, (m + 1) * P)
                        nc.tensor.matmul(pg[:, t % 4, :], vh[:, k, c], rh[:, k, :], start=(k == 0), stop=False)
                        nc.tensor.matmul(pg[:, t % 4, :], vh[:, k, c], rl[:, k, :], start=False, stop=False)
                        mm = nc.tensor.matmul(pg[:, t % 4, :], vl[:, k, c], rh[:, k, :], start=False, stop=(k == kt - 1))
                    mm.then_inc(s_mm, 1)
                pe.drain().then_inc(s_used, 1)

            def norm(i):
                for k in range(DK):
                    pe.wait_ge(s_sq[i], k + 1)
                    nc.tensor.matmul(pn[:, :], ones, sq[:, k % 2, :], start=(k == 0), stop=(k == DK - 1)).then_inc(s_ss[i], 1)

            def s5_in(s):
                t, j = s // 4, s % 4
                r = slice(CH * j, CH * (j + 1))
                if s == 0:
                    pe.wait_ge(s_par, 48)
                pe.wait_ge(s_ev, 4)
                if s >= 1:
                    pe.wait_ge(s_rot, s)
                nc.tensor.matmul(pb[:, 0, :], bw[r, 0, t, :], proj[r, U0 + t, :], start=True, stop=True)
                nc.tensor.matmul(pb[:, 1, :], bw[r, 1, t, :], proj[r, U0 + t, :], start=True, stop=True).then_inc(s_bu, 1)

            def s5_out(s):
                t, j = s // 4, s % 4
                r = slice(CH * j, CH * (j + 1))
                pe.wait_ge(s_st, s + 1)
                if j == 0 and t >= 1:
                    pe.wait_ge(s_yp, t)
                nc.tensor.matmul(py[r, :], cw_[:, 0, s, :], stt[:, 0, :], start=True, stop=False, tile_position=(0, CH * j))
                nc.tensor.matmul(py[r, :], cw_[:, 1, s, :], stt[:, 1, :], start=False, stop=True,
                                 tile_position=(0, CH * j)).then_inc(s_y, 1)

            def v_transposes(first, i):
                pe.wait_ge(s_ev, ev_free[i])
                for c in range(TT):
                    for h in range(4):
                        mm = nc.tensor.transpose(pg[:, c, P * h:P * (h + 1)], proj[:, first + h, P * c:P * (c + 1)], ident)
                    mm.then_inc(s_vt, 1)

            def retention():
                for i, tl in enumerate((QR, QR + 1, KR, KR + 1)):
                    if i >= 2:
                        pe.wait_ge(s_ro, i - 1)
                    nc.tensor.matmul(pb[:, i % 2, :], r_swap, proj[:, tl, :], start=True, stop=True).then_inc(s_sw, 1)
                pe.wait_ge(s_ro, 4)
                pe.wait_ge(s_vc, 4)
                for h in range(RH):
                    b = RQ * (h % 2)
                    r = slice(b, b + RQ)
                    for j in range(TT):
                        g = TT * h + j
                        if g >= 2:
                            pe.wait_ge(s_rd, g - 1)
                        nc.tensor.matmul(pb[:, g % 2, P * j:L], proj[r, KR + h // 2, P * j:P * (j + 1)],
                                         proj[r, QR + h // 2, P * j:L], start=True, stop=True).then_inc(s_rs, 1)
                        if j >= 1:
                            ret_out(h, j - 1)
                    ret_out(h, TT - 1)
                    pe.wait_ge(s_oc, h + 1)
                    nc.tensor.matmul(pn[:, :], mean128, osb[:, :], start=True, stop=True).then_inc(s_mu, 1)
                    pe.wait_ge(s_q2, h + 1)
                    nc.tensor.matmul(pn[:, :], mean128, rsq[:, 0, :], start=True, stop=True).then_inc(s_va, 1)

            def ret_out(h, j):
                pe.wait_ge(s_rd, TT * h + j + 1)
                if j == 0 and h >= 1:
                    pe.wait_ge(s_oc, h)
                mm = nc.tensor.matmul(py[:, P * j:L], proj[:, VR + j, P * h:P * (h + 1)],
                                      sd[:, DIAG[j]:DIAG[j + 1]], start=(j == 0), stop=(j == TT - 1))
                if j == TT - 1:
                    mm.then_inc(s_o, 1)

            def attention():
                for i in range(8):
                    pe.wait_ge(s_as, i + 1)
                    if i >= 2:
                        pe.wait_ge(s_ar, i - 1)
                    nc.tensor.matmul(pb[:, i % 2, :], blk64, asq[:, i % 2, :], start=True, stop=True).then_inc(s_am, 1)
                pe.wait_ge(s_ar, 8)
                for i in range(8):
                    pe.wait_ge(s_an, i + 1)
                    if i >= 2:
                        pe.wait_ge(s_ax, i - 1)
                    nc.tensor.matmul(pb[:, i % 2, :], a_swap, proj[:, QA + i, :], start=True, stop=True).then_inc(s_ap, 1)
                pe.wait_ge(s_ax, 8)
                pe.wait_ge(s_vc, 8)
                for h in range(AH):
                    b = AD * (h % 2)
                    r = slice(b, b + AD)
                    for i in range(TT + 1):
                        if i < TT:
                            g = TT * h + i
                            if g >= 2:
                                pe.wait_ge(s_ex, g - 1)
                            nc.tensor.matmul(pb[:, g % 2, 0:P * (i + 1)], proj[r, QA + h // 2, P * i:P * (i + 1)],
                                             proj[r, KA + h // 2, 0:P * (i + 1)], start=True, stop=True).then_inc(s_sc_, 1)
                        if i >= 1:
                            q = i - 1
                            pe.wait_ge(s_pn, TT * h + q + 1)
                            if h >= 1 and q == 0:
                                pe.wait_ge(s_tc, TT * h)
                            for j in range(q + 1):
                                mm = nc.tensor.transpose(pg[:, j, P * q:P * (q + 1)], pp[:, TRI[q] + P * j:TRI[q] + P * (j + 1)], ident)
                            if q == TT - 1:
                                mm.then_inc(s_tp, 1)
                    if h % 2 == 0 and h >= 2:
                        pe.wait_ge(s_yal, h // 2)
                    for j in range(TT):
                        pe.wait_ge(s_tc, TT * h + j + 1)
                        mm = nc.tensor.matmul(py[r, P * j:L], proj[:, VA + j, AD * h:AD * (h + 1)], pt[:, DIAG[j]:DIAG[j + 1]],
                                              start=(j == 0), stop=(j == TT - 1), tile_position=(0, b))
                    mm.then_inc(s_pv, 1)

            pe.wait_ge(s_x, 32)
            with pe.Fori(0, DEPTH) as l:
                tile = [0]
                norm(0)
                pe.wait_ge(s_xl[0], DK)
                for n in range(2):
                    slab(n, xh, xl, DK, 2)
                pe.wait_ge(s_cc, 1)
                for n in range(2, N_PROJ):
                    s5_in(n - 2)
                    slab(n, xh, xl, DK, 2)
                    s5_out(n - 2)
                for s in range(N_PROJ - 2, ST):
                    s5_in(s)
                    s5_out(s)
                pe.wait_ge(s_gl, 4)
                slab(S_GLU, gh, gl, 4, 4)
                for n in range(S_GS, S_GS + 4):
                    slab(n, xh, xl, DK, 2)
                pe.wait_ge(s_yl, 4)
                for n in range(S_BS, S_BS + 2):
                    slab(n, ysh, ysl, 4, 4)
                ev_free = {0: tile[0]}
                v_transposes(VR, 0)
                retention()
                pe.wait_ge(s_vc, 4)
                pe.wait_ge(s_yrl, 4)
                for i in range(2):
                    for n in range(2):
                        slab(S_R + 3 * i + n, xh, xl, DK, 2)
                    slab(S_R + 3 * i + 2, yrh, yrl, 4, 4)
                ev_free[1] = tile[0]
                v_transposes(VA, 1)
                attention()
                pe.wait_ge(s_yal, 4)
                for i in range(2):
                    for n in range(2):
                        slab(S_A + 3 * i + n, xh, xl, DK, 2)
                    slab(S_A + 3 * i + 2, yah, yal, 4, 4)
                pe.wait_ge(s_ml, DK)
                for n in range(S_O, S_O + 4):
                    slab(n, xh, xl, DK, 2)
                norm(1)
                pe.wait_ge(s_xl[1], DK)
                n = N_MIX
                for half in range(2):
                    for i in range(N_UP):
                        slab(n, xh, xl, DK, 2)
                        n += 1
                    pe.wait_ge(s_hl, FHALF * (half + 1))
                    for i in range(N_DOWN):
                        slab(n, hh, hl, FHALF, 1)
                        n += 1
                layer_end(pe)

        @block.scalar
        def _(act):
            def hi(n):
                if n >= N_SLABS:
                    return
                w = DOWN if is_down(n) else SLAB
                act.wait_ge(s_raw[n % 2], 16 * (n // 2 + 1))
                if n >= 2:
                    act.wait_ge(s_used, n - 1)
                nc.scalar.activation(wh[:, n % 2, 0:w], raw[:, n % 2, 0:w], ACT.Copy).then_inc(s_hi, 1)

            def norm(i):
                for k in range(DK):
                    if k >= 2:
                        act.wait_ge(s_ss[i], k - 1)
                    nc.scalar.activation(sq[:, k % 2, :], x[:, k, :], ACT.Square).then_inc(s_sq[i], 1)
                act.wait_ge(s_rc[i], 1)
                nc.scalar.activation(rstd[:, :], rstd[:, :], ACT.Sqrt).then_inc(s_rt[i], 1)
                for k in range(DK):
                    act.wait_ge(s_xn[i], k + 1)
                    nc.scalar.activation(xh[:, k, :], xn[:, k % 2, :], ACT.Copy).then_inc(s_xh[i], 1)

            def evac(dst, func=ACT.Copy, sig=None):
                t = tile[0]
                tile[0] += 1
                act.wait_ge(s_mm, t + 1)
                nc.scalar.activation(dst, pg[:, t % 4, :], func).then_inc(s_ev if sig is None else sig, 1)

            with act.Fori(0, DEPTH) as l:
                tile = [0]
                act.wait_ge(s_x, 32)
                norm(0)
                hi(0)
                act.wait_ge(s_par, 48)
                nc.scalar.activation(sm[:, 0, :], prm("ldt"), ACT.Exp).then_inc(s_dt, 1)
                act.wait_ge(s_th, 1)
                nc.scalar.activation(sm[:, 2, :], sm[:, 1, :], ACT.Exp).then_inc(s_dt, 1)
                act.wait_ge(s_th, 2)
                nc.scalar.activation(sm[:, 5, :], sm[:, 4, :], ACT.Sin)
                nc.scalar.activation(sm[:, 6, :], sm[:, 4, :], ACT.Sin, scale=0.5).then_inc(s_sc, 1)
                for n in range(N_PROJ):
                    hi(n + 1)
                    for m in range(2):
                        evac(proj[:, 2 * n + m, :])
                for t in range(4):
                    act.wait_ge(s_yp, t + 1)
                    nc.scalar.activation(proj[:, U0 + t, :], proj[:, U0 + t, :], ACT.Gelu_apprx_tanh).then_inc(s_ge, 1)
                act.drain()
                act.wait_ge(s_y, ST)
                for t in range(4):
                    nc.scalar.activation(gh[:, t, :], proj[:, U0 + t, :], ACT.Copy).then_inc(s_gh, 1)
                hi(S_GLU + 1)
                for m in range(4):
                    t = tile[0]
                    tile[0] += 1
                    act.wait_ge(s_mm, t + 1)
                    if m >= 2:
                        act.wait_ge(s_yf, m - 1)
                    nc.scalar.activation(sg[:, m % 2, :], pg[:, t % 4, :], ACT.Sigmoid).then_inc(s_ev, 1)
                for m in range(4):
                    act.wait_ge(s_yf, m + 1)
                    nc.scalar.activation(ysh[:, m, :], proj[:, U0 + m, :], ACT.Copy).then_inc(s_yh, 1)
                act.wait_ge(s_used, S_GLU + 1)
                for i in range(4):
                    hi(S_GS + i + 1)
                    for m in range(2):
                        evac(merged[:, 2 * i + m, :], ACT.Sigmoid)
                tile[0] += 8
                hi(S_BS + 1)
                hi(S_BS + 2)
                for c in range(TT):
                    act.wait_ge(s_vt, TT)
                    nc.scalar.activation(proj[:, VR + c, :], pg[:, c, :], ACT.Copy).then_inc(s_vc, 1)
                act.drain()
                for h in range(RH):
                    nc.scalar.activation(proj[:, GR + h, :], proj[:, GR + h, :], ACT.Silu)
                act.drain()
                for h in range(RH):
                    act.wait_ge(s_o, h + 1)
                    if h >= 1:
                        act.wait_ge(s_yrl, h)
                    nc.scalar.activation(osb[:, :], py[:, :], ACT.Copy).then_inc(s_oc, 1)
                    act.wait_ge(s_ct, h + 1)
                    nc.scalar.activation(rsq[:, 0, :], osb[:, :], ACT.Square).then_inc(s_q2, 1)
                    act.wait_ge(s_r2, h + 1)
                    nc.scalar.activation(rsq[:, 1, :], rsq[:, 1, :], ACT.Sqrt).then_inc(s_rr, 1)
                    act.wait_ge(s_yr, h + 1)
                    nc.scalar.activation(yrh[:, h, :], osb[:, :], ACT.Copy).then_inc(s_yrh, 1)

                def gate_slabs(first):
                    for i in range(2):
                        for q in range(2):
                            hi(first + 3 * i + q + 1)
                            for m in range(2):
                                if i >= 1 and q == 0 and m == 0:
                                    act.wait_ge(s_mg, mg[0])
                                evac(gates[:, 2 * q + m, :], ACT.Sigmoid)
                        hi(first + 3 * i + 3)
                        tile[0] += 4
                        mg[0] += 4

                mg = [8]
                act.wait_ge(s_yrl, RH)
                gate_slabs(S_R)
                for c in range(TT):
                    act.wait_ge(s_vt, 2 * TT)
                    nc.scalar.activation(proj[:, VA + c, :], pg[:, c, :], ACT.Copy).then_inc(s_vc, 1)
                for i in range(8):
                    if i >= 2:
                        act.wait_ge(s_am, i - 1)
                    nc.scalar.activation(asq[:, i % 2, :], proj[:, QA + i, :], ACT.Square).then_inc(s_as, 1)
                    act.wait_ge(s_ar, i + 1)
                    nc.scalar.activation(asq[:, i % 2, :], asq[:, i % 2, :], ACT.Sqrt).then_inc(s_at, 1)
                    act.wait_ge(s_an, i + 1)
                for h in range(AH):
                    for i in range(TT):
                        g = TT * h + i
                        act.wait_ge(s_mx, g + 1)
                        if h >= 1 and i == 0:
                            act.wait_ge(s_tp, h)
                        nc.scalar.activation(pp[:, TRI[i]:TRI[i + 1]], pb[:, g % 2, 0:P * (i + 1)], ACT.Exp, bias=ast[:, 1, i:i + 1],
                                             scale=AD ** -0.5, accum_out=ast[:, 2, i:i + 1]).then_inc(s_ex, 1)
                    act.wait_ge(s_tp, h + 1)
                    if h >= 1:
                        act.wait_ge(s_pv, h)
                    for j in range(TT):
                        nc.scalar.activation(pt[:, DIAG[j]:DIAG[j + 1]], pg[:, j, P * j:L], ACT.Copy).then_inc(s_tc, 1)
                    if h % 2 == 1:
                        act.wait_ge(s_pv, h + 1)
                        nc.scalar.activation(yah[:, h // 2, :], py[:, :], ACT.Copy).then_inc(s_yah, 1)
                act.wait_ge(s_mg, mg[0])
                act.wait_ge(s_yal, 4)
                gate_slabs(S_A)
                for k in range(DK):
                    act.wait_ge(s_mg, 8 * 3)
                    act.wait_ge(s_used, S_O)
                    nc.scalar.activation(xh[:, k, :], merged[:, k, :], ACT.Copy).then_inc(s_mh, 1)
                for i in range(4):
                    if S_O + i + 1 < N_MIX + 1:
                        hi(S_O + i + 1)
                    tile[0] += 2
                act.wait_ge(s_ev, tile[0])
                norm(1)
                n = N_MIX
                for half in range(2):
                    for i in range(N_UP):
                        hi(n + 1)
                        n += 1
                        g = half * N_UP + i
                        for m in range(2):
                            t = tile[0]
                            tile[0] += 1
                            act.wait_ge(s_mm, t + 1)
                            if g >= 2:
                                act.wait_ge(s_hd, g - 1)
                            dst = (cg, cu)[m][:, g % 2, :]
                            f = m * FT + half * N_UP + i
                            nc.scalar.activation(dst, pg[:, t % 4, :], ACT.Identity, bias=pr[:, PAR["cb"][0] + f:PAR["cb"][0] + f + 1],
                                                 scale=pr[:, PAR["cw"][0] + 2 * 2 * FT + f:PAR["cw"][0] + 2 * 2 * FT + f + 1]).then_inc(s_c0, 1)
                        act.wait_ge(s_c1, 2 * g + 1)
                        nc.scalar.activation(cg[:, g % 2, :], cg[:, g % 2, :], ACT.Silu).then_inc(s_si, 1)
                        act.wait_ge(s_hd, g + 1)
                        if half == 1 and i == 0:
                            act.wait_ge(s_used, n - 1)
                        nc.scalar.activation(hh[:, i, :], ht[:, g % 2, :], ACT.Copy).then_inc(s_hh, 1)
                    for i in range(N_DOWN):
                        hi(n + 1)
                        n += 1
                        tile[0] += 1
                layer_end(act)

        @block.vector
        def _(dve):
            V = nc.vector

            def norm(i, g):
                dve.wait_ge(s_ss[i], DK)
                V.tensor_scalar(rstd[:, :], pn[:, :], 1.0 / D, EPS, ALU.mult, ALU.add)
                dve.drain()
                V.reciprocal(rstd[:, :], rstd[:, :]).then_inc(s_rc[i], 1)
                dve.wait_ge(s_rt[i], 1)
                dve.wait_ge(s_par, 48)
                for k in range(DK + 1):
                    if k < DK:
                        V.scalar_tensor_tensor(xn[:, k % 2, :], x[:, k, :], prm(g)[:, k:k + 1], rstd[:, :], ALU.mult, ALU.mult)\
                         .then_inc(s_xn[i], 1)
                    if k >= 1:
                        dve.wait_ge(s_xh[i], k)
                        V.tensor_tensor(xl[:, k - 1, :], xn[:, (k - 1) % 2, :], xh[:, k - 1, :].bitcast(F32), ALU.subtract)\
                         .then_inc(s_xl[i], 1)
                        dve.drain()

            def tt(out, a, b, op):
                V.tensor_tensor(out, a, b, op)
                return dve.drain()

            def s5_prepare():
                dve.wait_ge(s_dt, 1)
                dve.wait_ge(s_par, 48)
                dt, lre, lim = sm[:, 0, :], prm("lre"), prm("lim")
                tt(sm[:, 1, :], lre, dt, ALU.mult).then_inc(s_th, 1)
                tt(sm[:, 3, :], lim, dt, ALU.mult)
                two_pi = 2 * np.pi
                c1 = float(np.float32(6.28125))
                c2 = float(np.float32(two_pi - c1))
                c2 = float(np.float32(np.floor(c2 * 2 ** 22) / 2 ** 22))
                c3 = float(np.float32(two_pi - c1 - c2))
                big = float(1.5 * 2 ** 23)
                V.tensor_scalar(sm[:, 7, :], sm[:, 3, :], float(np.float32(1 / two_pi)), big, ALU.mult, ALU.add)
                dve.drain()
                V.tensor_scalar(sm[:, 7, :], sm[:, 7, :], -big, None, ALU.add)
                dve.drain()
                for c in (c1, c2, c3):
                    V.scalar_tensor_tensor(sm[:, 3, :], sm[:, 7, :], -c, sm[:, 3, :], ALU.mult, ALU.add)
                    dve.drain()
                V.tensor_scalar(sm[:, 4, :], sm[:, 3, :], float(np.float32(3.1415925)), float(np.float32(-3.1415925)), ALU.min, ALU.max)
                dve.drain().then_inc(s_th, 1)
                dve.wait_ge(s_sc, 1)
                dve.wait_ge(s_dt, 2)
                sin, sh, r = sm[:, 5, :], sm[:, 6, :], sm[:, 2, :]
                cos = sm[:, 8, :]
                tt(cos, sh, sh, ALU.mult)
                V.tensor_scalar(cos, cos, -2.0, 1.0, ALU.mult, ALU.add)
                dve.drain()
                nre, nim, den, fr, fi, t1, t2 = [sm[:, 9 + i, :] for i in range(7)]
                tt(nre, cos, r, ALU.mult)
                V.tensor_scalar(nre, nre, -1.0, None, ALU.add)
                tt(nim, sin, r, ALU.mult)
                tt(t1, lre, lre, ALU.mult)
                tt(t2, lim, lim, ALU.mult)
                tt(den, t1, t2, ALU.add)
                V.reciprocal(den, den)
                tt(t1, nre, lre, ALU.mult)
                tt(t2, nim, lim, ALU.mult)
                tt(fr, t1, t2, ALU.add)
                tt(fr, fr, den, ALU.mult)
                tt(t1, nim, lre, ALU.mult)
                tt(t2, nre, lim, ALU.mult)
                tt(fi, t1, t2, ALU.subtract)
                tt(fi, fi, den, ALU.mult)
                frb = fr.unsqueeze(2).to_broadcast([P, ST, CH])
                fib = fi.unsqueeze(2).to_broadcast([P, ST, CH])
                q1, q2 = p1[:, 0, :].rearrange("p (s c) -> p s c", s=ST), p1[:, 1, :].rearrange("p (s c) -> p s c", s=ST)
                tt(q1, cw_[:, 0, :, :], fib, ALU.mult)
                tt(q2, cw_[:, 1, :, :], fib, ALU.mult)
                tt(cw_[:, 0, :, :], cw_[:, 0, :, :], frb, ALU.mult)
                tt(cw_[:, 1, :, :], cw_[:, 1, :, :], frb, ALU.mult)
                tt(cw_[:, 0, :, :], cw_[:, 0, :, :], q2, ALU.subtract)
                tt(cw_[:, 1, :, :], cw_[:, 1, :, :], q1, ALU.add)
                V.tensor_scalar(cw_[:, 1, :, :], cw_[:, 1, :, :], -1.0, None, ALU.mult)
                dve.drain().then_inc(s_cc, 1)
                V.tensor_copy(pw[:, 0, 0, :], cos)
                V.tensor_copy(pw[:, 1, 0, :], sin)
                dve.drain()
                for n in range(1, LEVELS):
                    c, s = pw[:, 0, n - 1, :], pw[:, 1, n - 1, :]
                    tt(t1, c, c, ALU.mult)
                    tt(t2, s, s, ALU.mult)
                    tt(pw[:, 0, n, :], t1, t2, ALU.subtract)
                    V.scalar_tensor_tensor(pw[:, 1, n, :], c, 2.0, s, ALU.mult, ALU.mult)
                    dve.drain()
                V.memset(ph0[:, :, 0, 0:1], 1.0)
                V.memset(ph0[:, :, 1, 0:1], 0.0)
                dve.drain()
                n = 1
                lv = 0
                while n < BASE:
                    c = pw[:, 0, lv, :].unsqueeze(2).to_broadcast([P, ST, n])
                    s = pw[:, 1, lv, :].unsqueeze(2).to_broadcast([P, ST, n])
                    q1 = p1[:, 0, 0:ST * n].rearrange("p (s c) -> p s c", s=ST)
                    q2 = p1[:, 1, 0:ST * n].rearrange("p (s c) -> p s c", s=ST)
                    C, S = ph0[:, :, 0, 0:n], ph0[:, :, 1, 0:n]
                    C2, S2 = ph0[:, :, 0, n:2 * n], ph0[:, :, 1, n:2 * n]
                    tt(q1, C, c, ALU.mult)
                    tt(q2, S, s, ALU.mult)
                    tt(C2, q1, q2, ALU.subtract)
                    tt(q1, C, s, ALU.mult)
                    tt(q2, S, c, ALU.mult)
                    tt(S2, q1, q2, ALU.add)
                    n *= 2
                    lv += 1

            def s5_tile(s):
                V.tensor_copy(ph[:, :, 0:BASE], ph0[:, s, :, :])
                dve.drain()
                n, lv = BASE, 5
                while n < L:
                    c, sn = pw[:, 0, lv, s:s + 1], pw[:, 1, lv, s:s + 1]
                    V.tensor_scalar(p1[:, :, 0:n], ph[:, :, 0:n], sn, None, ALU.mult)
                    dve.drain()
                    V.scalar_tensor_tensor(ph[:, 0, n:2 * n], ph[:, 0, 0:n], c, p1[:, 1, 0:n], ALU.mult, ALU.subtract)
                    V.scalar_tensor_tensor(ph[:, 1, n:2 * n], ph[:, 1, 0:n], c, p1[:, 0, 0:n], ALU.mult, ALU.add)
                    dve.drain()
                    n *= 2
                    lv += 1
                C = ph[:, 0:1, :].to_broadcast([P, 2, L])
                S = ph[:, 1:2, :].to_broadcast([P, 2, L])
                dve.wait_ge(s_bu, s + 1)
                V.tensor_tensor(p1[:, :, :], pb[:, :, :], C, ALU.mult)
                V.tensor_tensor(p2[:, :, :], pb[:, :, :], S, ALU.mult)
                dve.drain().then_inc(s_rot, 1)
                V.tensor_tensor(zz[:, 0, :], p1[:, 0, :], p2[:, 1, :], ALU.add)
                V.tensor_tensor(zz[:, 1, :], p1[:, 1, :], p2[:, 0, :], ALU.subtract)
                dve.drain()
                r = sm[:, 2, s:s + 1].to_broadcast([P, L])
                V.tensor_tensor_scan(zz[:, 0, :], r, zz[:, 0, :], 0.0, ALU.mult, ALU.add)
                V.tensor_tensor_scan(zz[:, 1, :], r, zz[:, 1, :], 0.0, ALU.mult, ALU.add)
                dve.drain()
                V.tensor_tensor(p1[:, :, :], zz[:, :, :], C, ALU.mult)
                V.tensor_tensor(p2[:, :, :], zz[:, :, :], S, ALU.mult)
                dve.drain()
                if s >= 1:
                    dve.wait_ge(s_y, s)
                V.tensor_tensor(stt[:, 0, :], p1[:, 0, :], p2[:, 1, :], ALU.subtract)
                V.tensor_tensor(stt[:, 1, :], p1[:, 1, :], p2[:, 0, :], ALU.add).then_inc(s_st, 1)
                dve.drain()

            def s5_channels(t):
                dve.wait_ge(s_y, 4 * t + 4)
                V.scalar_tensor_tensor(proj[:, U0 + t, :], proj[:, U0 + t, :], prm("d")[:, t:t + 1], py[:, :], ALU.mult, ALU.add)\
                 .then_inc(s_yp, 1)

            def retention():
                for i, tl in enumerate((QR, QR + 1, KR, KR + 1)):
                    sc = 1.0 if i < 2 else RQ ** -0.5
                    dve.wait_ge(s_sw, i + 1)
                    V.scalar_tensor_tensor(rsq[:, 0, :], pb[:, i % 2, :], sc, r_sin, ALU.mult, ALU.mult)
                    V.scalar_tensor_tensor(proj[:, tl, :], proj[:, tl, :], sc, r_cos, ALU.mult, ALU.mult)
                    dve.drain()
                    V.tensor_tensor(proj[:, tl, :], proj[:, tl, :], rsq[:, 0, :], ALU.add).then_inc(s_ro, 1)
                    dve.drain()
                for h in range(RH):
                    for j in range(TT):
                        g = TT * h + j
                        dve.wait_ge(s_rs, g + 1)
                        if j == 0 and h >= 1:
                            dve.wait_ge(s_o, h)
                        V.tensor_tensor(sd[:, DIAG[j]:DIAG[j + 1]], pb[:, g % 2, P * j:L], decay[:, h, 0:L - P * j], ALU.mult)\
                         .then_inc(s_rd, 1)
                    dve.wait_ge(s_mu, h + 1)
                    V.tensor_tensor(osb[:, :], osb[:, :], pn[:, :], ALU.subtract).then_inc(s_ct, 1)
                    dve.wait_ge(s_va, h + 1)
                    V.tensor_scalar(rsq[:, 1, :], pn[:, :], EPS, None, ALU.add)
                    dve.drain()
                    V.reciprocal(rsq[:, 1, :], rsq[:, 1, :]).then_inc(s_r2, 1)
                    dve.wait_ge(s_rr, h + 1)
                    V.scalar_tensor_tensor(osb[:, :], osb[:, :], prm("gn")[:, h:h + 1], rsq[:, 1, :], ALU.mult, ALU.mult)
                    dve.drain()
                    V.tensor_tensor(osb[:, :], osb[:, :], proj[:, GR + h, :], ALU.mult).then_inc(s_yr, 1)
                    dve.wait_ge(s_yrh, h + 1)
                    V.tensor_tensor(yrl[:, h, :], osb[:, :], yrh[:, h, :].bitcast(F32), ALU.subtract).then_inc(s_yrl, 1)

            def attention():
                for i in range(8):
                    a = asq[:, i % 2, :]
                    dve.wait_ge(s_am, i + 1)
                    V.tensor_scalar(a, pb[:, i % 2, :], EPS, None, ALU.add)
                    dve.drain()
                    V.reciprocal(a, a).then_inc(s_ar, 1)
                    dve.wait_ge(s_at, i + 1)
                    g = prm("qn") if i < 4 else prm("kn")
                    V.scalar_tensor_tensor(proj[:, QA + i, :], proj[:, QA + i, :], g, a, ALU.mult, ALU.mult).then_inc(s_an, 1)
                for i in range(8):
                    a = asq[:, i % 2, :]
                    dve.wait_ge(s_ap, i + 1)
                    dve.drain()
                    V.tensor_tensor(a, pb[:, i % 2, :], a_sin, ALU.mult)
                    V.tensor_tensor(proj[:, QA + i, :], proj[:, QA + i, :], a_cos, ALU.mult)
                    dve.drain()
                    V.tensor_tensor(proj[:, QA + i, :], proj[:, QA + i, :], a, ALU.add).then_inc(s_ax, 1)
                for h in range(AH):
                    for i in range(TT + 1):
                        if i < TT:
                            g = TT * h + i
                            dve.wait_ge(s_sc_, g + 1)
                            s = pb[:, g % 2, 0:P * (i + 1)]
                            diag = pb[:, g % 2, P * i:P * (i + 1)]
                            V.tensor_tensor(diag, diag, mask, ALU.add)
                            dve.drain()
                            V.reduce_max(ast[:, 0, i:i + 1], s, AX_X)
                            dve.drain()
                            V.tensor_scalar(ast[:, 1, i:i + 1], ast[:, 0, i:i + 1], -(AD ** -0.5), None, ALU.mult).then_inc(s_mx, 1)
                        if i >= 1:
                            q = i - 1
                            dve.wait_ge(s_ex, TT * h + q + 1)
                            V.reciprocal(ast[:, 3, q:q + 1], ast[:, 2, q:q + 1])
                            dve.drain()
                            V.tensor_scalar(pp[:, TRI[q]:TRI[q + 1]], pp[:, TRI[q]:TRI[q + 1]], ast[:, 3, q:q + 1], None, ALU.mult)\
                             .then_inc(s_pn, 1)
                    if h % 2 == 1:
                        dve.wait_ge(s_yah, h // 2 + 1)
                        V.tensor_tensor(yal[:, h // 2, :], py[:, :], yah[:, h // 2, :].bitcast(F32), ALU.subtract).then_inc(s_yal, 1)

            def merge(i, first):
                for m in range(4):
                    t = tile[0]
                    tile[0] += 1
                    dve.wait_ge(s_mm, t + 1)
                    o = merged[:, 4 * i + m, :]
                    if first:
                        dve.wait_ge(s_ev, t)
                        V.tensor_tensor(o, o, pg[:, t % 4, :], ALU.mult)
                        dve.drain().then_inc(s_ev, 1)
                        V.engine_nop().then_inc(s_mg, 1) if False else dve.drain().then_inc(s_mg, 1)
                    else:
                        V.tensor_tensor(mt[:, m % 2, :], pg[:, t % 4, :], gates[:, m, :], ALU.mult)
                        dve.drain().then_inc(s_ev, 1)
                        V.tensor_tensor(o, o, mt[:, m % 2, :], ALU.add)
                        dve.drain().then_inc(s_mg, 1)

            def residual(k):
                t = tile[0]
                tile[0] += 1
                dve.wait_ge(s_mm, t + 1)
                V.tensor_tensor(x[:, k, :], x[:, k, :], pg[:, t % 4, :], ALU.add).then_inc(s_ev, 1)

            with dve.Fori(0, DEPTH) as l:
                tile = [0]
                norm(0, "g1")
                s5_prepare()
                for s in range(ST):
                    s5_tile(s)
                    if s % 4 == 3:
                        s5_channels(s // 4)
                for t in range(4):
                    dve.wait_ge(s_gh, t + 1)
                    V.tensor_tensor(gl[:, t, :], proj[:, U0 + t, :], gh[:, t, :].bitcast(F32), ALU.subtract).then_inc(s_gl, 1)
                tile[0] += 2 * N_PROJ
                for m in range(4):
                    dve.wait_ge(s_ev, tile[0] + m + 1)
                    V.tensor_tensor(proj[:, U0 + m, :], proj[:, U0 + m, :], sg[:, m % 2, :], ALU.mult).then_inc(s_yf, 1)
                for m in range(4):
                    dve.wait_ge(s_yh, m + 1)
                    V.tensor_tensor(ysl[:, m, :], proj[:, U0 + m, :], ysh[:, m, :].bitcast(F32), ALU.subtract).then_inc(s_yl, 1)
                tile[0] += 4 + 8
                for i in range(2):
                    merge(i, True)
                retention()
                for i in range(2):
                    tile[0] += 4
                    dve.wait_ge(s_ev, tile[0])
                    merge(i, False)
                attention()
                for i in range(2):
                    tile[0] += 4
                    dve.wait_ge(s_ev, tile[0])
                    merge(i, False)
                for k in range(DK):
                    dve.wait_ge(s_mh, k + 1)
                    V.tensor_tensor(xl[:, k, :], merged[:, k, :], xh[:, k, :].bitcast(F32), ALU.subtract).then_inc(s_ml, 1)
                for k in range(DK):
                    residual(k)
                norm(1, "g2")
                dve.drain()
                for half in range(2):
                    for i in range(N_UP):
                        g = half * N_UP + i
                        for m in range(2):
                            t = tile[0]
                            tile[0] += 1
                            dve.wait_ge(s_c0, 2 * g + m + 1)
                            dst = (cg, cu)[m]
                            f = m * FT + half * N_UP + i
                            for tap, sh in ((1, 1), (0, 2)):
                                w = pr[:, PAR["cw"][0] + tap * 2 * FT + f:PAR["cw"][0] + tap * 2 * FT + f + 1]
                                V.scalar_tensor_tensor(dst[:, g % 2, sh:L], pg[:, t % 4, 0:L - sh], w, dst[:, g % 2, sh:L],
                                                       ALU.mult, ALU.add)
                                dr = dve.drain()
                            dr.then_inc(s_ev, 1)
                            dve.drain().then_inc(s_c1, 1)
                        dve.wait_ge(s_si, g + 1)
                        if g >= 2:
                            dve.wait_ge(s_hh, g - 1)
                        V.tensor_tensor(ht[:, g % 2, :], cg[:, g % 2, :], cu[:, g % 2, :], ALU.mult).then_inc(s_hd, 1)
                        dve.wait_ge(s_hh, g + 1)
                        V.tensor_tensor(hl[:, i, :], ht[:, g % 2, :], hh[:, i, :].bitcast(F32), ALU.subtract).then_inc(s_hl, 1)
                        dve.drain()
                    for k in range(N_DOWN):
                        residual(k)
                layer_end(dve)


def constants():
    f = np.float32
    p = np.arange(P)
    t = np.arange(L)
    lg = np.log1p(-np.exp2(f(-5.0) - np.arange(RH, dtype=f))).astype(f)
    rel = (t[None, :] - p[:, None]).astype(f)
    decay = np.where(rel[None] >= 0, np.exp(lg[:, None, None] * np.maximum(rel, 0)[None]), 0).astype(f)
    decay = decay.transpose(1, 0, 2).reshape(P, RH * L)
    half = RQ // 2
    inv = (f(1.0) / (f(10000.0) ** np.linspace(0.0, 1.0, half, dtype=f))).astype(f)
    ang = inv[p % half][:, None] * t[None, :].astype(f)
    r_cos, r_sin = np.cos(ang).astype(f), np.sin(ang).astype(f)
    rh = AD // 4 // 2
    inva = (f(500000.0) ** (-np.arange(rh, dtype=f) / f(rh))).astype(f)
    d = p % AD
    turned = (d < 2 * rh)[:, None]
    anga = inva[d % rh][:, None] * t[None, :].astype(f)
    a_cos = np.where(turned, np.cos(anga), 1).astype(f)
    a_sin = np.where(turned, np.sin(anga), 0).astype(f)
    ident = np.eye(P, dtype=f)

    def swap(h, block):
        m = np.zeros((P, P), f)
        for o in range(P):
            q = o % block
            if q < h:
                m[o + h, o] = -1.0
            elif q < 2 * h:
                m[o - h, o] = 1.0
        return m

    blk = np.where(p[:, None] // AD == p[None, :] // AD, 1.0 / AD, 0.0).astype(f)
    mask = np.where(p[None, :] <= p[:, None], 0.0, MASKED).astype(f)
    return np.ascontiguousarray(np.concatenate(
        [decay, r_cos, r_sin, a_cos, a_sin, ident, swap(half, RQ), swap(rh, AD), np.ones((P, P), f), blk,
         np.full((P, P), 1.0 / P, f), mask], axis=1).astype(f))


def kernel(x, norm1_g, w_in, ssm_lambda_re, ssm_lambda_im, ssm_log_dt, ssm_b_re, ssm_b_im, ssm_c_re, ssm_c_im, ssm_d,
           ssm_w_glu, ret_gn_g, attn_qn_g, attn_kn_g, w_br_ssm, w_br_ret, w_br_att, w_o, norm2_g, ffn_w_up, ffn_conv_w,
           ffn_conv_b, ffn_w_down):
    import numpy as _np
    import concourse.bacc as _bacc
    from concourse import mybir as _mybir
    from concourse.bass_utils import run_bass_kernel_spmd as _run

    A = _np.asarray

    def slabs(w, cols):
        w = A(w)
        n, k, c = w.shape
        return w.reshape(n, k // P, P, c // cols, cols).transpose(0, 3, 2, 1, 4).reshape(n, c // cols, P, -1)

    w_in = A(w_in)
    main = slabs(w_in[:, :, :2 * P * N_PROJ], 2 * P)
    g0 = 2 * P * N_PROJ
    gate = [slabs(w_in[:, :, g0 + D * i:g0 + D * (i + 1)], 2 * P) for i in range(3)]
    br = [slabs(w, 4 * P) for w in (w_br_ssm, w_br_ret, w_br_att)]
    up = A(ffn_w_up).reshape(DEPTH, D, 2, FT, P).transpose(0, 1, 3, 2, 4).reshape(DEPTH, D, 2 * FH)
    parts = [main, slabs(ssm_w_glu, 4 * P), gate[0], br[0]]
    for i in (1, 2):
        parts += [gate[i][:, 0:2], br[i][:, 0:1], gate[i][:, 2:4], br[i][:, 1:2]]
    parts += [slabs(w_o, 2 * P), slabs(up, 2 * P)]
    wslab = _np.ascontiguousarray(_np.concatenate(parts, axis=1))
    wd = A(ffn_w_down).reshape(DEPTH, 2, FHALF, P, DK, P).transpose(0, 1, 4, 3, 2, 5)
    wdown = _np.ascontiguousarray(wd.reshape(DEPTH, 2 * DK, P, DOWN))

    def cols(a, n):
        return A(a).reshape(DEPTH, n, P).transpose(0, 2, 1)

    ldt = _np.repeat(A(ssm_log_dt)[:, :, None], SSM_P, axis=2)
    cw = A(ffn_conv_w).reshape(DEPTH, 3, 2 * FT, P).transpose(0, 3, 1, 2).reshape(DEPTH, P, -1)
    par = _np.ascontiguousarray(_np.concatenate(
        [cols(norm1_g, DK), cols(norm2_g, DK), cols(ret_gn_g, RH),
         _np.concatenate([A(attn_qn_g)] * 2, axis=1)[:, :, None], _np.concatenate([A(attn_kn_g)] * 2, axis=1)[:, :, None],
         cols(ssm_d, 4), cols(ssm_lambda_re, ST), cols(ssm_lambda_im, ST), cols(ldt, ST), cw, cols(ffn_conv_b, 2 * FT),
         _np.zeros((DEPTH, P, N_PAR - _at), _np.float32)], axis=2))
    bblk = _np.zeros((DEPTH, P, 2, 4, P), _np.float32)
    cblk = _np.zeros((DEPTH, P, 2, ST, CH), _np.float32)
    for i, (b, c) in enumerate(((ssm_b_re, ssm_c_re), (ssm_b_im, ssm_c_im))):
        b, c = A(b), A(c)
        for s in range(ST):
            for g in range(2):
                st, ch = slice(SSM_P * g, SSM_P * (g + 1)), slice(SSM_H * g, SSM_H * (g + 1))
                row = CH * (s % 4) + SSM_H * g
                bblk[:, row:row + SSM_H, i, s // 4, st] = b[:, 2 * s + g].transpose(0, 2, 1)
                cblk[:, st, i, s, ch] = c[:, 2 * s + g].transpose(0, 2, 1)
    xT = _np.ascontiguousarray(A(x)[0].T.reshape(DK, P, L).transpose(1, 0, 2))
    arrays = {"xT": xT, "wslab": wslab, "wdown": wdown, "par": par, "bblk": bblk, "cblk": cblk, "cst": constants()}

    nc = _bacc.Bacc("TRN2", target_bir_lowering=False, num_devices=1, dynamic_dma_scratch_size=4096)
    args = [nc.dram_tensor(f"in_{n}", a.shape, _mybir.dt.from_np(a.dtype), kind="ExternalInput").ap() for n, a in arrays.items()]
    args.append(nc.dram_tensor("out_T", (P, DK, L), _mybir.dt.float32, kind="ExternalOutput").ap())
    hybrid_trunk(nc, *args)
    r = _run(nc, [{f"in_{n}": a for n, a in arrays.items()}], core_ids=[0])
    o = r.results[0]["out_T"]
    return _np.ascontiguousarray(o.transpose(1, 0, 2).reshape(D, L).T)[None]
```

```python
from contextlib import ExitStack

import numpy as np

import concourse.bass as bass
from concourse import mybir

F32 = mybir.dt.float32
F32R = mybir.dt.float32r
ALU = mybir.AluOpType
ACT = mybir.ActivationFunctionType
AX_X = mybir.AxisListType.X

P = 128
EPS = 1e-6
MASKED = -1e30

DEPTH = 2
D = 1024
L = 512
DK = D // P
SSM_W = 512
SSM_H = 16
SSM_P = 64
ST = SSM_W // SSM_H * SSM_P // P
CH = 2 * SSM_H
RH = 4
RQ = 64
AH = 8
AD = 64
FH = 2816
FT = FH // P
TT = L // P

SLAB = 1024
RAW = 2
RING = 4
N_PROJ = 28
SEGS = (8, 8, FT - 16)
STREAM = []


def _stream(kind, n, kt, mt):
    first = len(STREAM)
    STREAM.extend([(kind, kt, mt)] * n)
    return first


S_PROJ = _stream("proj", N_PROJ, DK, 1)
S_GS = _stream("gate", DK, DK, 1)
S_GLU = _stream("glu", 2, 4, 2)
S_BS = _stream("branch", 4, 4, 2)
S_R = len(STREAM)
for _i in range(2):
    _stream("gate", 4, DK, 1)
    _stream("branch", 2, 4, 2)
S_A = len(STREAM)
for _i in range(2):
    _stream("gate", 4, DK, 1)
    _stream("branch", 2, 4, 2)
S_O = _stream("residual", DK, DK, 1)
S_UP0 = _stream("up", 2 * SEGS[0], DK, 1)
S_UP1 = _stream("up", 2 * SEGS[1], DK, 1)
S_DN0 = _stream("residual", DK, SEGS[0], 1)
S_UP2 = _stream("up", 2 * SEGS[2], DK, 1)
S_DN1 = _stream("residual", DK, SEGS[1], 1)
S_DN2 = _stream("residual", DK, SEGS[2], 1)
N_SLABS = len(STREAM)
P3 = list(range(S_GS, S_A))


def width(n):
    return STREAM[n][1] * STREAM[n][2] * P


def tile_of(n):
    return sum(mt for _, _, mt in STREAM[:n])


OWNER = ["act" if kind in ("proj", "gate", "glu") else "dve" for kind, _, mt in STREAM for _ in range(mt)]


def evacuated(t):
    return OWNER[t], OWNER[:t + 1].count(OWNER[t])


_widths = [("g1", DK), ("g2", DK), ("gn", RH), ("qn", 1), ("kn", 1), ("d", 4), ("lre", ST), ("lim", ST),
           ("ldt", ST), ("cw", 3 * 2 * FT), ("cb", 2 * FT)]
PAR = {}
_at = 0
for _n, _w in _widths:
    PAR[_n] = (_at, _at + _w)
    _at += _w
N_PAR = -(-_at // 8) * 8

U0, QR, KR, VR, GR, QA, KA, VA = 0, 4, 6, 8, 12, 16, 20, 24

LEVELS = 9
BASE = 32
DIAG = [sum(L - P * i for i in range(j)) for j in range(TT + 1)]
TRI = [P * i * (i + 1) // 2 for i in range(TT + 1)]

N_RING = 4 + 4 + TT * RH + 2 * RH

RET0 = 17
HEAD0 = 10


def hybrid_trunk(nc, xT, wslab, par, bblk, cblk, cst, outT):
    ctx = ExitStack()
    with ctx:
        def sb(name, shape, dt=F32):
            return ctx.enter_context(nc.sbuf_tensor(name, shape, dt))

        sems = []

        def sem(name):
            s = ctx.enter_context(nc.semaphore(name))
            sems.append(s)
            return s

        x = sb("x_res", [P, DK, L])
        xh = sb("xn_hi", [P, DK, L], F32R)
        xl = sb("xn_lo", [P, DK, L], F32R)
        raw = sb("w_raw", [P, RAW, SLAB])
        wh = sb("w_hi", [P, RING, SLAB], F32R)
        wl = sb("w_lo", [P, RING, SLAB], F32R)
        consts = sb("consts", [P, cst.shape[1]])
        pr = sb("params", [P, N_PAR])
        off = 0

        def const(width):
            nonlocal off
            off += width
            return consts[:, off - width:off]

        decay = const(RH * L).rearrange("p (h t) -> p h t", h=RH)
        r_cos, r_sin, a_cos, a_sin = const(L), const(L), const(L), const(L)
        ident, r_swap, a_swap, ones, blk64, mask = [const(P) for _ in range(6)]

        def prm(name):
            return pr[:, PAR[name][0]:PAR[name][1]]

        base = nc.sbuf_base
        KB = 1024
        arena = sb("arena", [P, int((2 * N_PROJ + 55.5) * KB) // 4])

        def at(name, kb, shape, dt=F32):
            return nc.alloc_sbuf_tensor_at(name, shape, dt, offset=base + int(kb * KB))

        W0 = 2 * N_PROJ
        proj = at("proj", 0, [P, N_PROJ, L])
        ssum = at("sq_sum", W0 + 53, [P, L])
        sq = at("sq", W0 + 49, [P, 2, L])
        rstd = at("rstd", W0 + 45, [P, L])
        xn = at("xn", W0, [P, 4, L])
        ph = at("phase", W0, [P, 2, 2, L])
        zz = at("scan", W0 + 8, [P, 2, 2, L])
        p2 = at("prod", W0 + 16, [P, 2, L])
        pq = at("prod_back", W0 + 20, [P, 2, L])
        stt = at("states", W0 + 24, [P, 2, L])
        bw = at("b_blocks", W0 + 28, [P, 2, 4, P])
        cw_ = at("c_blocks", W0 + 32, [P, 2, ST, CH])
        ph0 = at("phase_base", W0 + 36, [P, ST, 2, BASE])
        pw = at("powers", W0 + 40, [P, 2, LEVELS, ST])
        sm = at("s5_small", W0 + 41.25, [P, 20, ST])
        sd = at("ret_scores", W0 + 42.5, [P, DIAG[TT]])
        osb = at("ret_out", W0 + 47.5, [P, 2, L])
        rsq = at("ret_sq", W0 + 51.5, [P, 2, L])
        yrh = at("yr_hi", 2 * GR, [P, 4, L], F32R)
        yrl_ = at("yr_lo", 2 * QR, [P, 4, L], F32R)
        yrl = [yrl_[:, i, :] for i in (0, 2, 1, 3)]
        gh = at("gelu_hi", W0, [P, 4, L], F32R)
        gl = at("gelu_lo", W0 + 8, [P, 4, L], F32R)
        sg = at("glu_sig", W0 + 49, [P, 2, L])
        ysh = at("ys_hi", 2 * U0, [P, 4, L], F32R)
        ysl = at("ys_lo", 2 * VR, [P, 4, L], F32R)
        merged = at("merged", W0 + 16, [P, DK, L])
        gates = at("gates", W0, [P, 4, L])
        mt = at("merge_tmp", W0 + 8, [P, 2, L])
        pp = at("probs", W0 + 32, [P, TRI[TT]])
        pt = at("probs_t", W0 + 37, [P, TT, L])
        asq = at("attn_sq", W0 + 45, [P, 2, L])
        atmp = at("attn_tmp", W0 + 32, [P, L])
        ast = at("attn_stat", W0 + 53, [P, 4, 2])
        yah = at("ya_hi", 2 * QA, [P, 4, L], F32R)
        yal = at("ya_lo", 2 * KA, [P, 4, L], F32R)
        hh = at("hid_hi", 0, [P, 2, 8, L], F32R)
        hl = at("hid_lo", 32, [P, 2, 8, L], F32R)
        cg = at("conv_g", 64, [P, 2, L])
        cu = at("conv_u", 68, [P, 2, L])
        ht = at("hid", 72, [P, 2, L])

        pg = ctx.enter_context(nc.psum_tensor("ps_gemm", [P, 2, L], F32))
        pb = ctx.enter_context(nc.psum_tensor("ps_pair", [P, 2, L], F32))
        py = ctx.enter_context(nc.psum_tensor("ps_out", [P, L], F32))
        pr2 = ctx.enter_context(nc.psum_tensor("ps_ring", [P, 2, L], F32))
        po = ctx.enter_context(nc.psum_tensor("ps_out2", [P, L], F32))

        s_x = ctx.enter_context(nc.semaphore("x_loaded"))
        s_store = ctx.enter_context(nc.semaphore("stored"))
        s_go = ctx.enter_context(nc.semaphore("layer_go"))
        s_ack = ctx.enter_context(nc.semaphore("layer_ack"))
        s_q0, s_s0 = [ctx.enter_context(nc.semaphore(n)) for n in ("first_sq", "first_ssum")]
        s_par = sem("params_in")
        s_raw = [sem(f"raw_in{i}") for i in range(RAW)]
        s_hi, s_lo = sem("w_hi_done"), sem("w_lo_done")
        s_mm = sem("gemm_done")
        s_ev = {"act": sem("evacuated_by_act"), "dve": sem("evacuated_by_dve")}
        s_sq = [sem("sq_a"), sem("sq_b")]
        s_su = [sem("sq_summed_a"), sem("sq_summed_b")]
        s_ss = [sem("ssum_a"), sem("ssum_b")]
        s_rc = [sem("recip_a"), sem("recip_b")]
        s_rt = [sem("rstd_a"), sem("rstd_b")]
        s_xn = [sem("xn_a"), sem("xn_b")]
        s_xh = [sem("xh_a"), sem("xh_b")]
        s_xl = [sem("xl_a"), sem("xl_b")]
        s_dt, s_th, s_sc = sem("s5_exp"), sem("s5_theta"), sem("s5_sincos")
        s_cc = sem("c_scaled")
        s_bu, s_rot, s_zz = sem("bu_done"), sem("bu_rotated"), sem("scanned")
        s_bk, s_st, s_y, s_yp = sem("scan_read"), sem("states_ready"), sem("y_done"), sem("y_pre")
        s_gh, s_gl = sem("gelu_hi_s"), sem("gelu_lo_s")
        s_yf, s_yh, s_yl = sem("ys_full"), sem("ys_hi_s"), sem("ys_lo_s")
        s_mg = sem("merged_part")
        s_mh, s_ml = sem("merged_hi"), sem("merged_lo")
        s_rr2, s_rd2 = sem("ring_filled"), sem("ring_read")
        s_ro, s_vc = sem("ret_rotated"), sem("v_copied")
        s_rd, s_o, s_oc = sem("ret_decayed"), sem("ret_o"), sem("ret_o_copied")
        s_mu, s_ct, s_q2, s_va, s_r2, s_rr = (sem("gn_mean"), sem("gn_centred"), sem("gn_square"), sem("gn_var"),
                                              sem("gn_recip"), sem("gn_rstd"))
        s_yr, s_yrh, s_yrl = sem("yr_full"), sem("yr_hi_s"), sem("yr_lo_s")
        s_as, s_am, s_ar, s_at, s_an = (sem("att_sq"), sem("att_ms"), sem("att_recip"), sem("att_rstd"), sem("att_normed"))
        s_ap, s_ax = sem("att_swapped"), sem("att_rotated")
        s_sc_, s_mx, s_ex, s_pn = sem("att_scores"), sem("att_max"), sem("att_exp"), sem("att_probs")
        s_vt, s_va2 = sem("att_v_transposed"), sem("att_v_copied")
        s_tp, s_tc, s_pv, s_yah, s_yal = (sem("att_transposed"), sem("att_t_copied"), sem("att_pv"), sem("ya_hi_s"), sem("ya_lo_s"))
        s_c0, s_c1, s_si, s_hd, s_hh, s_hl = (sem("conv_first"), sem("conv_done"), sem("silu"), sem("hidden"),
                                              sem("hid_hi_s"), sem("hid_lo_s"))
        s_end = sem("layer_end")
        nums = sorted(s.num if hasattr(s, "num") else int(s) for s in sems)
        assert nums == list(range(nums[0], nums[-1] + 1)), nums
        ENGINES = 5

        def layer_end(eng):
            eng.drain().then_inc(s_end, 1)
            eng.wait_ge(s_go, 1)
            eng.drain().then_inc(s_ack, 1)

        block = ctx.enter_context(nc.Block())

        @block.sync
        def _(sp):
            sp.dma_start(x[:, :, :], xT).then_inc(s_x, 16)
            sp.dma_start(consts[:, :], cst).then_inc(s_x, 16)
            with sp.Fori(0, DEPTH) as l:
                sp.dma_start(pr[:, :], par[l, :, :]).then_inc(s_par, 16)
                sp.dma_start(bw[:, :, :, :], bblk[l, :, :, :, :]).then_inc(s_par, 16)
                sp.dma_start(cw_[:, :, :, :], cblk[l, :, :, :, :]).then_inc(s_par, 16)
                for n in range(N_SLABS):
                    if n >= RAW:
                        sp.wait_ge(s_lo, n - RAW + 1)
                    sp.dma_start(raw[:, n % RAW, 0:width(n)], wslab[l, n, :, 0:width(n)]).then_inc(s_raw[n % RAW], 16)
                layer_end(sp)
            sp.dma_start(outT, x[:, :, :]).then_inc(s_store, 16)
            sp.wait_ge(s_store, 16)

        @block.gpsimd
        def _(pool):
            G = nc.gpsimd

            def lo(n):
                if n >= N_SLABS:
                    return
                w = width(n)
                pool.wait_ge(s_hi, n + 1)
                G.tensor_tensor(wl[:, n % RING, 0:w], raw[:, n % RAW, 0:w], wh[:, n % RING, 0:w].bitcast(F32),
                                ALU.subtract).then_inc(s_lo, 1)

            def s5_back_products(s):
                b = s % 2
                C = ph[:, b, 0:1, :].to_broadcast([P, 2, L])
                S = ph[:, b, 1:2, :].to_broadcast([P, 2, L])
                pool.wait_ge(s_zz, s + 1)
                if s >= 1:
                    pool.wait_ge(s_y, s)
                G.tensor_tensor(stt[:, :, :], zz[:, b, :, :], C, ALU.mult)
                G.tensor_tensor(pq[:, :, :], zz[:, b, :, :], S, ALU.mult)
                pool.drain().then_inc(s_bk, 1)

            def s5_back_sums(s):
                G.tensor_tensor(stt[:, 0, :], stt[:, 0, :], pq[:, 1, :], ALU.subtract)
                G.tensor_tensor(stt[:, 1, :], stt[:, 1, :], pq[:, 0, :], ALU.add)
                pool.drain().then_inc(s_st, 1)

            with pool.Fori(0, DEPTH) as l:
                for n in range(4):
                    lo(n)
                lo(4)
                lo(5)
                for p in range(2 * (N_PROJ - 4)):
                    if p % 2 == 0:
                        lo(6 + p // 2)
                    if p >= 3 and p % 3 == 0:
                        s5_back_products(p // 3 - 1)
                    if p >= 3 and p % 3 == 1:
                        s5_back_sums(p // 3 - 1)
                s5_back_products(ST - 1)
                s5_back_sums(ST - 1)
                for n in range(N_PROJ + 2, N_SLABS):
                    lo(n)
                pool.wait_ge(s_end, ENGINES - 1)
                pool.drain()
                pool.sem_clear(range(nums[0], nums[-1] + 1))
                pool.drain().then_inc(s_go, 1)
                pool.wait_ge(s_ack, ENGINES - 1)
                pool.drain()
                pool.sem_clear(s_go)
                pool.sem_clear(s_ack)

        @block.tensor
        def _(pe):
            T = nc.tensor

            def slab(n, rh, rl, point=lambda i: None, ready=None):
                _, kt, mts = STREAM[n]
                pe.wait_ge(s_lo, n + 1)
                vh = wh[:, n % RING, 0:width(n)].rearrange("p (k c) -> p k c", k=kt)
                vl = wl[:, n % RING, 0:width(n)].rearrange("p (k c) -> p k c", k=kt)
                for m in range(mts):
                    t = tile_of(n) + m
                    c = slice(m * P, (m + 1) * P)
                    if t >= 2:
                        who, count = evacuated(t - 2)
                        pe.wait_ge(s_ev[who], count)
                    for k in range(kt):
                        if ready is not None and m == 0:
                            pe.wait_ge(ready[0], ready[1] + k + 1)
                        T.matmul(pg[:, t % 2, :], vh[:, k, c], rh[k], start=(k == 0), stop=False)
                        T.matmul(pg[:, t % 2, :], vh[:, k, c], rl[k], start=False, stop=False)
                        mm = T.matmul(pg[:, t % 2, :], vl[:, k, c], rh[k], start=False, stop=(k == kt - 1))
                        if mts == 1 and k == kt // 2 - 1:
                            point(0)
                    mm.then_inc(s_mm, 1)
                    if mts == 2:
                        point(m)
                if mts == 1:
                    point(1)

            def tiles(a):
                return [a[:, k, :] for k in range(a.shape[1])]

            X = (tiles(xh), tiles(xl))

            def norm(i):
                pe.wait_ge(s_su[i], DK)
                T.matmul(po[:, :], ones, ssum[:, :], start=True, stop=True).then_inc(s_ss[i], 1)

            def s5_in(s):
                t, j = s // 4, s % 4
                r = slice(CH * j, CH * (j + 1))
                if s == 0:
                    pe.wait_ge(s_par, 48)
                pe.wait_ge(s_ev["act"], t + 1)
                if s >= 1:
                    pe.wait_ge(s_rot, s)
                T.matmul(pb[:, 0, :], bw[r, 0, t, :], proj[r, U0 + t, :], start=True, stop=True)
                T.matmul(pb[:, 1, :], bw[r, 1, t, :], proj[r, U0 + t, :], start=True, stop=True).then_inc(s_bu, 1)

            def s5_out(s):
                t, j = s // 4, s % 4
                r = slice(CH * j, CH * (j + 1))
                if s == 0:
                    pe.wait_ge(s_cc, 1)
                pe.wait_ge(s_st, s + 1)
                if j == 0 and t >= 1:
                    pe.wait_ge(s_yp, t)
                T.matmul(py[r, :], cw_[:, 0, s, :], stt[:, 0, :], start=True, stop=False, tile_position=(0, CH * j))
                T.matmul(py[r, :], cw_[:, 1, s, :], stt[:, 1, :], start=False, stop=True,
                         tile_position=(0, CH * j)).then_inc(s_y, 1)

            ring = [0]

            def ring_bank():
                n = ring[0]
                ring[0] += 1
                if 4 <= n - 2 < 8:
                    pe.wait_ge(s_vc, n - 5)
                elif n >= 2:
                    pe.wait_ge(s_rd2, n - 1 if n < 6 else n - 5)
                return pr2[:, n % 2, :]

            def transposes(bank, first, x):
                for i in range(TT):
                    mm = T.transpose(bank[:, P * i:P * (i + 1)], proj[:, first + (i ^ x), P * i:P * (i + 1)], ident)
                return mm

            def ret_visit(v):
                if v < 4:
                    pe.wait_ge(s_ev["act"], KR + 2)
                    T.matmul(ring_bank(), r_swap, proj[:, (QR, QR + 1, KR, KR + 1)[v], :], start=True, stop=True).then_inc(s_rr2, 1)
                elif v < 8:
                    pe.wait_ge(s_ev["act"], VR + 4)
                    transposes(ring_bank(), VR, v - 4).then_inc(s_rr2, 1)
                g = v - 8
                if 0 <= g < 4 * RH:
                    h, j = g // TT, g % TT
                    r = slice(RQ * (h % 2), RQ * (h % 2) + RQ)
                    pe.wait_ge(s_ro, 4)
                    T.matmul(ring_bank()[:, P * j:L], proj[r, KR + h // 2, P * j:P * (j + 1)], proj[r, QR + h // 2, P * j:L],
                             start=True, stop=True).then_inc(s_rr2, 1)
                if 1 <= g <= 4 * RH:
                    h, j = (g - 1) // TT, (g - 1) % TT
                    pe.wait_ge(s_vc, 4)
                    pe.wait_ge(s_rd, g)
                    if j == 0 and h >= 1:
                        pe.wait_ge(s_oc, h)
                    mm = T.matmul(po[:, P * j:L], proj[:, VR + j, P * h:P * (h + 1)], sd[:, DIAG[j]:DIAG[j + 1]],
                                  start=(j == 0), stop=(j == TT - 1))
                    if j == TT - 1:
                        mm.then_inc(s_o, 1)
                if g >= 6 and (g - 6) % 4 == 0 and (g - 6) // 4 < RH:
                    h = (g - 6) // 4
                    pe.wait_ge(s_oc, h + 1)
                    T.matmul(ring_bank(), ones, osb[:, h % 2, :], start=True, stop=True).then_inc(s_rr2, 1)
                if g >= 8 and (g - 8) % 4 == 0 and (g - 8) // 4 < RH:
                    h = (g - 8) // 4
                    pe.wait_ge(s_q2, h + 1)
                    T.matmul(ring_bank(), ones, rsq[:, 0, :], start=True, stop=True).then_inc(s_rr2, 1)

            def proj_point(p):
                if p % 3 == 0:
                    s5_in(p // 3)
                if p % 3 == 2 and p >= 5:
                    s5_out(p // 3 - 1)
                if p >= RET0:
                    ret_visit(p - RET0)

            def att_point(p):
                if p < 8:
                    pe.wait_ge(s_as, p + 1)
                    if p >= 1:
                        pe.wait_ge(s_ar, p)
                    else:
                        pe.wait_ge(s_rot, ST)
                    T.matmul(pb[:, 0, :], blk64, asq[:, p % 2, :], start=True, stop=True).then_inc(s_am, 1)
                if 2 <= p < 10:
                    i = p - 2
                    pe.wait_ge(s_an, i + 1)
                    if i >= 1:
                        pe.wait_ge(s_ax, i)
                    T.matmul(pb[:, 1, :], a_swap, proj[:, QA + i, :], start=True, stop=True).then_inc(s_ap, 1)
                if 6 <= p < 10:
                    i = p - 6
                    if i == 0:
                        pe.wait_ge(s_rd2, N_RING - 4)
                    if i >= 2:
                        pe.wait_ge(s_va2, i - 1)
                    transposes(pr2[:, i % 2, :], VA, i).then_inc(s_vt, 1)
                v = p - HEAD0
                if 0 <= v < TT * AH:
                    h, q = v // TT, v % TT
                    r = slice(AD * (h % 2), AD * (h % 2) + AD)
                    if v == 0:
                        pe.wait_ge(s_ax, 8)
                    if v >= 2:
                        pe.wait_ge(s_ex, v - 1)
                    T.matmul(pb[:, v % 2, 0:P * (q + 1)], proj[r, QA + h // 2, P * q:P * (q + 1)],
                             proj[r, KA + h // 2, 0:P * (q + 1)], start=True, stop=True).then_inc(s_sc_, 1)
                w = v - 2
                if 0 <= w < TT * AH:
                    q = w % TT
                    pe.wait_ge(s_pn, w + 1)
                    if w >= 2:
                        pe.wait_ge(s_tc, w - 1)
                    else:
                        pe.wait_ge(s_va2, 4)
                    for j in range(q + 1):
                        mm = T.transpose(pr2[:, w % 2, P * j:P * (j + 1)], pp[:, TRI[q] + P * j:TRI[q] + P * (j + 1)], ident)
                    mm.then_inc(s_tp, 1)
                if v >= 7 and (v - 7) % 4 == 0 and (v - 7) // 4 < AH:
                    h = (v - 7) // 4
                    b = AD * (h % 2)
                    pe.wait_ge(s_tc, TT * h + 4)
                    if h % 2 == 0 and h >= 2:
                        pe.wait_ge(s_yal, h // 2)
                    if h == 0:
                        pe.wait_ge(s_yp, 4)
                    for j in range(TT):
                        mm = T.matmul(py[b:b + AD, P * j:L], proj[:, VA + j, AD * h:AD * (h + 1)], pt[:, j, P * j:L],
                                      start=(j == 0), stop=(j == TT - 1), tile_position=(0, b))
                    mm.then_inc(s_pv, 1)

            def branch_slabs(first, n, a, point=lambda i, j: None):
                for i in range(n):
                    slab(first + i, a[0], a[1], lambda j: point(i, j))

            pe.wait_ge(s_x, 32)
            pe.wait_ge(s_s0, DK)
            with pe.Fori(0, DEPTH) as l:
                ring[0] = 0
                T.matmul(po[:, :], ones, ssum[:, :], start=True, stop=True).then_inc(s_ss[0], 1)
                for n in range(4):
                    slab(n, *X, ready=(s_xl[0], 0) if n == 0 else None)
                for n in range(4, N_PROJ):
                    slab(n, *X, point=lambda i: proj_point(2 * (n - 4) + i))
                assert ring[0] == N_RING, ring
                s5_out(ST - 1)
                for i, n in enumerate(P3):
                    kind = STREAM[n][0]
                    if kind == "gate":
                        a = X
                    elif kind == "glu":
                        a = (tiles(gh), tiles(gl))
                    elif n < S_R:
                        a = (tiles(ysh), tiles(ysl))
                    else:
                        a = (tiles(yrh), yrl)
                    if n == S_GLU:
                        pe.wait_ge(s_gl, 4)
                    if n == S_BS:
                        pe.wait_ge(s_yl, 4)
                    if n == S_R:
                        pe.wait_ge(s_yrl, 4)
                    slab(n, *a, point=lambda j: att_point(2 * i + j))
                for n in range(S_A, S_O):
                    if n == S_A + 4:
                        pe.wait_ge(s_yal, 4)
                    slab(n, *(X if STREAM[n][0] == "gate" else (tiles(yah), tiles(yal))))
                for n in range(S_O, S_O + DK):
                    slab(n, *X, ready=(s_ml, 0) if n == S_O else None)
                norm(1)
                for n in range(S_UP0, N_SLABS):
                    if STREAM[n][0] == "up":
                        slab(n, *X, ready=(s_xl[1], 0) if n == S_UP0 else None)
                    else:
                        seg = 0 if n < S_UP2 else 1 if n < S_DN2 else 2
                        if n in (S_DN0, S_DN1, S_DN2):
                            pe.wait_ge(s_hl, sum(SEGS[:seg + 1]))
                        slab(n, [hh[:, seg % 2, k, :] for k in range(8)], [hl[:, seg % 2, k, :] for k in range(8)])
                layer_end(pe)

        @block.scalar
        def _(act):
            A = nc.scalar

            def hi(n):
                if n >= N_SLABS:
                    return
                w = width(n)
                act.wait_ge(s_raw[n % RAW], 16 * (n // RAW + 1))
                if n >= RING:
                    act.wait_ge(s_mm, tile_of(n - RING + 1))
                A.activation(wh[:, n % RING, 0:w], raw[:, n % RAW, 0:w], ACT.Copy).then_inc(s_hi, 1)

            def squares(sem_sq, sem_su):
                for k in range(DK):
                    if k >= 2:
                        act.wait_ge(sem_su, k - 1)
                    A.activation(sq[:, k % 2, :], x[:, k, :], ACT.Square).then_inc(sem_sq, 1)

            def square_step(k, i):
                if k >= 2:
                    act.wait_ge(s_su[i], k - 1)
                A.activation(sq[:, k % 2, :], x[:, k, :], ACT.Square).then_inc(s_sq[i], 1)

            def norm(i):
                act.wait_ge(s_rc[i], 1)
                A.activation(rstd[:, :], rstd[:, :], ACT.Sqrt).then_inc(s_rt[i], 1)
                for k in range(DK):
                    act.wait_ge(s_xn[i], k + 1)
                    A.activation(xh[:, k, :], xn[:, k % 4, :], ACT.Copy).then_inc(s_xh[i], 1)

            def evac(t, dst, func=ACT.Copy):
                act.wait_ge(s_mm, t + 1)
                return A.activation(dst, pg[:, t % 2, :], func).then_inc(s_ev["act"], 1)

            def copy_transposed(bank, first, x):
                for i in range(TT):
                    A.activation(proj[:, first + i, P * (i ^ x):P * ((i ^ x) + 1)], bank[:, P * i:P * (i + 1)], ACT.Copy)

            def ret_visit(v):
                if 5 <= v < 9:
                    n = v - 1
                    act.wait_ge(s_rr2, n + 1)
                    copy_transposed(pr2[:, n % 2, :], VR, n - 4)
                    act.drain().then_inc(s_vc, 1)
                g = v - 8
                for h in range(RH):
                    if g == 4 * h + 5:
                        act.wait_ge(s_o, h + 1)
                        if h >= 2:
                            act.wait_ge(s_yrl, h - 1)
                        A.activation(osb[:, h % 2, :], po[:, :], ACT.Copy).then_inc(s_oc, 1)
                    if g == 4 * h + 7:
                        act.wait_ge(s_ct, h + 1)
                        A.activation(rsq[:, 0, :], osb[:, h % 2, :], ACT.Square).then_inc(s_q2, 1)
                    if g == 4 * h + 8:
                        act.wait_ge(s_r2, h + 1)
                        A.activation(rsq[:, 1, :], rsq[:, 1, :], ACT.Sqrt).then_inc(s_rr, 1)
                    if g == 4 * h + 9:
                        act.wait_ge(s_yr, h + 1)
                        A.activation(yrh[:, h, :], osb[:, h % 2, :], ACT.Copy).then_inc(s_yrh, 1)

            def att_point(p):
                if p < 8:
                    act.wait_ge(s_ar, p + 1)
                    A.activation(asq[:, p % 2, :], asq[:, p % 2, :], ACT.Sqrt).then_inc(s_at, 1)
                if p < 7:
                    i = p + 1
                    if i >= 2:
                        act.wait_ge(s_an, i - 1)
                    A.activation(asq[:, i % 2, :], proj[:, QA + i, :], ACT.Square).then_inc(s_as, 1)
                if 7 <= p < 11:
                    i = p - 7
                    act.wait_ge(s_vt, i + 1)
                    copy_transposed(pr2[:, i % 2, :], VA, i)
                    act.drain().then_inc(s_va2, 1)
                v = p - HEAD0 - 1
                if 0 <= v < TT * AH:
                    h, q = v // TT, v % TT
                    act.wait_ge(s_mx, v + 1)
                    if v >= 4:
                        act.wait_ge(s_tp, v - 3)
                    A.activation(pp[:, TRI[q]:TRI[q + 1]], pb[:, v % 2, 0:P * (q + 1)], ACT.Exp, bias=ast[:, 1, v % 2:v % 2 + 1],
                                 scale=AD ** -0.5, accum_out=ast[:, 2, v % 2:v % 2 + 1]).then_inc(s_ex, 1)
                w = p - HEAD0 - 3
                if 0 <= w < TT * AH:
                    h, q = w // TT, w % TT
                    act.wait_ge(s_tp, w + 1)
                    if h >= 1:
                        act.wait_ge(s_pv, h)
                    A.activation(pt[:, 0:q + 1, P * q:P * (q + 1)],
                                 pr2[:, w % 2, 0:P * (q + 1)].rearrange("p (j c) -> p j c", c=P), ACT.Copy).then_inc(s_tc, 1)
                v = p - HEAD0
                if v >= 12 and (v - 12) % 8 == 0 and (v - 12) // 8 < 4:
                    t = (v - 12) // 8
                    act.wait_ge(s_pv, 2 * t + 2)
                    A.activation(yah[:, t, :], py[:, :], ACT.Copy).then_inc(s_yah, 1)

            act.wait_ge(s_x, 32)
            squares(s_q0, s_s0)
            with act.Fori(0, DEPTH) as l:
                hi(0)
                norm(0)
                hi(1)
                hi(2)
                act.wait_ge(s_par, 48)
                A.activation(sm[:, 0, :], prm("ldt"), ACT.Exp).then_inc(s_dt, 1)
                act.wait_ge(s_th, 1)
                A.activation(sm[:, 2, :], sm[:, 1, :], ACT.Exp).then_inc(s_dt, 1)
                act.wait_ge(s_th, 2)
                A.activation(sm[:, 5, :], sm[:, 4, :], ACT.Sin)
                A.activation(sm[:, 6, :], sm[:, 4, :], ACT.Sin, scale=0.5).then_inc(s_sc, 1)
                for n in range(N_PROJ):
                    hi(n + 3)
                    for i in range(2):
                        p = 2 * (n - 4) + i
                        if p >= RET0:
                            ret_visit(p - RET0)
                    t = n - 1
                    evac(n, proj[:, n, :])
                    if n == GR + 4:
                        for h in range(RH):
                            A.activation(proj[:, GR + h, :], proj[:, GR + h, :], ACT.Silu)
                        act.drain()
                act.drain()
                for t in range(4):
                    act.wait_ge(s_yp, t + 1)
                    A.activation(proj[:, U0 + t, :], proj[:, U0 + t, :], ACT.Gelu_apprx_tanh)
                act.drain()
                act.wait_ge(s_y, ST)
                act.wait_ge(s_yrl, RH)
                A.activation(asq[:, 0, :], proj[:, QA, :], ACT.Square).then_inc(s_as, 1)
                for t in range(4):
                    A.activation(gh[:, t, :], proj[:, U0 + t, :], ACT.Copy).then_inc(s_gh, 1)
                for i, n in enumerate(P3):
                    kind = STREAM[n][0]
                    t = tile_of(n)
                    hi(n + 3)
                    att_point(2 * i)
                    if kind == "glu":
                        m = 2 * (n - S_GLU)
                        for q in range(2):
                            if m + q >= 2:
                                act.wait_ge(s_yl, m + q - 1)
                            evac(t + q, sg[:, (m + q) % 2, :], ACT.Sigmoid)
                    att_point(2 * i + 1)
                    if kind == "glu":
                        for q in range(2):
                            act.wait_ge(s_yf, m + q + 1)
                            A.activation(ysh[:, m + q, :], sg[:, (m + q) % 2, :], ACT.Copy).then_inc(s_yh, 1)
                    if kind == "gate" and n < S_GLU:
                        evac(t, merged[:, n - S_GS, :], ACT.Sigmoid)
                    elif kind == "gate":
                        j, q = (n - S_R) // 6, (n - S_R) % 6
                        if q == 0:
                            act.wait_ge(s_mg, 8 + 4 * j)
                            act.wait_ge(s_mm, tile_of(S_BS))
                        evac(t, gates[:, q, :], ACT.Sigmoid)
                for n in range(S_A, S_O):
                    hi(n + 3)
                    if STREAM[n][0] == "gate":
                        j, q = (n - S_A) // 6, (n - S_A) % 6
                        if q == 0:
                            act.wait_ge(s_mg, 16 + 4 * j)
                        evac(tile_of(n), gates[:, q, :], ACT.Sigmoid)
                act.wait_ge(s_mm, tile_of(S_O - 2))
                for k in range(DK):
                    act.wait_ge(s_mg, 16 + k + 1)
                    A.activation(xh[:, k, :], merged[:, k, :], ACT.Copy).then_inc(s_mh, 1)
                dv = evacuated(tile_of(S_O))[1] - 1
                for k in range(DK):
                    hi(S_O + k + 3)
                    if k >= 1:
                        act.wait_ge(s_ev["dve"], dv + k)
                        square_step(k - 1, 1)
                act.wait_ge(s_ev["dve"], dv + DK)
                square_step(DK - 1, 1)
                norm(1)
                g = 0
                for n in range(S_UP0, N_SLABS):
                    t = tile_of(n)
                    hi(n + 3)
                    if STREAM[n][0] == "up":
                        m, b = (t - tile_of(S_UP0)) % 2, g % 2
                        act.wait_ge(s_mm, t + 1)
                        if g >= 2:
                            act.wait_ge(s_hd, g - 1)
                        f = m * FT + g
                        c0, w0 = PAR["cb"][0] + f, PAR["cw"][0] + 2 * 2 * FT + f
                        A.activation((cg, cu)[m][:, b, :], pg[:, t % 2, :], ACT.Identity, bias=pr[:, c0:c0 + 1],
                                     scale=pr[:, w0:w0 + 1]).then_inc(s_c0, 1)
                        if m == 1:
                            act.wait_ge(s_c1, 2 * g + 1)
                            A.activation(cg[:, b, :], cg[:, b, :], ACT.Silu).then_inc(s_si, 1)
                            act.wait_ge(s_hd, g + 1)
                            seg = 0 if g < SEGS[0] else 1 if g < SEGS[0] + SEGS[1] else 2
                            i = g - sum(SEGS[:seg])
                            if seg == 2 and i == 0:
                                act.wait_ge(s_mm, tile_of(S_UP2))
                            A.activation(hh[:, seg % 2, i, :], ht[:, b, :], ACT.Copy).then_inc(s_hh, 1)
                            g += 1
                dv = evacuated(tile_of(S_DN2))[1] - 1
                for k in range(DK):
                    act.wait_ge(s_ev["dve"], dv + k + 1)
                    square_step(k, 0)
                layer_end(act)

        @block.vector
        def _(dve):
            V = nc.vector

            def sum_squares(sem_sq, sem_su):
                for k in range(DK):
                    sum_step(k, sem_sq, sem_su)

            def sum_step(k, sem_sq, sem_su):
                dve.wait_ge(sem_sq, k + 1)
                if k == 0:
                    V.tensor_copy(ssum[:, :], sq[:, 0, :])
                else:
                    V.tensor_tensor(ssum[:, :], ssum[:, :], sq[:, k % 2, :], ALU.add)
                dve.drain().then_inc(sem_su, 1)

            def norm(i, g):
                dve.wait_ge(s_ss[i], 1)
                V.tensor_scalar(rstd[:, :], po[:, :], 1.0 / D, EPS, ALU.mult, ALU.add)
                dve.drain()
                V.reciprocal(rstd[:, :], rstd[:, :]).then_inc(s_rc[i], 1)
                dve.wait_ge(s_rt[i], 1)
                dve.wait_ge(s_par, 48)
                for k in range(DK + 1):
                    if k < DK:
                        V.scalar_tensor_tensor(xn[:, k % 4, :], x[:, k, :], prm(g)[:, k:k + 1], rstd[:, :], ALU.mult, ALU.mult)\
                         .then_inc(s_xn[i], 1)
                    if k >= 1:
                        dve.wait_ge(s_xh[i], k)
                        V.tensor_tensor(xl[:, k - 1, :], xn[:, (k - 1) % 4, :], xh[:, k - 1, :].bitcast(F32), ALU.subtract)\
                         .then_inc(s_xl[i], 1)
                    if k == 3 or k == 7:
                        dve.drain()

            def tt(out, a, b, op):
                V.tensor_tensor(out, a, b, op)
                return dve.drain()

            def s5_prepare():
                dve.wait_ge(s_dt, 1)
                dve.wait_ge(s_par, 48)
                dt, lre, lim = sm[:, 0, :], prm("lre"), prm("lim")
                tt(sm[:, 1, :], lre, dt, ALU.mult).then_inc(s_th, 1)
                tt(sm[:, 3, :], lim, dt, ALU.mult)
                two_pi = 2 * np.pi
                c1 = float(np.float32(6.28125))
                c2 = float(np.float32(two_pi - c1))
                c2 = float(np.float32(np.floor(c2 * 2 ** 22) / 2 ** 22))
                c3 = float(np.float32(two_pi - c1 - c2))
                big = float(1.5 * 2 ** 23)
                V.tensor_scalar(sm[:, 7, :], sm[:, 3, :], float(np.float32(1 / two_pi)), big, ALU.mult, ALU.add)
                dve.drain()
                V.tensor_scalar(sm[:, 7, :], sm[:, 7, :], -big, None, ALU.add)
                dve.drain()
                for c in (c1, c2, c3):
                    V.scalar_tensor_tensor(sm[:, 3, :], sm[:, 7, :], -c, sm[:, 3, :], ALU.mult, ALU.add)
                    dve.drain()
                V.tensor_scalar(sm[:, 4, :], sm[:, 3, :], float(np.float32(3.1415925)), float(np.float32(-3.1415925)), ALU.min, ALU.max)
                dve.drain().then_inc(s_th, 1)
                dve.wait_ge(s_sc, 1)
                dve.wait_ge(s_dt, 2)
                sin, sh, r = sm[:, 5, :], sm[:, 6, :], sm[:, 2, :]
                cos = sm[:, 8, :]
                tt(cos, sh, sh, ALU.mult)
                V.tensor_scalar(cos, cos, -2.0, 1.0, ALU.mult, ALU.add)
                dve.drain()
                nre, nim, den, fr, fi, t1, t2 = [sm[:, 9 + i, :] for i in range(7)]
                tt(nre, cos, r, ALU.mult)
                V.tensor_scalar(nre, nre, -1.0, None, ALU.add)
                tt(nim, sin, r, ALU.mult)
                tt(t1, lre, lre, ALU.mult)
                tt(t2, lim, lim, ALU.mult)
                tt(den, t1, t2, ALU.add)
                V.reciprocal(den, den)
                tt(t1, nre, lre, ALU.mult)
                tt(t2, nim, lim, ALU.mult)
                tt(fr, t1, t2, ALU.add)
                tt(fr, fr, den, ALU.mult)
                tt(t1, nim, lre, ALU.mult)
                tt(t2, nre, lim, ALU.mult)
                tt(fi, t1, t2, ALU.subtract)
                tt(fi, fi, den, ALU.mult)
                frb = fr.unsqueeze(2).to_broadcast([P, ST, CH])
                fib = fi.unsqueeze(2).to_broadcast([P, ST, CH])
                q1, q2 = p2[:, 0, :].rearrange("p (s c) -> p s c", s=ST), p2[:, 1, :].rearrange("p (s c) -> p s c", s=ST)
                tt(q1, cw_[:, 0, :, :], fib, ALU.mult)
                tt(q2, cw_[:, 1, :, :], fib, ALU.mult)
                tt(cw_[:, 0, :, :], cw_[:, 0, :, :], frb, ALU.mult)
                tt(cw_[:, 1, :, :], cw_[:, 1, :, :], frb, ALU.mult)
                tt(cw_[:, 0, :, :], cw_[:, 0, :, :], q2, ALU.subtract)
                tt(cw_[:, 1, :, :], cw_[:, 1, :, :], q1, ALU.add)
                V.tensor_scalar(cw_[:, 1, :, :], cw_[:, 1, :, :], -1.0, None, ALU.mult)
                dve.drain().then_inc(s_cc, 1)
                V.tensor_copy(pw[:, 0, 0, :], cos)
                V.tensor_copy(pw[:, 1, 0, :], sin)
                dve.drain()
                for n in range(1, LEVELS):
                    c, s = pw[:, 0, n - 1, :], pw[:, 1, n - 1, :]
                    tt(t1, c, c, ALU.mult)
                    tt(t2, s, s, ALU.mult)
                    tt(pw[:, 0, n, :], t1, t2, ALU.subtract)
                    V.scalar_tensor_tensor(pw[:, 1, n, :], c, 2.0, s, ALU.mult, ALU.mult)
                    dve.drain()
                V.memset(ph0[:, :, 0, 0:1], 1.0)
                V.memset(ph0[:, :, 1, 0:1], 0.0)
                dve.drain()
                n = 1
                lv = 0
                while n < BASE:
                    c = pw[:, 0, lv, :].unsqueeze(2).to_broadcast([P, ST, n])
                    s = pw[:, 1, lv, :].unsqueeze(2).to_broadcast([P, ST, n])
                    q1 = p2[:, 0, 0:ST * n].rearrange("p (s c) -> p s c", s=ST)
                    q2 = p2[:, 1, 0:ST * n].rearrange("p (s c) -> p s c", s=ST)
                    C, S = ph0[:, :, 0, 0:n], ph0[:, :, 1, 0:n]
                    C2, S2 = ph0[:, :, 0, n:2 * n], ph0[:, :, 1, n:2 * n]
                    tt(q1, C, c, ALU.mult)
                    tt(q2, S, s, ALU.mult)
                    tt(C2, q1, q2, ALU.subtract)
                    tt(q1, C, s, ALU.mult)
                    tt(q2, S, c, ALU.mult)
                    tt(S2, q1, q2, ALU.add)
                    n *= 2
                    lv += 1

            def s5_phases(s):
                b = s % 2
                if s >= 2:
                    dve.wait_ge(s_bk, s - 1)
                V.tensor_copy(ph[:, b, :, 0:BASE], ph0[:, s, :, :])
                dve.drain()
                n, lv = BASE, 5
                while n < L:
                    c, sn = pw[:, 0, lv, s:s + 1], pw[:, 1, lv, s:s + 1]
                    V.tensor_scalar(p2[:, :, 0:n], ph[:, b, :, 0:n], sn, None, ALU.mult)
                    dve.drain()
                    V.scalar_tensor_tensor(ph[:, b, 0, n:2 * n], ph[:, b, 0, 0:n], c, p2[:, 1, 0:n], ALU.mult, ALU.subtract)
                    V.scalar_tensor_tensor(ph[:, b, 1, n:2 * n], ph[:, b, 1, 0:n], c, p2[:, 0, 0:n], ALU.mult, ALU.add)
                    dve.drain()
                    n *= 2
                    lv += 1

            def s5_rotate(s):
                b = s % 2
                C = ph[:, b, 0:1, :].to_broadcast([P, 2, L])
                S = ph[:, b, 1:2, :].to_broadcast([P, 2, L])
                dve.wait_ge(s_bu, s + 1)
                if s >= 2:
                    dve.wait_ge(s_bk, s - 1)
                V.tensor_tensor(zz[:, b, :, :], pb[:, :, :], C, ALU.mult)
                V.tensor_tensor(p2[:, :, :], pb[:, :, :], S, ALU.mult)
                dve.drain().then_inc(s_rot, 1)
                V.tensor_tensor(zz[:, b, 0, :], zz[:, b, 0, :], p2[:, 1, :], ALU.add)
                V.tensor_tensor(zz[:, b, 1, :], zz[:, b, 1, :], p2[:, 0, :], ALU.subtract)
                dve.drain()

            def s5_scan(s):
                b = s % 2
                r = sm[:, 2, s:s + 1].to_broadcast([P, L])
                V.tensor_tensor_scan(zz[:, b, 0, :], r, zz[:, b, 0, :], 0.0, ALU.mult, ALU.add)
                V.tensor_tensor_scan(zz[:, b, 1, :], r, zz[:, b, 1, :], 0.0, ALU.mult, ALU.add)
                dve.drain().then_inc(s_zz, 1)

            def s5_channels(t):
                dve.wait_ge(s_y, 4 * t + 4)
                V.scalar_tensor_tensor(proj[:, U0 + t, :], proj[:, U0 + t, :], prm("d")[:, t:t + 1], py[:, :], ALU.mult, ALU.add)\
                 .then_inc(s_yp, 1)

            ring = [0]

            def ring_wait():
                n = ring[0]
                ring[0] += 1
                dve.wait_ge(s_rr2, n + 1)
                return pr2[:, n % 2, :]

            def ret_visit(v):
                if v < 4:
                    tl, sc = (QR, QR + 1, KR, KR + 1)[v], (1.0, 1.0, RQ ** -0.5, RQ ** -0.5)[v]
                    bank = ring_wait()
                    V.scalar_tensor_tensor(rsq[:, 0, :], bank, sc, r_sin, ALU.mult, ALU.mult)
                    dve.drain().then_inc(s_rd2, 1)
                    V.scalar_tensor_tensor(proj[:, tl, :], proj[:, tl, :], sc, r_cos, ALU.mult, ALU.mult)
                    dve.drain()
                    V.tensor_tensor(proj[:, tl, :], proj[:, tl, :], rsq[:, 0, :], ALU.add).then_inc(s_ro, 1)
                    dve.drain()
                if v == 8:
                    ring[0] += 4
                g = v - 8
                if 0 <= g < TT * RH:
                    h, j = g // TT, g % TT
                    bank = ring_wait()
                    if h >= 1:
                        dve.wait_ge(s_o, h)
                    V.tensor_tensor(sd[:, DIAG[j]:DIAG[j + 1]], bank[:, P * j:L], decay[:, h, 0:L - P * j], ALU.mult)
                    dve.drain().then_inc(s_rd2, 1)
                    dve.drain().then_inc(s_rd, 1)
                for h in range(RH):
                    o = osb[:, h % 2, :]
                    if g == 4 * h + 6:
                        V.scalar_tensor_tensor(o, ring_wait(), -1.0 / P, o, ALU.mult, ALU.add)
                        dve.drain().then_inc(s_rd2, 1)
                        dve.drain().then_inc(s_ct, 1)
                    if g == 4 * h + 8:
                        V.tensor_scalar(rsq[:, 1, :], ring_wait(), 1.0 / P, EPS, ALU.mult, ALU.add)
                        dve.drain().then_inc(s_rd2, 1)
                        V.reciprocal(rsq[:, 1, :], rsq[:, 1, :]).then_inc(s_r2, 1)
                    if g == 4 * h + 9:
                        dve.wait_ge(s_rr, h + 1)
                        V.scalar_tensor_tensor(o, o, prm("gn")[:, h:h + 1], rsq[:, 1, :], ALU.mult, ALU.mult)
                        dve.drain()
                        V.tensor_tensor(o, o, proj[:, GR + h, :], ALU.mult).then_inc(s_yr, 1)
                    if g == 4 * h + 10:
                        dve.wait_ge(s_yrh, h + 1)
                        V.tensor_tensor(yrl[h], o, yrh[:, h, :].bitcast(F32), ALU.subtract).then_inc(s_yrl, 1)

            def att_point(p):
                if p < 8:
                    a = asq[:, p % 2, :]
                    dve.wait_ge(s_am, p + 1)
                    V.tensor_scalar(a, pb[:, 0, :], EPS, None, ALU.add)
                    dve.drain()
                    V.reciprocal(a, a).then_inc(s_ar, 1)
                if 2 <= p < 10:
                    i = p - 2
                    dve.wait_ge(s_ap, i + 1)
                    V.tensor_tensor(atmp[:, :], pb[:, 1, :], a_sin, ALU.mult)
                    V.tensor_tensor(proj[:, QA + i, :], proj[:, QA + i, :], a_cos, ALU.mult)
                    dve.drain()
                    V.tensor_tensor(proj[:, QA + i, :], proj[:, QA + i, :], atmp[:, :], ALU.add)
                    dve.drain().then_inc(s_ax, 1)
                if p < 8:
                    dve.wait_ge(s_at, p + 1)
                    g = prm("qn") if p < 4 else prm("kn")
                    V.scalar_tensor_tensor(proj[:, QA + p, :], proj[:, QA + p, :], g, asq[:, p % 2, :], ALU.mult, ALU.mult)
                    dve.drain().then_inc(s_an, 1)
                v = p - HEAD0
                if 0 <= v < TT * AH:
                    q, b = v % TT, v % 2
                    dve.wait_ge(s_sc_, v + 1)
                    diag = pb[:, b, P * q:P * (q + 1)]
                    V.tensor_tensor(diag, diag, mask, ALU.add)
                    dve.drain()
                    V.reduce_max(ast[:, 0, b:b + 1], pb[:, b, 0:P * (q + 1)], AX_X)
                    dve.drain()
                    if v >= 2:
                        dve.wait_ge(s_ex, v - 1)
                    V.tensor_scalar(ast[:, 1, b:b + 1], ast[:, 0, b:b + 1], -(AD ** -0.5), None, ALU.mult).then_inc(s_mx, 1)
                w = v - 1
                if 0 <= w < TT * AH:
                    q, b = w % TT, w % 2
                    dve.wait_ge(s_ex, w + 1)
                    V.reciprocal(ast[:, 3, b:b + 1], ast[:, 2, b:b + 1])
                    dve.drain()
                    V.tensor_scalar(pp[:, TRI[q]:TRI[q + 1]], pp[:, TRI[q]:TRI[q + 1]], ast[:, 3, b:b + 1], None, ALU.mult)\
                     .then_inc(s_pn, 1)
                if v >= 13 and (v - 13) % 8 == 0 and (v - 13) // 8 < 4:
                    t = (v - 13) // 8
                    dve.wait_ge(s_yah, t + 1)
                    V.tensor_tensor(yal[:, t, :], py[:, :], yah[:, t, :].bitcast(F32), ALU.subtract).then_inc(s_yal, 1)

            def merge(t, k, gate=None):
                dve.wait_ge(s_mm, t + 1)
                o = merged[:, k, :]
                if gate is None:
                    V.tensor_tensor(o, o, pg[:, t % 2, :], ALU.mult)
                    dve.drain().then_inc(s_ev["dve"], 1)
                else:
                    m = mt[:, k % 2, :]
                    V.tensor_tensor(m, pg[:, t % 2, :], gate, ALU.mult)
                    dve.drain().then_inc(s_ev["dve"], 1)
                    V.tensor_tensor(o, o, m, ALU.add)
                dve.drain().then_inc(s_mg, 1)

            def residual(t, k):
                dve.wait_ge(s_mm, t + 1)
                V.tensor_tensor(x[:, k, :], x[:, k, :], pg[:, t % 2, :], ALU.add)
                dve.drain().then_inc(s_ev["dve"], 1)

            dve.wait_ge(s_x, 32)
            sum_squares(s_q0, s_s0)
            with dve.Fori(0, DEPTH) as l:
                ring[0] = 0
                norm(0, "g1")
                dve.drain()
                s5_prepare()
                s5_phases(0)
                for p in range(2 * (N_PROJ - 4)):
                    s = p // 3
                    if p % 3 == 0:
                        s5_rotate(s)
                    if p % 3 == 1:
                        s5_scan(s)
                    if p % 3 == 2 and s + 1 < ST:
                        s5_phases(s + 1)
                    if p >= RET0:
                        ret_visit(p - RET0)
                    if p % 3 == 2 and s >= 1 and (s - 1) % 4 == 3:
                        s5_channels((s - 1) // 4)
                assert ring[0] == N_RING, ring
                s5_channels(3)
                for i, n in enumerate(P3):
                    kind = STREAM[n][0]
                    t = tile_of(n)
                    if n == S_GS:
                        att_point(0)
                        for k in range(4):
                            dve.wait_ge(s_gh, k + 1)
                            V.tensor_tensor(gl[:, k, :], proj[:, U0 + k, :], gh[:, k, :].bitcast(F32), ALU.subtract).then_inc(s_gl, 1)
                    else:
                        att_point(2 * i)
                    if kind == "branch":
                        k = 2 * (n - S_BS) if n < S_R else 4 * ((n - S_R) // 6) + 2 * ((n - S_R) % 6 - 4)
                        dve.wait_ge(s_ev["act"], OWNER[:t].count("act"))
                        merge(t, k, None if n < S_R else gates[:, k % 4, :])
                    att_point(2 * i + 1)
                    if kind == "branch":
                        merge(t + 1, k + 1, None if n < S_R else gates[:, k % 4 + 1, :])
                    if kind == "glu":
                        for q in range(2):
                            m = 2 * (n - S_GLU) + q
                            dve.wait_ge(s_ev["act"], evacuated(t + q)[1])
                            V.tensor_tensor(sg[:, m % 2, :], sg[:, m % 2, :], proj[:, U0 + m, :], ALU.mult).then_inc(s_yf, 1)
                        for q in range(2):
                            m = 2 * (n - S_GLU) + q
                            dve.wait_ge(s_yh, m + 1)
                            V.tensor_tensor(ysl[:, m, :], sg[:, m % 2, :], ysh[:, m, :].bitcast(F32), ALU.subtract).then_inc(s_yl, 1)
                for n in range(S_A, S_O):
                    if STREAM[n][0] == "branch":
                        t = tile_of(n)
                        k = 4 * ((n - S_A) // 6) + 2 * ((n - S_A) % 6 - 4)
                        dve.wait_ge(s_ev["act"], OWNER[:t].count("act"))
                        for m in range(2):
                            merge(t + m, k + m, gates[:, k % 4 + m, :])
                for k in range(DK):
                    dve.wait_ge(s_mh, k + 1)
                    V.tensor_tensor(xl[:, k, :], merged[:, k, :], xh[:, k, :].bitcast(F32), ALU.subtract).then_inc(s_ml, 1)
                for k in range(DK):
                    residual(tile_of(S_O) + k, k)
                    if k >= 1:
                        sum_step(k - 1, s_sq[1], s_su[1])
                sum_step(DK - 1, s_sq[1], s_su[1])
                norm(1, "g2")
                dve.drain()
                g = 0
                for n in range(S_UP0, N_SLABS):
                    t = tile_of(n)
                    if STREAM[n][0] == "up":
                        m, b = (t - tile_of(S_UP0)) % 2, g % 2
                        dve.wait_ge(s_c0, 2 * g + m + 1)
                        dst = (cg, cu)[m][:, b, :]
                        f = m * FT + g
                        for tap, sh in ((1, 1), (0, 2)):
                            w0 = PAR["cw"][0] + tap * 2 * FT + f
                            V.scalar_tensor_tensor(dst[:, sh:L], pg[:, t % 2, 0:L - sh], pr[:, w0:w0 + 1], dst[:, sh:L],
                                                   ALU.mult, ALU.add)
                            dr = dve.drain()
                        dr.then_inc(s_ev["dve"], 1)
                        dve.drain().then_inc(s_c1, 1)
                        if m == 1:
                            dve.wait_ge(s_si, g + 1)
                            if g >= 2:
                                dve.wait_ge(s_hh, g - 1)
                            V.tensor_tensor(ht[:, b, :], cg[:, b, :], cu[:, b, :], ALU.mult).then_inc(s_hd, 1)
                            dve.wait_ge(s_hh, g + 1)
                            seg = 0 if g < SEGS[0] else 1 if g < SEGS[0] + SEGS[1] else 2
                            i = g - sum(SEGS[:seg])
                            V.tensor_tensor(hl[:, seg % 2, i, :], ht[:, b, :], hh[:, seg % 2, i, :].bitcast(F32),
                                            ALU.subtract).then_inc(s_hl, 1)
                            dve.drain()
                            g += 1
                    else:
                        residual(t, (n - S_DN0) % DK if n < S_UP2 else (n - S_DN1) % DK)
                        if n > S_DN2:
                            sum_step(n - S_DN2 - 1, s_sq[0], s_su[0])
                sum_step(DK - 1, s_sq[0], s_su[0])
                layer_end(dve)


def constants():
    f = np.float32
    p = np.arange(P)
    t = np.arange(L)
    lg = np.log1p(-np.exp2(f(-5.0) - np.arange(RH, dtype=f))).astype(f)
    rel = (t[None, :] - p[:, None]).astype(f)
    decay = np.where(rel[None] >= 0, np.exp(lg[:, None, None] * np.maximum(rel, 0)[None]), 0).astype(f)
    decay = decay.transpose(1, 0, 2).reshape(P, RH * L)
    half = RQ // 2
    inv = (f(1.0) / (f(10000.0) ** np.linspace(0.0, 1.0, half, dtype=f))).astype(f)
    ang = inv[p % half][:, None] * t[None, :].astype(f)
    r_cos, r_sin = np.cos(ang).astype(f), np.sin(ang).astype(f)
    rh = AD // 4 // 2
    inva = (f(500000.0) ** (-np.arange(rh, dtype=f) / f(rh))).astype(f)
    d = p % AD
    turned = (d < 2 * rh)[:, None]
    anga = inva[d % rh][:, None] * t[None, :].astype(f)
    a_cos = np.where(turned, np.cos(anga), 1).astype(f)
    a_sin = np.where(turned, np.sin(anga), 0).astype(f)
    ident = np.eye(P, dtype=f)

    def swap(h, block):
        m = np.zeros((P, P), f)
        for o in range(P):
            q = o % block
            if q < h:
                m[o + h, o] = -1.0
            elif q < 2 * h:
                m[o - h, o] = 1.0
        return m

    blk = np.where(p[:, None] // AD == p[None, :] // AD, 1.0 / AD, 0.0).astype(f)
    mask = np.where(p[None, :] <= p[:, None], 0.0, MASKED).astype(f)
    return np.ascontiguousarray(np.concatenate(
        [decay, r_cos, r_sin, a_cos, a_sin, ident, swap(half, RQ), swap(rh, AD), np.ones((P, P), f), blk,
         mask], axis=1).astype(f))


def kernel(x, norm1_g, w_in, ssm_lambda_re, ssm_lambda_im, ssm_log_dt, ssm_b_re, ssm_b_im, ssm_c_re, ssm_c_im, ssm_d,
           ssm_w_glu, ret_gn_g, attn_qn_g, attn_kn_g, w_br_ssm, w_br_ret, w_br_att, w_o, norm2_g, ffn_w_up, ffn_conv_w,
           ffn_conv_b, ffn_w_down):
    import numpy as _np
    import concourse.bacc as _bacc
    from concourse import mybir as _mybir
    from concourse.bass_utils import run_bass_kernel_spmd as _run

    A = _np.asarray

    def slabs(w, cols):
        w = A(w)
        n, k, c = w.shape
        return w.reshape(n, k // P, P, c // cols, cols).transpose(0, 3, 2, 1, 4).reshape(n, c // cols, P, -1)

    w_in = A(w_in)
    g0 = P * N_PROJ
    main = slabs(w_in[:, :, :g0], P)
    gate = [slabs(w_in[:, :, g0 + D * i:g0 + D * (i + 1)], P) for i in range(3)]
    br = [slabs(w, 2 * P) for w in (w_br_ssm, w_br_ret, w_br_att)]
    up = A(ffn_w_up).reshape(DEPTH, D, 2, FT, P).transpose(0, 1, 3, 2, 4).reshape(DEPTH, D, 2 * FH)
    up = slabs(up, P)
    u1, u2 = 2 * SEGS[0], 2 * (SEGS[0] + SEGS[1])
    down, at = [], 0
    for n in SEGS:
        w = slabs(A(ffn_w_down)[:, at * P:(at + n) * P], P)
        down.append(_np.concatenate([w, _np.zeros(w.shape[:3] + (SLAB - w.shape[3],), w.dtype)], axis=3))
        at += n
    parts = [main, gate[0], slabs(ssm_w_glu, 2 * P), br[0]]
    for i in (1, 2):
        parts += [gate[i][:, 0:4], br[i][:, 0:2], gate[i][:, 4:8], br[i][:, 2:4]]
    parts += [slabs(w_o, P), up[:, :u2], down[0], up[:, u2:], down[1], down[2]]
    wslab = _np.ascontiguousarray(_np.concatenate(parts, axis=1))
    assert wslab.shape[1] == N_SLABS

    def cols(a, n):
        return A(a).reshape(DEPTH, n, P).transpose(0, 2, 1)

    ldt = _np.repeat(A(ssm_log_dt)[:, :, None], SSM_P, axis=2)
    cw = A(ffn_conv_w).reshape(DEPTH, 3, 2 * FT, P).transpose(0, 3, 1, 2).reshape(DEPTH, P, -1)
    par = _np.ascontiguousarray(_np.concatenate(
        [cols(norm1_g, DK), cols(norm2_g, DK), cols(ret_gn_g, RH),
         _np.concatenate([A(attn_qn_g)] * 2, axis=1)[:, :, None], _np.concatenate([A(attn_kn_g)] * 2, axis=1)[:, :, None],
         cols(ssm_d, 4), cols(ssm_lambda_re, ST), cols(ssm_lambda_im, ST), cols(ldt, ST), cw, cols(ffn_conv_b, 2 * FT),
         _np.zeros((DEPTH, P, N_PAR - _at), _np.float32)], axis=2))
    bblk = _np.zeros((DEPTH, P, 2, 4, P), _np.float32)
    cblk = _np.zeros((DEPTH, P, 2, ST, CH), _np.float32)
    for i, (b, c) in enumerate(((ssm_b_re, ssm_c_re), (ssm_b_im, ssm_c_im))):
        b, c = A(b), A(c)
        for s in range(ST):
            for g in range(2):
                st, ch = slice(SSM_P * g, SSM_P * (g + 1)), slice(SSM_H * g, SSM_H * (g + 1))
                row = CH * (s % 4) + SSM_H * g
                bblk[:, row:row + SSM_H, i, s // 4, st] = b[:, 2 * s + g].transpose(0, 2, 1)
                cblk[:, st, i, s, ch] = c[:, 2 * s + g].transpose(0, 2, 1)
    xT = _np.ascontiguousarray(A(x)[0].T.reshape(DK, P, L).transpose(1, 0, 2))
    arrays = {"xT": xT, "wslab": wslab, "par": par, "bblk": bblk, "cblk": cblk, "cst": constants()}

    nc = _bacc.Bacc("TRN2", target_bir_lowering=False, num_devices=1, dynamic_dma_scratch_size=4096)
    args = [nc.dram_tensor(f"in_{n}", a.shape, _mybir.dt.from_np(a.dtype), kind="ExternalInput").ap() for n, a in arrays.items()]
    args.append(nc.dram_tensor("out_T", (P, DK, L), _mybir.dt.float32, kind="ExternalOutput").ap())
    hybrid_trunk(nc, *args)
    r = _run(nc, [{f"in_{n}": a for n, a in arrays.items()}], core_ids=[0])
    o = r.results[0]["out_T"]
    return _np.ascontiguousarray(o.transpose(1, 0, 2).reshape(D, L).T)[None]
```

```python
from contextlib import ExitStack

import numpy as np

import concourse.bass as bass
from concourse import mybir

F32 = mybir.dt.float32
F32R = mybir.dt.float32r
ALU = mybir.AluOpType
ACT = mybir.ActivationFunctionType
AX_X = mybir.AxisListType.X

P = 128
EPS = 1e-6
MASKED = -1e30

DEPTH = 2
D = 1024
L = 512
DK = D // P
SSM_W = 512
SSM_H = 16
SSM_P = 64
ST = SSM_W // SSM_H * SSM_P // P
CH = 2 * SSM_H
RH = 4
RQ = 64
AH = 8
AD = 64
FH = 2816
FT = FH // P
TT = L // P

SLAB = 1024
RAW = 2
RING = 4
N_PROJ = 28
SEGS = (8, 8, FT - 16)
STREAM = []


def _stream(kind, n, kt, mt):
    first = len(STREAM)
    STREAM.extend([(kind, kt, mt)] * n)
    return first


S_PROJ = _stream("proj", N_PROJ, DK, 1)
S_GS = _stream("gate", DK, DK, 1)
S_GLU = _stream("glu", 4, 4, 1)
S_GR = _stream("gate", 4, DK, 1)
S_BS = _stream("branch", 4, 4, 2)
S_BR = _stream("branch", 2, 4, 2)
S_GR2 = _stream("gate", 4, DK, 1)
S_BR2 = _stream("branch", 2, 4, 2)
S_A = len(STREAM)
for _i in range(2):
    _stream("gate", 4, DK, 1)
    _stream("branch", 2, 4, 2)
S_O = _stream("residual", DK, DK, 1)
S_UP0 = _stream("up", 2 * SEGS[0], DK, 1)
S_UP1 = _stream("up", 2 * SEGS[1], DK, 1)
S_DN0 = _stream("residual", DK, SEGS[0], 1)
S_UP2 = _stream("up", 2 * SEGS[2], DK, 1)
S_DN1 = _stream("residual", DK, SEGS[1], 1)
S_DN2 = _stream("residual", DK, SEGS[2], 1)
N_SLABS = len(STREAM)
HEAD = 2
AHEAD = RING - 1
assert N_SLABS % RING == 0 and N_SLABS % RAW == 0
P3 = list(range(S_GS, S_A))


def width(n):
    n %= N_SLABS
    return STREAM[n][1] * STREAM[n][2] * P


def tile_of(n):
    return sum(mt for _, _, mt in STREAM[:n])


OWNER = ["act" if kind in ("proj", "gate", "glu") else "dve" for kind, _, mt in STREAM for _ in range(mt)]


def evacuated(t):
    return OWNER[t], OWNER[:t + 1].count(OWNER[t])


T_O = tile_of(S_O)


def tile_before(t):
    if t >= T_O + 4:
        return t - 4
    if t >= T_O + 2:
        return None
    return t - 2 if t >= 2 else None


def _columns(widths):
    at, where = 0, {}
    for name, w in widths:
        where[name] = (at, at + w)
        at += w
    return where, at


PAR, N_PAR = _columns([("g2", DK), ("gn", RH), ("qn", 1), ("kn", 1), ("d", 4), ("cw", 3 * 2 * FT), ("cb", 2 * FT)])
EARLY, N_EARLY = _columns([("g1", DK), ("lre", ST), ("lim", ST), ("ldt", ST)])

U0, QR, KR, VR, GR, QA, KA, VA = 0, 4, 6, 8, 12, 16, 20, 24

CHUNK = 256
LEVELS = 9
BASE = 32
PHASE_LEVELS = (5, 6, 7)
assert BASE == 2 ** PHASE_LEVELS[0] and CHUNK == 2 ** (PHASE_LEVELS[-1] + 1) and L == 2 * CHUNK
DIAG = [sum(L - P * i for i in range(j)) for j in range(TT + 1)]
TRI = [P * i * (i + 1) // 2 for i in range(TT + 1)]

N_POINTS = 2 * (N_PROJ - 2)
RET0 = 16
MSQ0 = 2 * (QA - 1)
HEAD0 = 9


STACK_AT = [4, 5, 6, 7, 10, 11, 12, 13, 16, 17, 18, 21, 22, 23, 24, 25]
BLOCKS_AT = [8, 14, 19, 26]
assert all(2 + (3 * s + 1) // 2 <= STACK_AT[s] and 2 + 3 * s // 2 < BLOCKS_AT[s // 4] for s in range(ST))


def point_steps(p):
    steps = []
    v = p - RET0
    g = v - 8
    if 0 <= v < 4:
        steps.append(("swap_r", v, "dve"))
    elif 4 <= v < 8:
        steps.append(("turn_vr", v - 4, "act"))
    if 0 <= g < TT * RH:
        steps.append(("score_r", g, "dve"))
    for h in range(RH):
        if g == 4 * h + 6:
            steps.append(("var", h, "dve"))
        if g == 4 * h + 8:
            steps.append(("rstd_r", h, "dve"))
    m = p - MSQ0 - 1
    if m >= 0 and m % 2 == 0 and m < 16:
        steps.append(("msq", m // 2, "dve"))
    a = p - N_POINTS
    if 0 <= a < 8:
        steps.append(("swap_a", a, "dve"))
    if 4 <= a < 8:
        steps.append(("turn_va", a - 4, "act"))
    w = a - HEAD0 - 2
    if 0 <= w < TT * AH:
        steps.append(("turn_p", w, "act"))
    return steps


RING_FILLS = [s for p in range(N_POINTS + 2 * len(P3)) for s in point_steps(p)]
FILL = {(step, i): n for n, (step, i, _) in enumerate(RING_FILLS)}


def reads_until(n):
    who = RING_FILLS[n][2]
    return who, sum(1 for s in RING_FILLS[:n + 1] if s[2] == who)


def hybrid_trunk(nc, xT, wslab, par, early, bblk, cblk, cst, outT):
    ctx = ExitStack()
    with ctx:
        def sb(name, shape, dt=F32):
            return ctx.enter_context(nc.sbuf_tensor(name, shape, dt))

        sems = []

        def sem(name):
            s = ctx.enter_context(nc.semaphore(name))
            sems.append(s)
            return s

        x = sb("x_res", [P, DK, L])
        xh = sb("xn_hi", [P, DK, L], F32R)
        xl = sb("xn_lo", [P, DK, L], F32R)
        raw = sb("w_raw", [P, RAW, SLAB])
        wh = sb("w_hi", [P, RING, SLAB], F32R)
        wl = sb("w_lo", [P, RING, SLAB], F32R)
        consts = sb("consts", [P, cst.shape[1]])
        pr = sb("params", [P, N_PAR])
        er = sb("early_params", [P, N_EARLY])
        off = 0

        def const(width):
            nonlocal off
            off += width
            return consts[:, off - width:off]

        ident, r_swap, a_swap, ones, centre, blk64, mask = [const(P) for _ in range(7)]
        small = off
        decay = const(RH * L).rearrange("p (h t) -> p h t", h=RH)
        r_cos, r_sin, a_cos, a_sin = const(L), const(L), const(L), const(L)

        def prm(name):
            if name in EARLY:
                return er[:, EARLY[name][0]:EARLY[name][1]]
            return pr[:, PAR[name][0]:PAR[name][1]]

        base = nc.sbuf_base
        KB = 1024
        arena = sb("arena", [P, int((2 * N_PROJ + 55) * KB) // 4])

        def at(name, kb, shape, dt=F32):
            return nc.alloc_sbuf_tensor_at(name, shape, dt, offset=base + int(kb * KB))

        W0 = 2 * N_PROJ
        proj = at("proj", 0, [P, N_PROJ, L])
        ssum = at("sq_sum", W0 + 53, [P, L])
        sq = at("sq", W0 + 49, [P, 2, L])
        nst = at("norm_stat", W0 + 45, [P, 3, TT])
        xn = at("xn", W0, [P, 4, L])
        ph = at("phase", W0, [P, 2, 2, CHUNK])
        zz = at("scan", W0 + 8, [P, 2, 2, L])
        p2 = at("prod", W0 + 16, [P, 2, L])
        pq = at("prod_back", W0 + 20, [P, 2, L])
        stt = at("states", W0 + 24, [P, 2, L])
        stack = [at(f"u_stack{s}", 2 * STACK_AT[s], [P, L], F32R) for s in range(ST)]
        braw = [at(f"b_raw{t}", 2 * BLOCKS_AT[t], [P, SLAB]) for t in range(4)]
        bsplit = [at(f"b_split{t}", 2 * BLOCKS_AT[t], [P, 4, 2, P], F32R) for t in range(4)]
        btmp = at("b_hi", W0 + 42.5, [P, SLAB], F32R)
        uhi = at("u_hi", W0 + 4, [P, L], F32R)
        ulo = at("u_lo", W0 + 6, [P, L], F32R)
        pscr = at("phase_prod", W0 + 30, [P, 2, CHUNK // 2])
        cneg = at("c_blocks_neg", W0 + 28, [P, ST, CH])
        cw_ = at("c_blocks", W0 + 32, [P, 2, ST, CH])
        ph0 = at("phase_base", W0 + 36, [P, ST, 2, BASE])
        pw = at("powers", W0 + 40, [P, 2, LEVELS, ST])
        sm = at("s5_small", W0 + 41.25, [P, 20, ST])
        sd = at("ret_scores", W0 + 42.5, [P, DIAG[TT]])
        osb = at("ret_out", W0 + 47.5, [P, 2, L])
        rsq = at("ret_sq", W0 + 51.5, [P, L])
        rst = at("ret_stat", W0 + 53.5, [P, 2, 2, TT])
        cini = at("carry", W0 + 41.125, [P, 4])
        yrh = at("yr_hi", 2 * GR, [P, 4, L], F32R)
        yrl_ = at("yr_lo", 2 * QR, [P, 4, L], F32R)
        yrl = [yrl_[:, i, :] for i in (0, 2, 1, 3)]
        gh = at("gelu_hi", W0, [P, 4, L], F32R)
        gl = at("gelu_lo", W0 + 8, [P, 4, L], F32R)
        sg = at("glu_sig", W0 + 49, [P, 2, L])
        ysh = at("ys_hi", 2 * U0, [P, 4, L], F32R)
        ysl = at("ys_lo", 2 * VR, [P, 4, L], F32R)
        merged = at("merged", W0 + 16, [P, DK, L])
        gates = at("gates", W0, [P, 4, L])
        mt = at("merge_tmp", W0 + 8, [P, 2, L])
        pp = at("probs", W0 + 32, [P, TRI[TT]])
        pt = at("probs_t", W0 + 37, [P, TT, L])
        asq = at("attn_sq", W0 + 4, [P, 2, L])
        ams = at("attn_rms", W0 + 54, [P, 2, 2 * AH // 2, TT, 2])
        kwide = at("k_rms_wide", W0 + 45, [P, 2, L])
        gswap = at("swap_gained", W0 + 34, [P, 2, P])
        atmp = at("attn_tmp", W0 + 32, [P, L])
        ast = at("attn_stat", W0 + 54.75, [P, 4, 2])
        yah = at("ya_hi", 2 * QA, [P, 4, L], F32R)
        yal = at("ya_lo", 2 * KA, [P, 4, L], F32R)
        hh = at("hid_hi", 0, [P, 2, 8, L], F32R)
        hl = at("hid_lo", 32, [P, 2, 8, L], F32R)
        cg = at("conv_g", 64, [P, 2, L])
        cu = at("conv_u", 68, [P, 2, L])
        ht = at("hid", 72, [P, 2, L])

        pg = ctx.enter_context(nc.psum_tensor("ps_gemm", [P, 2, L], F32))
        pb = ctx.enter_context(nc.psum_tensor("ps_pair", [P, 2, L], F32))
        py = ctx.enter_context(nc.psum_tensor("ps_out", [P, L], F32))
        pr2 = ctx.enter_context(nc.psum_tensor("ps_ring", [P, 2, L], F32))
        po = ctx.enter_context(nc.psum_tensor("ps_out2", [P, L], F32))

        s_x = [ctx.enter_context(nc.semaphore(f"x_loaded{i}")) for i in range(4)]
        s_small = ctx.enter_context(nc.semaphore("small_consts_loaded"))
        s_tables = ctx.enter_context(nc.semaphore("tables_loaded"))
        s_early0 = ctx.enter_context(nc.semaphore("first_early_params"))
        s_dt0, s_th0, s_sc0 = [ctx.enter_context(nc.semaphore(n)) for n in ("first_exp", "first_theta", "first_sincos")]
        s_f0 = ctx.enter_context(nc.semaphore("first_factor"))
        s_cc0 = ctx.enter_context(nc.semaphore("first_c_scaled"))
        s_blk0 = ctx.enter_context(nc.semaphore("first_blocks"))
        s_raw0 = [ctx.enter_context(nc.semaphore(f"first_raw{i}")) for i in range(HEAD)]
        s_hi0, s_lo0 = [ctx.enter_context(nc.semaphore(n)) for n in ("first_w_hi", "first_w_lo")]
        s_store = ctx.enter_context(nc.semaphore("stored"))
        s_go = ctx.enter_context(nc.semaphore("layer_go"))
        s_ack = ctx.enter_context(nc.semaphore("layer_ack"))
        s_q0, s_s0 = [ctx.enter_context(nc.semaphore(n)) for n in ("first_sq", "first_ssum")]
        s_par = sem("params_in")
        s_early, s_blk = sem("early_params_in"), sem("blocks_in")
        s_raw = [sem(f"raw_in{i}") for i in range(RAW)]
        s_hi, s_lo = sem("w_hi_done"), sem("w_lo_done")
        s_mm = sem("gemm_done")
        s_ev = {"act": sem("evacuated_by_act"), "dve": sem("evacuated_by_dve")}
        s_sq = [sem("sq_a"), sem("sq_b")]
        s_su = [sem("sq_summed_a"), sem("sq_summed_b")]
        s_ss = [sem("ssum_a"), sem("ssum_b")]
        s_rc = [sem("recip_a"), sem("recip_b")]
        s_rb = [sem("rstd_spread_a"), sem("rstd_spread_b")]
        s_rt = [sem("rstd_a"), sem("rstd_b")]
        s_xn = [sem("xn_a"), sem("xn_b")]
        s_xh = [sem("xh_a"), sem("xh_b")]
        s_xl = [sem("xl_a"), sem("xl_b")]
        s_dt, s_th, s_sc = sem("s5_exp"), sem("s5_theta"), sem("s5_sincos")
        s_braw = [sem(f"b_raw_in{t}") for t in range(4)]
        s_bh, s_bs = sem("b_hi_s"), sem("b_split_s")
        s_uh, s_ul = sem("u_hi_s"), sem("u_lo_s")
        s_stack = [sem(f"u_stacked{j}") for j in range(4)]
        s_bu, s_rot, s_zz = sem("bu_done"), sem("bu_rotated"), sem("scanned")
        s_st, s_y, s_yp = sem("states_ready"), sem("y_done"), sem("y_pre")
        s_gh, s_gl = sem("gelu_hi_s"), sem("gelu_lo_s")
        s_yf, s_yh, s_yl = sem("ys_full"), sem("ys_hi_s"), sem("ys_lo_s")
        s_mg = sem("merged_part")
        s_mh, s_ml = sem("merged_hi"), sem("merged_lo")
        s_fill = sem("ring_filled")
        s_read = {"act": sem("ring_read_by_act"), "dve": sem("ring_read_by_dve")}
        s_ro, s_vc = sem("ret_rotated"), sem("v_copied")
        s_o, s_oc = sem("ret_o"), sem("ret_o_copied")
        s_q2, s_r2, s_rr = sem("gn_square"), sem("gn_recip"), sem("gn_rstd")
        s_yr, s_yrh, s_yrl = sem("yr_full"), sem("yr_hi_s"), sem("yr_lo_s")
        s_as, s_ar, s_at = (sem("att_sq"), sem("att_recip"), sem("att_rstd"))
        s_gw, s_kw, s_kb, s_ax = sem("swap_gained_s"), sem("k_rms_wide_s"), sem("k_rms_spread"), sem("att_rotated")
        s_sc_, s_mx, s_ex, s_pn = sem("att_scores"), sem("att_max"), sem("att_exp"), sem("att_probs")
        s_va2 = sem("att_v_copied")
        s_pv, s_yah, s_yal = sem("att_pv"), sem("ya_hi_s"), sem("ya_lo_s")
        s_c0, s_c1, s_si, s_hd, s_hh, s_hl = (sem("conv_first"), sem("conv_done"), sem("silu"), sem("hidden"),
                                              sem("hid_hi_s"), sem("hid_lo_s"))
        s_end = sem("layer_end")
        nums = sorted(s.num if hasattr(s, "num") else int(s) for s in sems)
        assert nums == list(range(nums[0], nums[-1] + 1)), nums
        ENGINES = 5

        def layer_end(eng):
            eng.drain().then_inc(s_end, 1)
            eng.wait_ge(s_go, 1)
            eng.drain().then_inc(s_ack, 1)

        def s5_output_blocks(eng, part):
            frb = sm[:, 12, :].unsqueeze(2).to_broadcast([P, ST, CH])
            fib = sm[:, 13, :].unsqueeze(2).to_broadcast([P, ST, CH])
            q1, q2 = pq[:, 0, :].rearrange("p (s c) -> p s c", s=ST), pq[:, 1, :].rearrange("p (s c) -> p s c", s=ST)
            if part == 0:
                eng.tensor_tensor(q1, cw_[:, 0, :, :], fib, ALU.mult)
                eng.tensor_tensor(q2, cw_[:, 1, :, :], fib, ALU.mult)
            if part == 1:
                eng.tensor_tensor(cw_[:, 0, :, :], cw_[:, 0, :, :], frb, ALU.mult)
                eng.tensor_tensor(cw_[:, 1, :, :], cw_[:, 1, :, :], frb, ALU.mult)
            if part == 2:
                eng.tensor_tensor(cw_[:, 0, :, :], cw_[:, 0, :, :], q2, ALU.subtract)
                eng.tensor_tensor(cw_[:, 1, :, :], cw_[:, 1, :, :], q1, ALU.add)
                eng.drain()
                eng.tensor_scalar(cw_[:, 1, :, :], cw_[:, 1, :, :], -1.0, None, ALU.mult)
                eng.tensor_scalar(cneg[:, :, :], cw_[:, 0, :, :], -1.0, None, ALU.mult)
            eng.drain()

        def bank_of(t):
            if t < T_O:
                return pg[:, t % 2, :]
            i = (t - T_O) % 4
            return (pg[:, i, :] if i < 2 else pb[:, i - 2, :])

        def filled(eng, step, i):
            n = FILL[step, i]
            eng.wait_ge(s_fill, n + 1)
            return pr2[:, n % 2, :]

        block = ctx.enter_context(nc.Block())

        @block.sync
        def _(sp):
            sp.dma_start(er[:, :], early[0, :, :]).then_inc(s_early0, 16)
            for i in range(4):
                k = slice(i * DK // 4, (i + 1) * DK // 4)
                sp.dma_start(x[:, k, :], xT[:, k, :]).then_inc(s_x[i], 16)
            sp.dma_start(consts[:, 0:small], cst[:, 0:small]).then_inc(s_small, 16)
            for n in range(HEAD):
                sp.dma_start(raw[:, n, :], wslab[n, :, :]).then_inc(s_raw0[n], 16)
            sp.dma_start(cw_[:, :, :, :], cblk[0, :, :, :, :]).then_inc(s_blk0, 16)
            sp.dma_start(consts[:, small:], cst[:, small:]).then_inc(s_tables, 16)
            sp.wait_ge(s_lo0, HEAD)
            with sp.Fori(0, DEPTH) as l:
                sp.dma_start(braw[0][:, :], bblk[l, :, 0, :]).then_inc(s_braw[0], 16)
                sp.dma_start(pr[:, :], par[l, :, :]).then_inc(s_par, 16)
                for n in range(HEAD, N_SLABS + HEAD):
                    if n >= HEAD + RAW:
                        sp.wait_ge(s_lo, n - RAW + 1 - HEAD)
                    sp.dma_start(raw[:, n % RAW, 0:width(n)], wslab[l * N_SLABS + n, :, 0:width(n)])\
                      .then_inc(s_raw[n % RAW], 16)
                    if 3 <= n < 6:
                        sp.dma_start(braw[n - 2][:, :], bblk[l, :, n - 2, :]).then_inc(s_braw[n - 2], 16)
                    if 5 <= n < 5 + ST:
                        t, j = (n - 5) // 4, (n - 5) % 4
                        sp.wait_ge(s_ul, t + 1)
                        for c in range(4):
                            sp.dma_start(stack[n - 5][CH * c:CH * (c + 1), :].bitcast(F32),
                                         (uhi, ulo)[c % 2][CH * j:CH * (j + 1), :].bitcast(F32))\
                              .then_inc(s_stack[j], 16)
                    if n == S_UP0 + 6:
                        sp.wait_ge(s_mm, tile_of(S_UP0) + 1)
                        sp.dma_start(er[:, :], early[l + 1, :, :]).then_inc(s_early, 16)
                        sp.dma_start(cw_[:, :, :, :], cblk[l + 1, :, :, :, :]).then_inc(s_blk, 16)
                sp.wait_ge(s_blk, 16)
                layer_end(sp)
            sp.dma_start(outT, x[:, :, :]).then_inc(s_store, 16)
            sp.wait_ge(s_store, 16)

        @block.gpsimd
        def _(pool):
            G = nc.gpsimd

            def lo(n, sem_hi=s_hi, sem_lo=s_lo, before=HEAD):
                w = width(n)
                pool.wait_ge(sem_hi, n + 1 - before)
                G.tensor_tensor(wl[:, n % RING, 0:w], raw[:, n % RAW, 0:w], wh[:, n % RING, 0:w].bitcast(F32),
                                ALU.subtract).then_inc(sem_lo, 1)

            def s5_back_products(s):
                b = s % 2
                C, S = [ph[:, b, i:i + 1, :].to_broadcast([P, 2 * L // CHUNK, CHUNK]) for i in range(2)]
                src = zz[:, b, :, :].rearrange("p a t -> p (a t)").rearrange("p (a t) -> p a t", t=CHUNK)
                pool.wait_ge(s_zz, s + 1)
                if s >= 1:
                    pool.wait_ge(s_y, s)
                G.tensor_tensor(stt[:, :, :].rearrange("p a t -> p (a t)").rearrange("p (a t) -> p a t", t=CHUNK), src, C, ALU.mult)
                G.tensor_tensor(pq[:, :, :].rearrange("p a t -> p (a t)").rearrange("p (a t) -> p a t", t=CHUNK), src, S, ALU.mult)
                pool.drain().then_inc(s_st, 1)

            for k in range(DK):
                pool.wait_ge(s_q0, k + 1)
                if k == 0:
                    G.tensor_copy(ssum[:, :], sq[:, 0, :])
                else:
                    G.tensor_tensor(ssum[:, :], ssum[:, :], sq[:, k % 2, :], ALU.add)
                pool.drain().then_inc(s_s0, 1)
            lo(0, s_hi0, s_lo0, 0)
            pool.wait_ge(s_f0, 1)
            pool.wait_ge(s_blk0, 16)
            for part in range(3):
                s5_output_blocks(nc.gpsimd, part)
            pool.drain().then_inc(s_cc0, 1)
            with pool.Fori(0, DEPTH) as l:
                lo(2)
                lo(3)
                for p in range(N_POINTS):
                    if p % 2 == 0:
                        lo(4 + p // 2)
                    if p >= 3 and p % 3 == 0 and p <= 3 * ST:
                        s5_back_products(p // 3 - 1)
                for n in range(4 + N_POINTS // 2, N_SLABS + HEAD):
                    lo(n)
                pool.wait_ge(s_end, ENGINES - 1)
                pool.drain()
                pool.sem_clear(range(nums[0], nums[-1] + 1))
                pool.drain().then_inc(s_go, 1)
                pool.wait_ge(s_ack, ENGINES - 1)
                pool.drain()
                pool.sem_clear(s_go)
                pool.sem_clear(s_ack)

        @block.tensor
        def _(pe):
            T = nc.tensor

            def bank_is_free(t):
                if tile_before(t) is not None:
                    who, count = evacuated(tile_before(t))
                    pe.wait_ge(s_ev[who], count)

            def slab(n, rh, rl, point=lambda i: None):
                _, kt, mts = STREAM[n]
                pe.wait_ge(s_lo, n + 1 - HEAD)
                vh = wh[:, n % RING, 0:width(n)].rearrange("p (k c) -> p k c", k=kt)
                vl = wl[:, n % RING, 0:width(n)].rearrange("p (k c) -> p k c", k=kt)
                for m in range(mts):
                    t = tile_of(n) + m
                    c = slice(m * P, (m + 1) * P)
                    bank_is_free(t)
                    for k in range(kt):
                        T.matmul(bank_of(t), vh[:, k, c], rh[k], start=(k == 0), stop=False)
                        T.matmul(bank_of(t), vh[:, k, c], rl[k], start=False, stop=False)
                        mm = T.matmul(bank_of(t), vl[:, k, c], rh[k], start=False, stop=(k == kt - 1))
                        if mts == 1 and k == kt // 2 - 1:
                            point(0)
                    mm.then_inc(s_mm, 1)
                    if mts == 2:
                        point(m)
                if mts == 1:
                    point(1)

            def slab_pair(n, rh, rl, ready):
                if n >= HEAD:
                    pe.wait_ge(s_lo, n + 2 - HEAD)
                for m in range(2):
                    bank_is_free(tile_of(n) + m)
                for k in range(DK):
                    pe.wait_ge(ready, k + 1)
                    for m in range(2):
                        bank = bank_of(tile_of(n) + m)
                        c = slice(k * P, (k + 1) * P)
                        vh, vl = wh[:, (n + m) % RING, c], wl[:, (n + m) % RING, c]
                        T.matmul(bank, vh, rh[k], start=(k == 0), stop=False)
                        T.matmul(bank, vh, rl[k], start=False, stop=False)
                        mm = T.matmul(bank, vl, rh[k], start=False, stop=(k == DK - 1))
                        if k == DK - 1:
                            mm.then_inc(s_mm, 1)

            def tiles(a):
                return [a[:, k, :] for k in range(a.shape[1])]

            X = (tiles(xh), tiles(xl))

            def norm_stat(i):
                for q in range(TT):
                    mm = T.matmul(po[:, q:q + 1], ssum[:, P * q:P * (q + 1)], ones[:, 0:1], start=True, stop=True)
                mm.then_inc(s_ss[i], 1)

            def spread(bank, stat):
                for q in range(TT):
                    mm = T.transpose(bank[:, P * q:P * (q + 1)], stat[:, q:q + 1].to_broadcast([P, P]), ident)
                return mm

            def norm_spread(i):
                pe.wait_ge(s_rt[i], 1)
                spread(po, nst[:, 1, :]).then_inc(s_rb[i], 1)

            def s5_in(s):
                t, j = s // 4, s % 4
                pe.wait_ge(s_bs, t + 1)
                pe.wait_ge(s_stack[j], 64 * (t + 1))
                if s >= 1:
                    pe.wait_ge(s_rot, s)
                T.matmul(pb[:, 0, :], bsplit[t][:, j, 0, :], stack[s][:, :], start=True, stop=True)
                T.matmul(pb[:, 1, :], bsplit[t][:, j, 1, :], stack[s][:, :], start=True, stop=True).then_inc(s_bu, 1)

            def s5_out(s):
                t, j = s // 4, s % 4
                r = slice(CH * j, CH * (j + 1))
                if s == 0:
                    pe.wait_ge(s_cc0, 1)
                pe.wait_ge(s_st, s + 1)
                if j == 0 and t >= 1:
                    pe.wait_ge(s_yp, t)
                parts = ((cw_[:, 0, s, :], stt[:, 0, :]), (cw_[:, 1, s, :], stt[:, 1, :]),
                         (cw_[:, 1, s, :], pq[:, 0, :]), (cneg[:, s, :], pq[:, 1, :]))
                for i, (c, z) in enumerate(parts):
                    mm = T.matmul(py[r, :], c, z, start=(i == 0), stop=(i == 3), tile_position=(0, CH * j))
                mm.then_inc(s_y, 1)

            def claim(step, i):
                n = FILL[step, i]
                if n >= 2:
                    who, count = reads_until(n - 2)
                    pe.wait_ge(s_read[who], count)
                return pr2[:, n % 2, :]

            def transposes(bank, first, x, centred=False):
                for i in range(TT):
                    out, block = bank[:, P * i:P * (i + 1)], proj[:, first + (i ^ x), P * i:P * (i + 1)]
                    if centred:
                        mm = T.matmul(out, block, centre, start=True, stop=True)
                    else:
                        mm = T.transpose(out, block, ident)
                return mm

            def ring_steps(p):
                for step, i, _ in point_steps(p):
                    if step == "swap_r":
                        if i == 0:
                            pe.wait_ge(s_ev["act"], KR + 2)
                        mm = T.matmul(claim(step, i), r_swap, proj[:, QR + i, :], start=True, stop=True)
                    if step == "turn_vr":
                        if i == 0:
                            pe.wait_ge(s_ev["act"], VR + 4)
                        mm = transposes(claim(step, i), VR, i, centred=True)
                    if step == "score_r":
                        h, j = i // TT, i % TT
                        r = slice(RQ * (h % 2), RQ * (h % 2) + RQ)
                        if i == 0:
                            pe.wait_ge(s_ro, 4)
                        mm = T.matmul(claim(step, i)[:, P * j:L], proj[r, KR + h // 2, P * j:P * (j + 1)],
                                      proj[r, QR + h // 2, P * j:L], start=True, stop=True)
                    if step == "var":
                        pe.wait_ge(s_q2, i + 1)
                        bank = claim(step, i)
                        for q in range(TT):
                            mm = T.matmul(bank[:, q:q + 1], rsq[:, P * q:P * (q + 1)], ones[:, 0:1], start=True, stop=True)
                    if step == "rstd_r":
                        pe.wait_ge(s_rr, i + 1)
                        mm = spread(claim(step, i), rst[:, i % 2, 1, :])
                    if step == "msq":
                        pe.wait_ge(s_as, i + 1)
                        bank = claim(step, i)
                        for q in range(TT):
                            mm = T.matmul(bank[:, 2 * q:2 * q + 2], asq[:, i % 2, P * q:P * (q + 1)], blk64[:, 0:P:AD],
                                          start=True, stop=True)
                    if step == "swap_a":
                        tile, half = QA + i // 2 + 4 * (i % 2), i % 2
                        if i == 0:
                            pe.wait_ge(s_gw, 1)
                        mm = T.matmul(claim(step, i), gswap[:, half, :], proj[:, tile, :], start=True, stop=True)
                    if step == "turn_va":
                        mm = transposes(claim(step, i), VA, i)
                    if step == "turn_p":
                        q = i % TT
                        pe.wait_ge(s_pn, i + 1)
                        bank = claim(step, i)
                        for j in range(q + 1):
                            mm = T.transpose(bank[:, P * j:P * (j + 1)], pp[:, TRI[q] + P * j:TRI[q] + P * (j + 1)], ident)
                    mm.then_inc(s_fill, 1)

            def ret_out(p):
                g = p - RET0 - 8
                if 1 <= g <= 4 * RH:
                    h, j = (g - 1) // TT, (g - 1) % TT
                    if g == 1:
                        pe.wait_ge(s_vc, 4)
                    pe.wait_ge(s_read["dve"], reads_until(FILL["score_r", g - 1])[1])
                    if j == 0 and h >= 1:
                        pe.wait_ge(s_oc, h)
                    mm = T.matmul(po[:, P * j:L], proj[:, VR + j, P * h:P * (h + 1)], sd[:, DIAG[j]:DIAG[j + 1]],
                                  start=(j == 0), stop=(j == TT - 1))
                    if j == TT - 1:
                        mm.then_inc(s_o, 1)

            def proj_point(p):
                if p % 3 == 0 and p < 3 * ST:
                    s5_in(p // 3)
                if p % 3 == 2 and 5 <= p < 3 * ST + 3:
                    s5_out(p // 3 - 1)
                ring_steps(p)
                ret_out(p)

            def att_point(p):
                if p < 8 and p % 2 == 1:
                    i = p // 2
                    pe.wait_ge(s_kw, i + 1)
                    if i == 0:
                        pe.wait_ge(s_rot, ST)
                    if i >= 2:
                        pe.wait_ge(s_ax, 2 * (i - 2) + 2)
                    for q in range(TT):
                        mm = T.transpose(pb[:, i % 2, P * q:P * (q + 1)], kwide[:, i % 2, P * q:P * (q + 1)], ident)
                    mm.then_inc(s_kb, 1)
                v = p - HEAD0
                if 0 <= v < TT * AH:
                    h, q = v // TT, v % TT
                    r = slice(AD * (h % 2), AD * (h % 2) + AD)
                    if v % (2 * TT) == 0:
                        pe.wait_ge(s_ax, h + 2)
                    if v == 0:
                        pe.wait_ge(s_ax, 8)
                    if v >= 2:
                        pe.wait_ge(s_ex, v - 1)
                    T.matmul(pb[:, v % 2, 0:P * (q + 1)], proj[r, QA + h // 2, P * q:P * (q + 1)],
                             proj[r, KA + h // 2, 0:P * (q + 1)], start=True, stop=True).then_inc(s_sc_, 1)
                ring_steps(N_POINTS + p)
                if v >= 7 and (v - 7) % 4 == 0 and (v - 7) // 4 < AH:
                    h = (v - 7) // 4
                    b = AD * (h % 2)
                    pe.wait_ge(s_read["act"], reads_until(FILL["turn_p", TT * h + 3])[1])
                    if h % 2 == 0 and h >= 2:
                        pe.wait_ge(s_yal, h // 2)
                    if h == 0:
                        pe.wait_ge(s_yp, 4)
                        pe.wait_ge(s_va2, 4)
                    for j in range(TT):
                        mm = T.matmul(py[b:b + AD, P * j:L], proj[:, VA + j, AD * h:AD * (h + 1)], pt[:, j, P * j:L],
                                      start=(j == 0), stop=(j == TT - 1), tile_position=(0, b))
                    mm.then_inc(s_pv, 1)

            def branch_slabs(first, n, a, point=lambda i, j: None):
                for i in range(n):
                    slab(first + i, a[0], a[1], lambda j: point(i, j))

            pe.wait_ge(s_small, 16)
            pe.wait_ge(s_s0, DK)
            pe.wait_ge(s_lo0, HEAD)
            with pe.Fori(0, DEPTH) as l:
                norm_stat(0)
                norm_spread(0)
                slab_pair(0, *X, s_xl[0])
                for n in range(2, N_PROJ):
                    slab(n, *X, point=lambda i: proj_point(2 * (n - 2) + i))
                for i, n in enumerate(P3):
                    kind = STREAM[n][0]
                    if kind == "gate":
                        a = X
                    elif kind == "glu":
                        a = (tiles(gh), tiles(gl))
                    elif n < S_BR:
                        a = (tiles(ysh), tiles(ysl))
                    else:
                        a = (tiles(yrh), yrl)
                    if n == S_GLU:
                        pe.wait_ge(s_gl, 4)
                    if n == S_BS:
                        pe.wait_ge(s_yl, 4)
                    if n == S_BR:
                        pe.wait_ge(s_yrl, 4)
                    slab(n, *a, point=lambda j: att_point(2 * i + j))
                for n in range(S_A, S_O):
                    if n == S_A + 4:
                        pe.wait_ge(s_yal, 4)
                    slab(n, *(X if STREAM[n][0] == "gate" else (tiles(yah), tiles(yal))))
                slab_pair(S_O, *X, s_ml)
                for n in range(S_O + 2, S_O + DK):
                    slab(n, *X)
                pe.wait_ge(s_su[1], DK)
                norm_stat(1)
                norm_spread(1)
                slab_pair(S_UP0, *X, s_xl[1])
                for n in range(S_UP0 + 2, N_SLABS):
                    if STREAM[n][0] == "up":
                        slab(n, *X)
                    else:
                        seg = 0 if n < S_UP2 else 1 if n < S_DN2 else 2
                        if n in (S_DN0, S_DN1, S_DN2):
                            pe.wait_ge(s_hl, sum(SEGS[:seg + 1]))
                        slab(n, [hh[:, seg % 2, k, :] for k in range(8)], [hl[:, seg % 2, k, :] for k in range(8)])
                layer_end(pe)

        @block.scalar
        def _(act):
            A = nc.scalar

            def hi(n):
                w = width(n)
                if n >= HEAD:
                    act.wait_ge(s_raw[n % RAW], 16 * ((n - HEAD) // RAW + 1))
                else:
                    act.wait_ge(s_raw0[n], 16)
                if n >= RING:
                    act.wait_ge(s_mm, tile_of(n - RING + 1))
                A.activation(wh[:, n % RING, 0:w], raw[:, n % RAW, 0:w], ACT.Copy).then_inc(s_hi if n >= HEAD else s_hi0, 1)

            def square_step(k, i):
                if k >= 2:
                    act.wait_ge(s_su[i], k - 1)
                A.activation(sq[:, k % 2, :], x[:, k, :], ACT.Square).then_inc(s_sq[i], 1)

            def norm(i):
                A.activation(nst[:, 2, :], ident[:, 0:TT], ACT.Sqrt)
                act.wait_ge(s_rc[i], 1)
                A.activation(nst[:, 1, :], nst[:, 0, :], ACT.Sqrt).then_inc(s_rt[i], 1)
                for k in range(DK):
                    act.wait_ge(s_xn[i], k + 1)
                    A.activation(xh[:, k, :], xn[:, k % 4, :], ACT.Copy).then_inc(s_xh[i], 1)
                    if i == 0 and k in (2, 5):
                        hi(2 + k // 5)

            def evac(t, dst, func=ACT.Copy, scale=1.0):
                act.wait_ge(s_mm, t + 1)
                return A.activation(dst, bank_of(t), func, scale=scale).then_inc(s_ev["act"], 1)

            def copy_transposed(bank, first, x):
                for i in range(TT):
                    A.activation(proj[:, first + i, P * (i ^ x):P * ((i ^ x) + 1)], bank[:, P * i:P * (i + 1)], ACT.Copy)

            def read_done():
                act.drain().then_inc(s_read["act"], 1)

            def proj_point(p):
                v = p - RET0
                if 5 <= v < 9:
                    copy_transposed(filled(act, "turn_vr", v - 5), VR, v - 5)
                    act.drain().then_inc(s_vc, 1)
                    read_done()
                g = v - 8
                for h in range(RH):
                    if g == 4 * h + 5:
                        act.wait_ge(s_o, h + 1)
                        A.activation(rsq[:, :], po[:, :], ACT.Square).then_inc(s_q2, 1)
                        if h >= 2:
                            act.wait_ge(s_yrl, h - 1)
                        A.activation(osb[:, h % 2, :], po[:, :], ACT.Copy, scale=prm("gn")[:, h:h + 1]).then_inc(s_oc, 1)
                        act.drain()
                    if g == 4 * h + 7:
                        act.wait_ge(s_r2, h + 1)
                        A.activation(rst[:, h % 2, 1, :], rst[:, h % 2, 0, :], ACT.Sqrt).then_inc(s_rr, 1)
                    if g == 4 * h + 9:
                        act.wait_ge(s_yr, h + 1)
                        A.activation(yrh[:, h, :], osb[:, h % 2, :], ACT.Copy).then_inc(s_yrh, 1)
                m = p - MSQ0
                if m >= 0 and m % 2 == 0 and m < 16:
                    i = m // 2
                    if i >= 2:
                        act.wait_ge(s_fill, FILL["msq", i - 2] + 1)
                    act.wait_ge(s_ev["act"], QA + i + 1)
                    if i == 0:
                        for j in range(4):
                            act.wait_ge(s_stack[j], 256)
                    A.activation(asq[:, i % 2, :], proj[:, QA + i, :], ACT.Square).then_inc(s_as, 1)
                if m == 18:
                    act.wait_ge(s_ar, 1)
                    A.activation(ams[:, 1, :, :, :], ams[:, 0, :, :, :], ACT.Sqrt).then_inc(s_at, 1)

            def att_point(p):
                if p < 8 and p % 2 == 0:
                    i = p // 2
                    if i >= 2:
                        act.wait_ge(s_kb, i - 1)
                    A.activation(kwide[:, i % 2, :].rearrange("p (q d) -> p q d", d=AD),
                                 ams[:, 1, 4 + i, :, :].rearrange("p q h -> p (q h)").unsqueeze(2).to_broadcast([P, 2 * TT, AD]),
                                 ACT.Copy).then_inc(s_kw, 1)
                if 5 <= p < 9:
                    copy_transposed(filled(act, "turn_va", p - 5), VA, p - 5)
                    act.drain().then_inc(s_va2, 1)
                    read_done()
                v = p - HEAD0 - 1
                if 0 <= v < TT * AH:
                    h, q = v // TT, v % TT
                    act.wait_ge(s_mx, v + 1)
                    if v >= 4:
                        act.wait_ge(s_fill, FILL["turn_p", v - 4] + 1)
                    A.activation(pp[:, TRI[q]:TRI[q + 1]], pb[:, v % 2, 0:P * (q + 1)], ACT.Exp, bias=ast[:, 1, v % 2:v % 2 + 1],
                                 scale=ams[:, 0, h // 2, q, h % 2:h % 2 + 1], accum_out=ast[:, 2, v % 2:v % 2 + 1]).then_inc(s_ex, 1)
                w = p - HEAD0 - 3
                if 0 <= w < TT * AH:
                    h, q = w // TT, w % TT
                    bank = filled(act, "turn_p", w)
                    if h >= 1:
                        act.wait_ge(s_pv, h)
                    A.activation(pt[:, 0:q + 1, P * q:P * (q + 1)], bank[:, 0:P * (q + 1)].rearrange("p (j c) -> p j c", c=P),
                                 ACT.Copy)
                    read_done()
                v = p - HEAD0
                if v >= 12 and (v - 12) % 8 == 0 and (v - 12) // 8 < 4:
                    t = (v - 12) // 8
                    act.wait_ge(s_pv, 2 * t + 2)
                    A.activation(yah[:, t, :], py[:, :], ACT.Copy).then_inc(s_yah, 1)

            def s5_exp(sem_dt, sem_th):
                A.activation(sm[:, 0, :], prm("ldt"), ACT.Exp).then_inc(sem_dt, 1)
                act.wait_ge(sem_th, 1)
                A.activation(sm[:, 2, :], sm[:, 1, :], ACT.Exp).then_inc(sem_dt, 1)

            def s5_sin(sem_th, sem_sc):
                act.wait_ge(sem_th, 2)
                A.activation(sm[:, 5, :], sm[:, 4, :], ACT.Sin)
                A.activation(sm[:, 6, :], sm[:, 4, :], ACT.Sin, scale=0.5).then_inc(sem_sc, 1)

            act.wait_ge(s_early0, 16)
            s5_exp(s_dt0, s_th0)
            s5_sin(s_th0, s_sc0)
            for k in range(DK):
                if k % 2 == 0:
                    act.wait_ge(s_x[k // 2], 16)
                if k >= 2:
                    act.wait_ge(s_s0, k - 1)
                A.activation(sq[:, k % 2, :], x[:, k, :], ACT.Square).then_inc(s_q0, 1)
            hi(0)
            hi(1)
            act.wait_ge(s_small, 16)
            with act.Fori(0, DEPTH) as l:
                norm(0)
                act.wait_ge(s_par, 16)
                for n in range(N_PROJ):
                    if n >= 1:
                        hi(n + AHEAD)
                    for i in range(2):
                        if n >= 2:
                            proj_point(2 * (n - 2) + i)
                    if n >= 5 and (n - 1) % 4 == 0 and n < 17:
                        t = (n - 1) // 4
                        act.wait_ge(s_ev["act"], t + 1)
                        if t >= 1:
                            for j in range(4):
                                act.wait_ge(s_stack[j], 64 * t)
                        A.activation(uhi[:, :], proj[:, U0 + t, :], ACT.Copy).then_inc(s_uh, 1)
                    evac(n, proj[:, n, :], ACT.Silu if GR <= n < GR + RH else ACT.Copy)
                    if n == 0:
                        act.wait_ge(s_ev["act"], 1)
                        A.activation(uhi[:, :], proj[:, U0, :], ACT.Copy).then_inc(s_uh, 1)
                    if n < 4:
                        act.wait_ge(s_braw[n], 16)
                        if n >= 1:
                            act.wait_ge(s_bs, n)
                        A.activation(btmp[AD:P, :], braw[n][AD:P, :], ACT.Copy)
                        A.activation(bsplit[n][0:AD, :, :, :].rearrange("p j i c -> p (j i c)"), braw[n][0:AD, :], ACT.Copy)
                        act.drain().then_inc(s_bh, 1)
                act.drain()
                for t in range(4):
                    act.wait_ge(s_yp, t + 1)
                    A.activation(proj[:, U0 + t, :], proj[:, U0 + t, :], ACT.Gelu_apprx_tanh)
                act.drain()
                act.wait_ge(s_y, ST)
                act.wait_ge(s_yrl, RH)
                act.wait_ge(s_fill, FILL["msq", 7] + 1)
                for t in range(4):
                    A.activation(gh[:, t, :], proj[:, U0 + t, :], ACT.Copy).then_inc(s_gh, 1)
                for i, n in enumerate(P3):
                    kind = STREAM[n][0]
                    t = tile_of(n)
                    hi(n + AHEAD)
                    att_point(2 * i)
                    att_point(2 * i + 1)
                    if kind == "glu":
                        m = n - S_GLU
                        if m >= 2:
                            act.wait_ge(s_yl, m - 1)
                        evac(t, sg[:, m % 2, :], ACT.Tanh, 0.5)
                    if S_GLU < n <= S_GR:
                        m = n - S_GLU - 1
                        act.wait_ge(s_yf, m + 1)
                        A.activation(ysh[:, m, :], sg[:, m % 2, :], ACT.Copy, scale=0.5).then_inc(s_yh, 1)
                    if kind == "gate" and n < S_GLU:
                        evac(t, merged[:, n - S_GS, :], ACT.Tanh, 0.5)
                    elif kind == "gate":
                        q = n - S_GR if n < S_BS else n - S_GR2
                        if n == S_GR:
                            act.wait_ge(s_mm, tile_of(S_GR))
                        if n == S_GR2:
                            act.wait_ge(s_mg, 8 + 4)
                        evac(t, gates[:, q, :], ACT.Tanh, 0.5)
                for n in range(S_A, S_O):
                    hi(n + AHEAD)
                    if STREAM[n][0] == "gate":
                        j, q = (n - S_A) // 6, (n - S_A) % 6
                        if q == 0:
                            act.wait_ge(s_mg, 16 + 4 * j)
                        evac(tile_of(n), gates[:, q, :], ACT.Tanh, 0.5)
                act.wait_ge(s_mm, tile_of(S_O - 2))
                for k in range(DK):
                    act.wait_ge(s_mg, 16 + k + 1)
                    A.activation(xh[:, k, :], merged[:, k, :], ACT.Copy, scale=0.5).then_inc(s_mh, 1)
                dv = evacuated(tile_of(S_O))[1] - 1
                for k in range(DK):
                    hi(S_O + k + AHEAD)
                    if k >= 1:
                        act.wait_ge(s_ev["dve"], dv + k)
                        square_step(k - 1, 1)
                act.wait_ge(s_ev["dve"], dv + DK)
                square_step(DK - 1, 1)
                norm(1)
                g = 0
                for n in range(S_UP0, N_SLABS):
                    t = tile_of(n)
                    if n + AHEAD < N_SLABS + HEAD:
                        hi(n + AHEAD)
                    if STREAM[n][0] == "up":
                        m, b = (t - tile_of(S_UP0)) % 2, g % 2
                        act.wait_ge(s_mm, t + 1)
                        if g >= 2:
                            act.wait_ge(s_hd, g - 1)
                        f = m * FT + g
                        c0, w0 = PAR["cb"][0] + f, PAR["cw"][0] + 2 * 2 * FT + f
                        A.activation((cg, cu)[m][:, b, :], bank_of(t), ACT.Identity, bias=pr[:, c0:c0 + 1],
                                     scale=pr[:, w0:w0 + 1]).then_inc(s_c0, 1)
                        if m == 1:
                            act.wait_ge(s_c1, 2 * g + 1)
                            A.activation(cg[:, b, :], cg[:, b, :], ACT.Silu).then_inc(s_si, 1)
                            act.wait_ge(s_hd, g + 1)
                            seg = 0 if g < SEGS[0] else 1 if g < SEGS[0] + SEGS[1] else 2
                            i = g - sum(SEGS[:seg])
                            if seg == 2 and i == 0:
                                act.wait_ge(s_mm, tile_of(S_UP2))
                            A.activation(hh[:, seg % 2, i, :], ht[:, b, :], ACT.Copy).then_inc(s_hh, 1)
                            g += 1
                    elif n == S_DN0:
                        act.wait_ge(s_early, 16)
                        s5_exp(s_dt, s_th)
                    elif n == S_DN0 + 1:
                        s5_sin(s_th, s_sc)
                    if n > S_DN2:
                        act.wait_ge(s_ev["dve"], evacuated(t - 1)[1])
                        square_step(n - S_DN2 - 1, 0)
                act.wait_ge(s_ev["dve"], evacuated(tile_of(N_SLABS - 1))[1])
                square_step(DK - 1, 0)
                layer_end(act)

        @block.vector
        def _(dve):
            V = nc.vector

            def sum_step(k, sem_sq, sem_su):
                dve.wait_ge(sem_sq, k + 1)
                if k == 0:
                    V.tensor_copy(ssum[:, :], sq[:, 0, :])
                else:
                    V.tensor_tensor(ssum[:, :], ssum[:, :], sq[:, k % 2, :], ALU.add)
                dve.drain().then_inc(sem_su, 1)

            def norm(i, g):
                dve.wait_ge(s_ss[i], 1)
                V.tensor_scalar(nst[:, 0, :], po[:, 0:TT], 1.0 / D, EPS, ALU.mult, ALU.add)
                dve.drain()
                V.reciprocal(nst[:, 0, :], nst[:, 0, :]).then_inc(s_rc[i], 1)
                dve.wait_ge(s_rb[i], 1)
                for k in range(DK + 1):
                    if k < DK:
                        V.scalar_tensor_tensor(xn[:, k % 4, :], x[:, k, :], prm(g)[:, k:k + 1], po[:, :], ALU.mult, ALU.mult)\
                         .then_inc(s_xn[i], 1)
                    if k >= 1:
                        dve.wait_ge(s_xh[i], k)
                        V.tensor_tensor(xl[:, k - 1, :], xn[:, (k - 1) % 4, :], xh[:, k - 1, :].bitcast(F32), ALU.subtract)\
                         .then_inc(s_xl[i], 1)
                    if k == 3 or k == 7:
                        dve.drain()

            def tt(out, a, b, op):
                V.tensor_tensor(out, a, b, op)
                return dve.drain()

            def s5_theta(sem_early, sem_dt, sem_th):
                dve.wait_ge(sem_early, 16)
                dve.wait_ge(sem_dt, 1)
                dt, lre, lim = sm[:, 0, :], prm("lre"), prm("lim")
                tt(sm[:, 1, :], lre, dt, ALU.mult).then_inc(sem_th, 1)
                tt(sm[:, 3, :], lim, dt, ALU.mult)
                two_pi = 2 * np.pi
                c1 = float(np.float32(6.28125))
                c2 = float(np.float32(two_pi - c1))
                c2 = float(np.float32(np.floor(c2 * 2 ** 22) / 2 ** 22))
                c3 = float(np.float32(two_pi - c1 - c2))
                big = float(1.5 * 2 ** 23)
                V.tensor_scalar(sm[:, 7, :], sm[:, 3, :], float(np.float32(1 / two_pi)), big, ALU.mult, ALU.add)
                dve.drain()
                V.tensor_scalar(sm[:, 7, :], sm[:, 7, :], -big, None, ALU.add)
                dve.drain()
                for c in (c1, c2, c3):
                    V.scalar_tensor_tensor(sm[:, 3, :], sm[:, 7, :], -c, sm[:, 3, :], ALU.mult, ALU.add)
                    dve.drain()
                V.tensor_scalar(sm[:, 4, :], sm[:, 3, :], float(np.float32(3.1415925)), float(np.float32(-3.1415925)), ALU.min, ALU.max)
                dve.drain().then_inc(sem_th, 1)

            def s5_cos(sem_sc, sem_dt):
                dve.wait_ge(sem_sc, 1)
                dve.wait_ge(sem_dt, 2)
                sh, cos = sm[:, 6, :], sm[:, 8, :]
                tt(cos, sh, sh, ALU.mult)
                V.tensor_scalar(cos, cos, -2.0, 1.0, ALU.mult, ALU.add)
                dve.drain()
                V.tensor_copy(pw[:, 0, 0, :], cos)
                V.tensor_copy(pw[:, 1, 0, :], sm[:, 5, :])
                dve.drain()

            def s5_powers(levels):
                t1, t2 = sm[:, 14, :], sm[:, 15, :]
                for n in levels:
                    c, s = pw[:, 0, n - 1, :], pw[:, 1, n - 1, :]
                    V.tensor_tensor(t1, c, c, ALU.mult)
                    V.tensor_tensor(t2, s, s, ALU.mult)
                    V.scalar_tensor_tensor(pw[:, 1, n, :], c, 2.0, s, ALU.mult, ALU.mult)
                    dve.drain()
                    tt(pw[:, 0, n, :], t1, t2, ALU.subtract)

            def s5_first_phases(lv):
                if lv == 0:
                    V.memset(ph0[:, :, 0, 0:1], 1.0)
                    V.memset(ph0[:, :, 1, 0:1], 0.0)
                    dve.drain()
                n = 2 ** lv
                c = pw[:, 0, lv, :].unsqueeze(2).to_broadcast([P, ST, n])
                s = pw[:, 1, lv, :].unsqueeze(2).to_broadcast([P, ST, n])
                q1, q2, q3, q4 = [pq[:, i // 2, ST * BASE // 2 * (i % 2):ST * BASE // 2 * (i % 2) + ST * n]
                                  .rearrange("p (s c) -> p s c", s=ST) for i in range(4)]
                C, S = ph0[:, :, 0, 0:n], ph0[:, :, 1, 0:n]
                V.tensor_tensor(q1, C, c, ALU.mult)
                V.tensor_tensor(q2, S, s, ALU.mult)
                V.tensor_tensor(q3, C, s, ALU.mult)
                V.tensor_tensor(q4, S, c, ALU.mult)
                dve.drain()
                V.tensor_tensor(ph0[:, :, 0, n:2 * n], q1, q2, ALU.subtract)
                V.tensor_tensor(ph0[:, :, 1, n:2 * n], q3, q4, ALU.add)
                dve.drain()

            def s5_prepare_part(i):
                if i == 0:
                    s5_theta(s_early, s_dt, s_th)
                if i == 1:
                    s5_cos(s_sc, s_dt)
                if i in (2, 3, 4, 5):
                    s5_powers((2 * i - 3, 2 * i - 2))
                if 6 <= i < 11:
                    s5_first_phases(i - 6)
                if i == 11:
                    s5_input_factor()
                if i == 12:
                    dve.wait_ge(s_blk, 16)
                if 12 <= i < 15:
                    s5_output_blocks(nc.vector, i - 12)

            def s5_input_factor():
                lre, lim = prm("lre"), prm("lim")
                sin, r, cos = sm[:, 5, :], sm[:, 2, :], sm[:, 8, :]
                nre, nim, den, fr, fi, t1, t2 = [sm[:, 9 + i, :] for i in range(7)]
                tt(nre, cos, r, ALU.mult)
                V.tensor_scalar(nre, nre, -1.0, None, ALU.add)
                tt(nim, sin, r, ALU.mult)
                tt(t1, lre, lre, ALU.mult)
                tt(t2, lim, lim, ALU.mult)
                tt(den, t1, t2, ALU.add)
                V.reciprocal(den, den)
                tt(t1, nre, lre, ALU.mult)
                tt(t2, nim, lim, ALU.mult)
                tt(fr, t1, t2, ALU.add)
                tt(fr, fr, den, ALU.mult)
                tt(t1, nim, lre, ALU.mult)
                tt(t2, nre, lim, ALU.mult)
                tt(fi, t1, t2, ALU.subtract)
                tt(fi, fi, den, ALU.mult)

            def phases_scaled(s, lv):
                n = 2 ** lv
                known = ph0[:, s, :, :] if n == BASE else ph[:, s % 2, :, 0:n]
                V.tensor_scalar(pscr[:, :, 0:n], known, pw[:, 1, lv, s:s + 1], None, ALU.mult)

            def phases_doubled(s, lv):
                b, n = s % 2, 2 ** lv
                known = ph0[:, s, :, :] if n == BASE else ph[:, b, :, 0:n]
                c = pw[:, 0, lv, s:s + 1]
                if n == BASE:
                    if s >= 2:
                        dve.wait_ge(s_st, s - 1)
                    V.tensor_copy(ph[:, b, :, 0:n], known)
                V.scalar_tensor_tensor(ph[:, b, 0, n:2 * n], known[:, 0, :], c, pscr[:, 1, 0:n], ALU.mult, ALU.subtract)
                V.scalar_tensor_tensor(ph[:, b, 1, n:2 * n], known[:, 1, :], c, pscr[:, 0, 0:n], ALU.mult, ALU.add)

            def s5_phases(s):
                for lv in PHASE_LEVELS:
                    phases_scaled(s, lv)
                    dve.drain()
                    phases_doubled(s, lv)
                    dve.drain()

            def b_remainder(t):
                dve.wait_ge(s_bh, t + 1)
                V.tensor_tensor(bsplit[t][AD:P, :, :, :].rearrange("p j i c -> p (j i c)"), braw[t][AD:P, :],
                                btmp[AD:P, :].bitcast(F32), ALU.subtract).then_inc(s_bs, 1)

            def u_remainder(t):
                dve.wait_ge(s_uh, t + 1)
                V.tensor_tensor(ulo[:, :], proj[:, U0 + t, :], uhi[:, :].bitcast(F32), ALU.subtract).then_inc(s_ul, 1)

            def s5_rotate(s):
                b = s % 2
                C, S = [ph[:, b, i:i + 1, :].to_broadcast([P, 2 * L // CHUNK, CHUNK]) for i in range(2)]
                src = pb[:, :, :].rearrange("p a t -> p (a t)").rearrange("p (a t) -> p a t", t=CHUNK)
                dst = zz[:, b, :, :].rearrange("p a t -> p (a t)").rearrange("p (a t) -> p a t", t=CHUNK)
                tmp = p2[:, :, :].rearrange("p a t -> p (a t)").rearrange("p (a t) -> p a t", t=CHUNK)
                dve.wait_ge(s_bu, s + 1)
                if s >= 2:
                    dve.wait_ge(s_st, s - 1)
                V.tensor_tensor(dst, src, C, ALU.mult)
                V.tensor_tensor(tmp, src, S, ALU.mult)
                dve.drain().then_inc(s_rot, 1)
                V.tensor_tensor(zz[:, b, 0, :], zz[:, b, 0, :], p2[:, 1, :], ALU.add)
                V.tensor_tensor(zz[:, b, 1, :], zz[:, b, 1, :], p2[:, 0, :], ALU.subtract)
                dve.drain()

            def s5_scan(s):
                b = s % 2
                r = sm[:, 2, s:s + 1].to_broadcast([P, CHUNK])
                c, sn = pw[:, 0, LEVELS - 1, s:s + 1], pw[:, 1, LEVELS - 1, s:s + 1]
                more = s + 1 < ST
                for a in range(2):
                    z = zz[:, b, a, 0:CHUNK]
                    V.tensor_tensor_scan(z, r, z, 0.0, ALU.mult, ALU.add)
                if more:
                    phases_scaled(s + 1, 5)
                dve.drain()
                last = zz[:, b, :, CHUNK - 1]
                V.tensor_scalar(cini[:, 0:2], last, sn, None, ALU.mult)
                if more:
                    phases_doubled(s + 1, 5)
                dve.drain()
                V.scalar_tensor_tensor(cini[:, 2:3], last[:, 0:1], c, cini[:, 1:2], ALU.mult, ALU.subtract)
                V.scalar_tensor_tensor(cini[:, 3:4], last[:, 1:2], c, cini[:, 0:1], ALU.mult, ALU.add)
                if more:
                    phases_scaled(s + 1, 6)
                dve.drain()
                for a in range(2):
                    z = zz[:, b, a, CHUNK:L]
                    V.tensor_tensor_scan(z, r, z, cini[:, 2 + a:3 + a], ALU.mult, ALU.add)
                if more:
                    phases_doubled(s + 1, 6)
                dve.drain().then_inc(s_zz, 1)
                if more:
                    phases_scaled(s + 1, 7)
                    dve.drain()
                    phases_doubled(s + 1, 7)
                    dve.drain()

            def s5_channels(t):
                dve.wait_ge(s_y, 4 * t + 4)
                V.scalar_tensor_tensor(proj[:, U0 + t, :], proj[:, U0 + t, :], prm("d")[:, t:t + 1], py[:, :], ALU.mult, ALU.add)\
                 .then_inc(s_yp, 1)

            def read_done():
                dve.drain().then_inc(s_read["dve"], 1)

            def proj_point(p):
                v = p - RET0
                if 0 <= v < 4:
                    tl, sc = QR + v, (1.0, 1.0, RQ ** -0.5, RQ ** -0.5)[v]
                    V.scalar_tensor_tensor(rsq[:, :], filled(dve, "swap_r", v), sc, r_sin, ALU.mult, ALU.mult)
                    V.scalar_tensor_tensor(proj[:, tl, :], proj[:, tl, :], sc, r_cos, ALU.mult, ALU.mult)
                    read_done()
                    V.tensor_tensor(proj[:, tl, :], proj[:, tl, :], rsq[:, :], ALU.add).then_inc(s_ro, 1)
                    dve.drain()
                g = v - 8
                if 0 <= g < TT * RH:
                    h, j = g // TT, g % TT
                    bank = filled(dve, "score_r", g)
                    if h >= 1 and j == 0:
                        dve.wait_ge(s_o, h)
                    V.tensor_tensor(sd[:, DIAG[j]:DIAG[j + 1]], bank[:, P * j:L], decay[:, h, 0:L - P * j], ALU.mult)
                    read_done()
                for h in range(RH):
                    o, b = osb[:, h % 2, :], h % 2
                    if g == 4 * h + 6:
                        V.tensor_scalar(rst[:, b, 0, :], filled(dve, "var", h)[:, 0:TT], 1.0 / P, EPS, ALU.mult, ALU.add)
                        read_done()
                        V.reciprocal(rst[:, b, 0, :], rst[:, b, 0, :]).then_inc(s_r2, 1)
                    if g == 4 * h + 8:
                        dve.wait_ge(s_oc, h + 1)
                        dve.wait_ge(s_ev["act"], GR + h + 1)
                        V.tensor_tensor(o, o, filled(dve, "rstd_r", h), ALU.mult)
                        read_done()
                        V.tensor_tensor(o, o, proj[:, GR + h, :], ALU.mult).then_inc(s_yr, 1)
                    if g == 4 * h + 10:
                        dve.wait_ge(s_yrh, h + 1)
                        V.tensor_tensor(yrl[h], o, yrh[:, h, :].bitcast(F32), ALU.subtract).then_inc(s_yrl, 1)
                m = p - MSQ0 - 1
                if m >= 0 and m % 2 == 0 and m < 16:
                    V.tensor_scalar(ams[:, 0, m // 2, :, :].rearrange("p q h -> p (q h)"), filled(dve, "msq", m // 2)[:, 0:2 * TT],
                                    EPS, None, ALU.add)
                    read_done()
                if m == 15:
                    V.reciprocal(ams[:, 0, :, :, :], ams[:, 0, :, :, :]).then_inc(s_ar, 1)
                if m == 17:
                    dve.wait_ge(s_at, 1)
                    V.tensor_scalar(ams[:, 0, 0:4, :, :], ams[:, 1, 0:4, :, :], AD ** -0.5, None, ALU.mult)
                    dve.drain()

            def swap_gains():
                V.tensor_scalar(gswap[:, 0, :], a_swap, prm("qn"), None, ALU.mult)
                V.tensor_scalar(gswap[:, 1, :], a_swap, prm("kn"), None, ALU.mult).then_inc(s_gw, 1)

            def att_point(p):
                if 1 <= p < 9:
                    i, half = (p - 1) // 2, (p - 1) % 2
                    a = proj[:, QA + i + 4 * half, :]
                    V.tensor_tensor(atmp[:, :], filled(dve, "swap_a", p - 1), a_sin, ALU.mult)
                    V.scalar_tensor_tensor(a, a, prm("kn" if half else "qn"), a_cos, ALU.mult, ALU.mult)
                    read_done()
                    V.tensor_tensor(a, a, atmp[:, :], ALU.add)
                    if half:
                        dve.drain()
                        dve.wait_ge(s_kb, i + 1)
                        V.tensor_tensor(a, a, pb[:, i % 2, :], ALU.mult)
                    dve.drain().then_inc(s_ax, 1)
                v = p - HEAD0
                if 0 <= v < TT * AH:
                    q, b = v % TT, v % 2
                    dve.wait_ge(s_sc_, v + 1)
                    diag = pb[:, b, P * q:P * (q + 1)]
                    V.tensor_tensor(diag, diag, mask, ALU.add)
                    dve.drain()
                    V.reduce_max(ast[:, 0, b:b + 1], pb[:, b, 0:P * (q + 1)], AX_X)
                    dve.drain()
                    h = v // TT
                    if v >= 2:
                        dve.wait_ge(s_ex, v - 1)
                    V.tensor_scalar(ast[:, 1, b:b + 1], ast[:, 0, b:b + 1], ams[:, 0, h // 2, q, h % 2:h % 2 + 1], -1.0,
                                    ALU.mult, ALU.mult).then_inc(s_mx, 1)
                w = v - 1
                if 0 <= w < TT * AH:
                    q, b = w % TT, w % 2
                    dve.wait_ge(s_ex, w + 1)
                    V.reciprocal(ast[:, 3, b:b + 1], ast[:, 2, b:b + 1])
                    dve.drain()
                    V.tensor_scalar(pp[:, TRI[q]:TRI[q + 1]], pp[:, TRI[q]:TRI[q + 1]], ast[:, 3, b:b + 1], None, ALU.mult)\
                     .then_inc(s_pn, 1)
                if v >= 13 and (v - 13) % 8 == 0 and (v - 13) // 8 < 4:
                    t = (v - 13) // 8
                    dve.wait_ge(s_yah, t + 1)
                    V.tensor_tensor(yal[:, t, :], py[:, :], yah[:, t, :].bitcast(F32), ALU.subtract).then_inc(s_yal, 1)

            def merge(t, k, gate=None):
                dve.wait_ge(s_mm, t + 1)
                o = merged[:, k, :]
                if gate is None:
                    V.scalar_tensor_tensor(o, o, 1.0, bank_of(t), ALU.add, ALU.mult)
                    dve.drain().then_inc(s_ev["dve"], 1)
                else:
                    m = mt[:, k % 2, :]
                    V.scalar_tensor_tensor(m, gate, 1.0, bank_of(t), ALU.add, ALU.mult)
                    dve.drain().then_inc(s_ev["dve"], 1)
                    V.tensor_tensor(o, o, m, ALU.add)
                dve.drain().then_inc(s_mg, 1)

            def residual(t, k):
                dve.wait_ge(s_mm, t + 1)
                V.tensor_tensor(x[:, k, :], x[:, k, :], bank_of(t), ALU.add).then_inc(s_ev["dve"], 1)

            s5_theta(s_early0, s_dt0, s_th0)
            s5_cos(s_sc0, s_dt0)
            s5_powers(range(1, LEVELS))
            for lv in range(5):
                s5_first_phases(lv)
            s5_input_factor()
            dve.drain().then_inc(s_f0, 1)
            dve.wait_ge(s_hi0, 2)
            V.tensor_tensor(wl[:, 1, :], raw[:, 1, :], wh[:, 1, :].bitcast(F32), ALU.subtract).then_inc(s_lo0, 1)
            dve.wait_ge(s_small, 16)
            with dve.Fori(0, DEPTH) as l:
                norm(0, "g1")
                dve.drain()
                s5_phases(0)
                u_remainder(0)
                b_remainder(0)
                b_remainder(1)
                dve.wait_ge(s_par, 16)
                dve.wait_ge(s_tables, 16)
                for p in range(N_POINTS):
                    s = p // 3
                    if p in (1, 2):
                        b_remainder(p + 1)
                    if p >= 6 and p % 8 == 6 and p < 24:
                        u_remainder((p + 2) // 8)
                    proj_point(p)
                    if p % 3 == 0 and s < ST:
                        s5_rotate(s)
                    if p % 3 == 1 and s < ST:
                        s5_scan(s)
                    if p % 3 == 2 and s % 4 == 0 and 4 <= s <= ST:
                        s5_channels(s // 4 - 1)
                swap_gains()
                for i, n in enumerate(P3):
                    kind = STREAM[n][0]
                    t = tile_of(n)
                    if n == S_GS:
                        att_point(0)
                        for k in range(4):
                            dve.wait_ge(s_gh, k + 1)
                            V.tensor_tensor(gl[:, k, :], proj[:, U0 + k, :], gh[:, k, :].bitcast(F32), ALU.subtract).then_inc(s_gl, 1)
                    else:
                        att_point(2 * i)
                    if kind == "branch":
                        k = 2 * (n - (S_BS if n < S_BR else S_BR)) if n < S_GR2 else 4 + 2 * (n - S_BR2)
                        dve.wait_ge(s_ev["act"], OWNER[:t].count("act"))
                        merge(t, k, None if n < S_BR else gates[:, k % 4, :])
                    att_point(2 * i + 1)
                    if kind == "branch":
                        merge(t + 1, k + 1, None if n < S_BR else gates[:, k % 4 + 1, :])
                    if kind == "glu":
                        m = n - S_GLU
                        dve.wait_ge(s_ev["act"], evacuated(t)[1])
                        V.scalar_tensor_tensor(sg[:, m % 2, :], sg[:, m % 2, :], 1.0, proj[:, U0 + m, :], ALU.add, ALU.mult)\
                         .then_inc(s_yf, 1)
                    if S_GLU < n <= S_GR:
                        m = n - S_GLU - 1
                        dve.wait_ge(s_yh, m + 1)
                        V.scalar_tensor_tensor(ysl[:, m, :], sg[:, m % 2, :], 0.5, ysh[:, m, :].bitcast(F32), ALU.mult, ALU.subtract)\
                         .then_inc(s_yl, 1)
                for n in range(S_A, S_O):
                    if STREAM[n][0] == "branch":
                        t = tile_of(n)
                        k = 4 * ((n - S_A) // 6) + 2 * ((n - S_A) % 6 - 4)
                        dve.wait_ge(s_ev["act"], OWNER[:t].count("act"))
                        for m in range(2):
                            merge(t + m, k + m, gates[:, k % 4 + m, :])
                for k in range(DK):
                    dve.wait_ge(s_mh, k + 1)
                    V.scalar_tensor_tensor(xl[:, k, :], merged[:, k, :], 0.5, xh[:, k, :].bitcast(F32), ALU.mult, ALU.subtract)\
                     .then_inc(s_ml, 1)
                for k in range(DK):
                    residual(tile_of(S_O) + k, k)
                    if k >= 1:
                        sum_step(k - 1, s_sq[1], s_su[1])
                sum_step(DK - 1, s_sq[1], s_su[1])
                norm(1, "g2")
                dve.drain()
                g = 0
                for n in range(S_UP0, N_SLABS):
                    t = tile_of(n)
                    if STREAM[n][0] == "up":
                        m, b = (t - tile_of(S_UP0)) % 2, g % 2
                        dve.wait_ge(s_c0, 2 * g + m + 1)
                        dst = (cg, cu)[m][:, b, :]
                        f = m * FT + g
                        for tap, sh in ((1, 1), (0, 2)):
                            w0 = PAR["cw"][0] + tap * 2 * FT + f
                            V.scalar_tensor_tensor(dst[:, sh:L], bank_of(t)[:, 0:L - sh], pr[:, w0:w0 + 1], dst[:, sh:L],
                                                   ALU.mult, ALU.add)
                            dr = dve.drain()
                        dr.then_inc(s_ev["dve"], 1)
                        dve.drain().then_inc(s_c1, 1)
                        if m == 1:
                            dve.wait_ge(s_si, g + 1)
                            if g >= 2:
                                dve.wait_ge(s_hh, g - 1)
                            V.tensor_tensor(ht[:, b, :], cg[:, b, :], cu[:, b, :], ALU.mult).then_inc(s_hd, 1)
                            dve.wait_ge(s_hh, g + 1)
                            seg = 0 if g < SEGS[0] else 1 if g < SEGS[0] + SEGS[1] else 2
                            i = g - sum(SEGS[:seg])
                            V.tensor_tensor(hl[:, seg % 2, i, :], ht[:, b, :], hh[:, seg % 2, i, :].bitcast(F32),
                                            ALU.subtract).then_inc(s_hl, 1)
                            dve.drain()
                            g += 1
                    else:
                        residual(t, (n - S_DN0) % DK if n < S_UP2 else (n - S_DN1) % DK)
                        s5_prepare_part(n - S_DN0 if n < S_UP2 else DK + n - S_DN1)
                        if n > S_DN2:
                            sum_step(n - S_DN2 - 1, s_sq[0], s_su[0])
                sum_step(DK - 1, s_sq[0], s_su[0])
                layer_end(dve)


def constants():
    f = np.float32
    p = np.arange(P)
    t = np.arange(L)
    lg = np.log1p(-np.exp2(f(-5.0) - np.arange(RH, dtype=f))).astype(f)
    rel = (t[None, :] - p[:, None]).astype(f)
    decay = np.where(rel[None] >= 0, np.exp(lg[:, None, None] * np.maximum(rel, 0)[None]), 0).astype(f)
    decay = decay.transpose(1, 0, 2).reshape(P, RH * L)
    half = RQ // 2
    inv = (f(1.0) / (f(10000.0) ** np.linspace(0.0, 1.0, half, dtype=f))).astype(f)
    ang = inv[p % half][:, None] * t[None, :].astype(f)
    r_cos, r_sin = np.cos(ang).astype(f), np.sin(ang).astype(f)
    rh = AD // 4 // 2
    inva = (f(500000.0) ** (-np.arange(rh, dtype=f) / f(rh))).astype(f)
    d = p % AD
    turned = (d < 2 * rh)[:, None]
    anga = inva[d % rh][:, None] * t[None, :].astype(f)
    a_cos = np.where(turned, np.cos(anga), 1).astype(f)
    a_sin = np.where(turned, np.sin(anga), 0).astype(f)
    ident = np.eye(P, dtype=f)

    def swap(h, block):
        m = np.zeros((P, P), f)
        for o in range(P):
            q = o % block
            if q < h:
                m[o + h, o] = -1.0
            elif q < 2 * h:
                m[o - h, o] = 1.0
        return m

    blk = np.where(p[:, None] // AD == p[None, :] // AD, 1.0 / AD, 0.0).astype(f)
    mask = np.where(p[None, :] <= p[:, None], 0.0, MASKED).astype(f)
    return np.ascontiguousarray(np.concatenate(
        [ident, swap(half, RQ), swap(rh, AD), np.ones((P, P), f), (ident - f(1.0 / P)).astype(f), blk, mask,
         decay, r_cos, r_sin, a_cos, a_sin], axis=1).astype(f))


def kernel(x, norm1_g, w_in, ssm_lambda_re, ssm_lambda_im, ssm_log_dt, ssm_b_re, ssm_b_im, ssm_c_re, ssm_c_im, ssm_d,
           ssm_w_glu, ret_gn_g, attn_qn_g, attn_kn_g, w_br_ssm, w_br_ret, w_br_att, w_o, norm2_g, ffn_w_up, ffn_conv_w,
           ffn_conv_b, ffn_w_down):
    import numpy as _np
    import concourse.bacc as _bacc
    from concourse import mybir as _mybir
    from concourse.bass_utils import run_bass_kernel_spmd as _run

    A = _np.asarray

    def slabs(w, cols):
        w = A(w)
        n, k, c = w.shape
        return w.reshape(n, k // P, P, c // cols, cols).transpose(0, 3, 2, 1, 4).reshape(n, c // cols, P, -1)

    w_in = A(w_in)
    g0 = P * N_PROJ
    main = slabs(w_in[:, :, :g0], P)
    gate = [slabs(w_in[:, :, g0 + D * i:g0 + D * (i + 1)], P) for i in range(3)]
    br = [slabs(w, 2 * P) for w in (w_br_ssm, w_br_ret, w_br_att)]
    up = A(ffn_w_up).reshape(DEPTH, D, 2, FT, P).transpose(0, 1, 3, 2, 4).reshape(DEPTH, D, 2 * FH)
    up = slabs(up, P)
    u1, u2 = 2 * SEGS[0], 2 * (SEGS[0] + SEGS[1])
    down, at = [], 0
    for n in SEGS:
        w = slabs(A(ffn_w_down)[:, at * P:(at + n) * P], P)
        down.append(_np.concatenate([w, _np.zeros(w.shape[:3] + (SLAB - w.shape[3],), w.dtype)], axis=3))
        at += n
    parts = [main, gate[0], _np.concatenate([slabs(ssm_w_glu, P), _np.zeros((DEPTH, 4, P, SLAB // 2), _np.float32)], axis=3), gate[1][:, 0:4], br[0]]
    parts += [br[1][:, 0:2], gate[1][:, 4:8], br[1][:, 2:4]]
    parts += [gate[2][:, 0:4], br[2][:, 0:2], gate[2][:, 4:8], br[2][:, 2:4]]
    parts += [slabs(w_o, P), up[:, :u2], down[0], up[:, u2:], down[1], down[2]]
    wslab = _np.concatenate(parts, axis=1)
    assert wslab.shape[1] == N_SLABS
    wslab = wslab.reshape(DEPTH * N_SLABS, P, SLAB)
    wslab = _np.concatenate([wslab, wslab[0:HEAD]])

    def cols(a, n):
        return A(a).reshape(DEPTH, n, P).transpose(0, 2, 1)

    ldt = _np.repeat(A(ssm_log_dt)[:, :, None], SSM_P, axis=2)
    cw = A(ffn_conv_w).reshape(DEPTH, 3, 2 * FT, P).transpose(0, 3, 1, 2).reshape(DEPTH, P, -1)
    par = _np.ascontiguousarray(_np.concatenate(
        [cols(norm2_g, DK), cols(ret_gn_g, RH),
         _np.concatenate([A(attn_qn_g)] * 2, axis=1)[:, :, None], _np.concatenate([A(attn_kn_g)] * 2, axis=1)[:, :, None],
         cols(ssm_d, 4), cw, cols(ffn_conv_b, 2 * FT)], axis=2))

    def wrapped(a):
        return _np.ascontiguousarray(_np.concatenate([a, a[0:1]]))

    early = wrapped(_np.concatenate([cols(norm1_g, DK), cols(ssm_lambda_re, ST), cols(ssm_lambda_im, ST), cols(ldt, ST)], axis=2))
    bblk = _np.zeros((DEPTH, P, 4, 4, 2, P), _np.float32)
    cblk = _np.zeros((DEPTH, P, 2, ST, CH), _np.float32)
    for i, (b, c) in enumerate(((ssm_b_re, ssm_c_re), (ssm_b_im, ssm_c_im))):
        b, c = A(b), A(c)
        for s in range(ST):
            for g in range(2):
                st, ch = slice(SSM_P * g, SSM_P * (g + 1)), slice(SSM_H * g, SSM_H * (g + 1))
                for copy in range(4):
                    row = CH * copy + SSM_H * g
                    bblk[:, row:row + SSM_H, s // 4, s % 4, i, st] = b[:, 2 * s + g].transpose(0, 2, 1)
                cblk[:, st, i, s, ch] = c[:, 2 * s + g].transpose(0, 2, 1)
    bblk = bblk.reshape(DEPTH, P, 4, SLAB)
    xT = _np.ascontiguousarray(A(x)[0].T.reshape(DK, P, L).transpose(1, 0, 2))
    arrays = {"xT": xT, "wslab": wslab, "par": par, "early": early, "bblk": bblk, "cblk": wrapped(cblk),
              "cst": constants()}

    nc = _bacc.Bacc("TRN2", target_bir_lowering=False, num_devices=1, dynamic_dma_scratch_size=4096)
    args = [nc.dram_tensor(f"in_{n}", a.shape, _mybir.dt.from_np(a.dtype), kind="ExternalInput").ap() for n, a in arrays.items()]
    args.append(nc.dram_tensor("out_T", (P, DK, L), _mybir.dt.float32, kind="ExternalOutput").ap())
    hybrid_trunk(nc, *args)
    r = _run(nc, [{f"in_{n}": a for n, a in arrays.items()}], core_ids=[0])
    o = r.results[0]["out_T"]
    return _np.ascontiguousarray(o.transpose(1, 0, 2).reshape(D, L).T)[None]
```
